# Optimizing a Trainium2 kernel written in Bass

```python
import jax, jax.numpy as jnp
from jax import lax
import numpy as np

D_MODEL = 1024
BATCH = 1
SEQ = 512
DEPTH = 2

CHUNK = 64
Q_BLOCK = 128
MIX_WIDTH = D_MODEL
FOX_HEADS = 8
FOX_HEAD_DIM = 64
FOX_WIDTH = FOX_HEADS * FOX_HEAD_DIM
RET_HEADS = 4
RET_HEAD_DIM = 128
RET_WIDTH = RET_HEADS * RET_HEAD_DIM
IN_WIDTH = 3 * FOX_WIDTH + FOX_HEADS + 4 * RET_WIDTH
ROPE_BASE = 10000.0
N_GROUPS = 4
EXPERTS_PER_GROUP = 8
N_EXPERTS = N_GROUPS * EXPERTS_PER_GROUP
TOP_K_INNER = 2
D_EXPERT = D_MODEL // 2
DISPATCH_BLOCK = 128
RMS_EPS = 1e-6

kernel_name = 'hybrid_fox_retnet_hmoe_trunk'

def rmsnorm(x, w):
    xf = x.astype(jnp.float32)
    y = xf * lax.rsqrt(jnp.mean(xf * xf, axis=-1, keepdims=True) + RMS_EPS)
    return y.astype(x.dtype) * w

def head_rmsnorm(x):
    xf = x.astype(jnp.float32)
    y = xf * lax.rsqrt(jnp.mean(xf * xf, axis=-1, keepdims=True) + RMS_EPS)
    return y.astype(x.dtype)

def rotary(x):
    S, D = x.shape[1], x.shape[-1]
    half = D // 2
    inv_freq = 1.0 / (ROPE_BASE ** (jnp.arange(half, dtype=jnp.float32) / half))
    ang = jnp.arange(S, dtype=jnp.float32)[:, None] * inv_freq[None, :]
    cos = jnp.cos(ang)[None, :, None, :].astype(x.dtype)
    sin = jnp.sin(ang)[None, :, None, :].astype(x.dtype)
    x1, x2 = x[..., :half], x[..., half:]
    return jnp.concatenate([x1 * cos - x2 * sin, x1 * sin + x2 * cos], axis=-1)

def forgetting_attention(q, k, v, log_f):
    B, S, H, Dh = q.shape
    c = jnp.cumsum(log_f, axis=1).transpose(0, 2, 1)
    scale = Dh ** -0.5
    outs = []
    for i in range(S // Q_BLOCK):
        q0 = i * Q_BLOCK
        kend = q0 + Q_BLOCK
        s = jnp.einsum('bqhd,bkhd->bhqk', q[:, q0:kend], k[:, :kend]).astype(jnp.float32) * scale
        s = s + (c[:, :, q0:kend, None] - c[:, :, None, :kend])
        q_pos = q0 + jnp.arange(Q_BLOCK)
        mask = q_pos[:, None] >= jnp.arange(kend)[None, :]
        s = jnp.where(mask[None, None], s, -jnp.inf)
        p = jax.nn.softmax(s, axis=-1).astype(v.dtype)
        outs.append(jnp.einsum('bhqk,bkhd->bqhd', p, v[:, :kend]))
    return jnp.concatenate(outs, axis=1)

def retention(q, k, v):
    B, S, H, Dk = q.shape
    Dv = v.shape[-1]
    NC = S // CHUNK
    out_dtype = v.dtype
    qc = q.astype(jnp.float32).reshape(B, NC, CHUNK, H, Dk)
    kc = k.astype(jnp.float32).reshape(B, NC, CHUNK, H, Dk) * (Dk ** -0.5)
    vc = v.astype(jnp.float32).reshape(B, NC, CHUNK, H, Dv)
    log_gamma = jnp.log(1.0 - 2.0 ** (-5.0 - jnp.arange(H, dtype=jnp.float32)))
    idx = jnp.arange(CHUNK, dtype=jnp.float32)
    dist = jnp.abs(idx[:, None] - idx[None, :])
    intra_decay = jnp.exp(log_gamma[:, None, None] * dist)
    scores = jnp.einsum('bnjhd,bnlhd->bnhjl', qc, kc) * intra_decay
    intra = jnp.einsum('bnhjl,bnlhe->bnjhe', scores, vc)
    k_decay = jnp.exp(log_gamma[None, :] * (CHUNK - idx)[:, None])
    chunk_kv = jnp.einsum('bnlhd,bnlhe->nbhde', kc * k_decay[:, :, None], vc)
    chunk_decay = jnp.exp(log_gamma * CHUNK)[:, None, None]

    def step(state, kv):
        return chunk_decay * state + kv, state

    _, states = lax.scan(step, jnp.zeros((B, H, Dk, Dv), jnp.float32), chunk_kv)
    q_decay = jnp.exp(log_gamma[None, :] * idx[:, None])
    cross = jnp.einsum('bnjhd,nbhde->bnjhe', qc * q_decay[:, :, None], states)
    return (intra + cross).reshape(B, S, H, Dv).astype(out_dtype)

def mixer(h, w_in, fox_forget_b, w_out):
    B, S, _ = h.shape
    proj = h @ w_in
    splits = [int(i) for i in np.cumsum([FOX_WIDTH] * 3 + [FOX_HEADS] + [RET_WIDTH] * 3)]
    fq, fk, fv, ff, rq, rk, rv, rg = jnp.split(proj, splits, axis=-1)
    log_f = jax.nn.log_sigmoid((ff + fox_forget_b).astype(jnp.float32))
    fox = forgetting_attention(fq.reshape(B, S, FOX_HEADS, FOX_HEAD_DIM),
                               fk.reshape(B, S, FOX_HEADS, FOX_HEAD_DIM),
                               fv.reshape(B, S, FOX_HEADS, FOX_HEAD_DIM), log_f)
    ret = retention(rotary(rq.reshape(B, S, RET_HEADS, RET_HEAD_DIM)),
                    rotary(rk.reshape(B, S, RET_HEADS, RET_HEAD_DIM)),
                    rv.reshape(B, S, RET_HEADS, RET_HEAD_DIM))
    ret = head_rmsnorm(ret) * jax.nn.silu(rg).reshape(B, S, RET_HEADS, RET_HEAD_DIM)
    mixed = jnp.concatenate([fox.reshape(B, S, FOX_WIDTH), ret.reshape(B, S, RET_WIDTH)], axis=-1)
    return mixed @ w_out

def hierarchical_moe(h, w_router_group, b_router_group, w_router_expert, b_router_expert,
                     w_expert_gate, w_expert_up, w_expert_down):
    B, S, D = h.shape
    N = B * S
    K = TOP_K_INNER
    hf = h.reshape(N, D)
    g_logits = (hf @ w_router_group + b_router_group).astype(jnp.float32)
    g_prob = jax.nn.softmax(g_logits, axis=-1)
    g_idx = jnp.argmax(g_logits, axis=-1)
    g_w = jnp.take_along_axis(g_prob, g_idx[:, None], axis=-1)
    e_logits = (hf @ w_router_expert + b_router_expert).astype(jnp.float32)
    e_logits = e_logits.reshape(N, N_GROUPS, EXPERTS_PER_GROUP)
    e_in_group = jnp.take_along_axis(e_logits, g_idx[:, None, None], axis=1)[:, 0]
    top_v, top_i = lax.top_k(e_in_group, K)
    weights = (g_w * jax.nn.softmax(top_v, axis=-1)).reshape(-1)
    eid = (g_idx[:, None] * EXPERTS_PER_GROUP + top_i).reshape(-1).astype(jnp.int32)
    tok = jnp.repeat(jnp.arange(N, dtype=jnp.int32), K)
    order = jnp.argsort(eid)
    eid_s, tok_s, w_s = eid[order], tok[order], weights[order]
    counts = jnp.bincount(eid, length=N_EXPERTS)
    starts = jnp.cumsum(counts) - counts
    padded = (counts + DISPATCH_BLOCK - 1) // DISPATCH_BLOCK * DISPATCH_BLOCK
    pend = jnp.cumsum(padded)
    pstarts = pend - padded
    dest = pstarts[eid_s] + (jnp.arange(N * K, dtype=jnp.int32) - starts[eid_s])
    P = N * K + N_EXPERTS * DISPATCH_BLOCK
    tok_buf = jnp.zeros((P,), jnp.int32).at[dest].set(tok_s)
    w_buf = jnp.zeros((P,), jnp.float32).at[dest].set(w_s)
    nb = P // DISPATCH_BLOCK
    blk_e = jnp.searchsorted(pend, jnp.arange(nb, dtype=pend.dtype) * DISPATCH_BLOCK, side='right')
    blk_e = jnp.minimum(blk_e, N_EXPERTS - 1)
    xb = hf[tok_buf].reshape(nb, DISPATCH_BLOCK, D)

    def expert_block(args):
        xblk, e = args
        a = jax.nn.silu(xblk @ w_expert_gate[e]) * (xblk @ w_expert_up[e])
        return a @ w_expert_down[e]

    yb = lax.map(expert_block, (xb, blk_e)).reshape(P, D)
    out = jax.ops.segment_sum(yb * w_buf.astype(yb.dtype)[:, None], tok_buf, num_segments=N)
    return out.reshape(B, S, D)

def setup_inputs(seed: int = 0) -> dict:
    key = jax.random.key(seed)
    ks = jax.random.split(key, 14)
    f32 = jnp.float32

    def nrm(k, shape, scale):
        return jax.random.normal(k, shape, f32) * scale

    return {
        'x': nrm(ks[0], (BATCH, SEQ, D_MODEL), 1.0),
        'norm_mix_w': 1.0 + nrm(ks[1], (DEPTH, D_MODEL), 0.1),
        'w_in': nrm(ks[2], (DEPTH, D_MODEL, IN_WIDTH), D_MODEL ** -0.5),
        'fox_forget_b': jax.random.uniform(ks[3], (DEPTH, FOX_HEADS), f32, 1.0, 3.0),
        'w_out': nrm(ks[4], (DEPTH, MIX_WIDTH, D_MODEL), MIX_WIDTH ** -0.5),
        'norm_ffn_w': 1.0 + nrm(ks[5], (DEPTH, D_MODEL), 0.1),
        'w_router_group': nrm(ks[6], (DEPTH, D_MODEL, N_GROUPS), D_MODEL ** -0.5),
        'b_router_group': nrm(ks[7], (DEPTH, N_GROUPS), 0.01),
        'w_router_expert': nrm(ks[8], (DEPTH, D_MODEL, N_EXPERTS), D_MODEL ** -0.5),
        'b_router_expert': nrm(ks[9], (DEPTH, N_EXPERTS), 0.01),
        'w_expert_gate': nrm(ks[10], (DEPTH, N_EXPERTS, D_MODEL, D_EXPERT), D_MODEL ** -0.5),
        'w_expert_up': nrm(ks[11], (DEPTH, N_EXPERTS, D_MODEL, D_EXPERT), D_MODEL ** -0.5),
        'w_expert_down': nrm(ks[12], (DEPTH, N_EXPERTS, D_EXPERT, D_MODEL), D_EXPERT ** -0.5),
        'norm_final_w': 1.0 + nrm(ks[13], (D_MODEL,), 0.1),
    }

def reference(x, norm_mix_w, w_in, fox_forget_b, w_out, norm_ffn_w, w_router_group, b_router_group,
              w_router_expert, b_router_expert, w_expert_gate, w_expert_up, w_expert_down, norm_final_w):
    for layer in range(DEPTH):
        x = x + mixer(rmsnorm(x, norm_mix_w[layer]), w_in[layer], fox_forget_b[layer], w_out[layer])
        x = x + hierarchical_moe(rmsnorm(x, norm_ffn_w[layer]), w_router_group[layer], b_router_group[layer],
                                 w_router_expert[layer], b_router_expert[layer], w_expert_gate[layer],
                                 w_expert_up[layer], w_expert_down[layer])
    return rmsnorm(x, norm_final_w)


_drawn_inputs = setup_inputs


def setup_inputs(seed=0):
    import zlib

    import numpy as np

    out = dict(_drawn_inputs(seed))
    spreads = {}
    factors = {'b_router_group': 3.272}
    for name, (base, spread) in spreads.items():
        noise = np.random.default_rng([zlib.crc32(name.encode()), seed]).standard_normal(out[name].shape)
        drawn = base * np.exp(spread * noise) if base else spread * noise
        out[name] = __import__('jax').numpy.asarray(drawn.astype(out[name].dtype))
    for name, factor in factors.items():
        out[name] = (out[name] * factor).astype(out[name].dtype)
    return out
```

```python
import numpy as np
import concourse.bass as bass
from concourse import mybir
from contextlib import ExitStack

F32 = mybir.dt.float32
I32 = mybir.dt.int32
ALU = mybir.AluOpType
ACT = mybir.ActivationFunctionType
AX = mybir.AxisListType

P = 128
DEPTH, T, D = 2, 512, 1024
NT = T // P
KC = D // P
FH, FD = 8, 64
RH, RD = 4, 128
CHUNK = 64
NG, EPG, TOPK = 4, 8, 2
NE = NG * EPG
DE = D // 2
EPS = 1e-6
ROPE_BASE = 10000.0
NEG = -3.0e38

SLOTS = 64
MAXBLK = T // SLOTS
NOV = max(k for k in range(NE * MAXBLK)
          if min(k, NE) * (SLOTS + 1) + max(k - NE, 0) * SLOTS <= T * TOPK)
NCOL = NE + NOV + 1

EXPERT = 2 * KC * DE + (DE // P) * D
RING = 3
SLAB = KC * 512
HT0 = 0
QT0 = HT0 + KC * T
KT0 = QT0 + FH * T
FV0 = EXPERT
RQ0 = FV0 + NT * 512
RK0 = RQ0 + RH * T
RV0 = RK0 + RH * T
RG0 = RV0 + NT * 512
DK0 = RG0 + RH * T
WR0 = 2 * EXPERT
WK0 = RING * EXPERT
MX0 = WK0
PB0 = MX0 + KC * T
PLEN = P * NT * (NT + 1) // 2
PT0 = PB0 + 2 * PLEN
TA0 = PT0 + PLEN
CS0 = TA0 + 2 * T
AREA = CS0 + 2 * T
XN0 = PT0
XG0 = PB0
XT0 = XG0 + 3 * 512
SG0 = XT0 + 512
HH0 = SG0 + 256
HX0 = HH0 + 256
YY0 = HX0 + 256
WB0 = YY0 + 3 * 512
assert WB0 + 512 <= CS0 and DK0 + RH * T <= 2 * EXPERT and KT0 + FH * T <= EXPERT
YC0 = QT0


def pblk(qb):
    return P * qb * (qb + 1) // 2


def tblk(j):
    return sum(T - P * i for i in range(j))


def const_layout():
    parts = [("ident", P), ("mask", P), ("ones", P), ("lower", P), ("slot", P), ("col", NCOL), ("exp", NE),
             ("g", NG), ("o", EPG), ("over", MAXBLK - 1), ("step", MAXBLK - 1), ("blk", NOV),
             ("val", NT * TOPK), ("tok", NT), ("half", 1), ("eps", 1), ("one", 1)]
    at, out = 0, {}
    for name, n in parts:
        out[name] = (at, at + n)
        at += n
    return out, at


CONST, NCONST = const_layout()


def constants():
    p = np.arange(P)
    c = np.zeros((P, NCONST), np.float32)

    def put(name, v):
        c[:, CONST[name][0]:CONST[name][1]] = v

    put("ident", np.eye(P))
    put("mask", np.where(p[:, None] >= p[None, :], 0.0, NEG))
    put("ones", 1.0)
    put("lower", p[:, None] < p[None, :])
    put("slot", p % SLOTS)
    put("col", np.arange(NCOL))
    put("exp", np.arange(NE))
    put("g", np.arange(NG) - NG)
    put("o", np.arange(EPG) - EPG)
    put("over", SLOTS * np.arange(1, MAXBLK) + 1)
    put("step", SLOTS * np.arange(1, MAXBLK))
    put("blk", np.arange(NOV))
    tok = p[:, None] + P * np.arange(NT)[None]
    put("val", (TOPK * tok[:, :, None] + np.arange(TOPK) + 1).reshape(P, -1))
    put("tok", tok)
    put("half", (p >= SLOTS)[:, None])
    put("eps", EPS)
    put("one", 1.0)
    half = RD // 2
    inv = (np.float32(1.0) / (np.float32(ROPE_BASE) ** (np.arange(half, dtype=np.float32) / np.float32(half)))).astype(np.float32)
    ang = inv[:, None] * np.arange(T, dtype=np.float32)[None, :]
    cos, sin = np.cos(ang), np.sin(ang)
    cs = np.concatenate([np.concatenate([cos, cos]), np.concatenate([-sin, sin])], axis=1).astype(np.float32)
    lg = np.log(1.0 - 2.0 ** (-5.0 - np.arange(RH)))
    l, j = np.arange(P)[:, None], np.arange(T)[None, :]
    power = np.where(l // CHUNK == j // CHUNK, np.abs(j - l), j - l)
    live = (l // CHUNK) <= (j // CHUNK)
    decay = np.where(live[None], np.exp(lg[:, None, None] * power[None]), 0.0) * RD ** -0.5
    decay = decay.transpose(1, 0, 2).reshape(P, RH * T).astype(np.float32)
    return {"const": c, "rope": cs, "decay": decay}


SLAB_OF = {"fq": 0, "fk": 1, "fv": 2, "rq": 3, "rk": 4, "rv": 5, "rg": 6}
NSLAB = 9
FF_COL = 3 * FH * FD
SLAB_COL = [0, 512, 1024] + [FF_COL + FH + 512 * i for i in range(4)]


def steps():
    out = [("normT", c) for c in range(KC)] + [("ff",)]
    out += [(k, i) for k in ("fq", "fk", "fv") for i in range(4)]
    ret = [(k, i) for k in ("rq", "rk", "rv", "rg") for i in range(4)]
    for h in range(FH + 1):
        if h < FH:
            out += [("S", h, 0), ("S", h, 1)]
        if h:
            out += [("PT", h - 1, 0), ("PT", h - 1, 1)]
        out += ret[2 * h:2 * h + 1]
        if h == FH:
            out += [("RS", 0, j) for j in range(2)]
        if h:
            out += [("PV", h - 1, 0), ("PV", h - 1, 1), ("PT", h - 1, 2), ("PT", h - 1, 3)]
        if h < FH:
            out += [("S", h, 2), ("S", h, 3)]
        out += ret[2 * h + 1:2 * h + 2]
        if h:
            out += [("PV", h - 1, 2), ("PV", h - 1, 3)]
    out += [("RS", 0, 2), ("RS", 0, 3)]
    for r in range(RH):
        if r + 1 < RH:
            out += [("RS", r + 1, j) for j in range(NT)]
        out += [("RV", r)]
        if r:
            out += [("RN", r - 1)]
    out += [("RN", RH - 1)]
    out += [("wo", 0, 0), ("wo", 0, 1), ("wo", 1, 0), ("wo", 1, 1), ("fT", 0, 0), ("fT", 0, 1),
            ("wo", 2, 0), ("wo", 2, 1), ("lg", 0), ("fT", 1, 0), ("fT", 1, 1), ("wo", 3, 0), ("wo", 3, 1),
            ("lg", 1), ("fT", 2, 0), ("fT", 2, 1), ("lg", 2), ("fT", 3, 0), ("fT", 3, 1), ("lg", 3),
            ("rank",), ("table",)]
    return out


STEPS = steps()


def banks():
    acc, uses, where = 0, [0] * 8, {}
    for s in STEPS:
        kind = s[0]
        if kind == "S":
            b = 2 + s[2] % 2
        elif kind == "PT":
            b = 4 + s[2] % 2
        elif kind == "PV":
            s = ("O", s[1] // 2)
            b = 6 + s[1] % 2
        elif kind == "RS":
            b = 2 + s[2]
        elif kind == "RV":
            b = 6 + s[1] % 2
        elif kind == "lg":
            s, b = ("lg",), 2
        elif kind == "rank":
            b = 3
        elif kind == "table":
            b = 4
        else:
            b = acc % 2
            acc += 1
        if s not in where:
            where[s] = (b, uses[b])
            uses[b] += 1
    return where, uses


WHERE, USES = banks()


def trunk_kernel(nc, x, norm_mix_w, w_in, fox_forget_b, w_out, norm_ffn_w, w_router_group, b_router_group,
                 w_router_expert, b_router_expert, w_expert_gate, w_expert_up, w_expert_down, norm_final_w,
                 const, rope, decay, out):
    with ExitStack() as ctx:
        def sb(name, shape, dt=F32):
            return ctx.enter_context(nc.sbuf_tensor(name, shape, dt))

        def sem(name):
            return ctx.enter_context(nc.semaphore(name))

        rows_dram = nc.dram_tensor("rows", [2 * T, 512], F32, kind="Internal").ap()
        pair_dram = nc.dram_tensor("pairs", [2 * TOPK * T, 512], F32, kind="Internal").ap()

        area = sb("area", [P, AREA])
        xres = sb("xres", [P, NT, D])
        kst = sb("kst", [P, NCONST])
        ffw = sb("ffw", [P, DEPTH, KC, FH])
        rtw = sb("rtw", [P, DEPTH, KC, NG + NE])
        rtb = sb("rtb", [P, DEPTH, NG + NE])
        nmw = sb("nmw", [P, DEPTH, KC])
        nfw = sb("nfw", [P, DEPTH, KC])
        fgb = sb("fgb", [FH, DEPTH])
        stat = sb("stat", [P, 32])
        rowsum = sb("rowsum", [P, 16])
        gath = sb("gath", [P, NCOL], I32)
        scat = sb("scat", [P, NCOL], I32)
        wgt = sb("wgt", [P, NCOL])
        gcur = sb("gcur", [P, 4], I32)
        scur = sb("scur", [P, 4], I32)
        wcur = sb("wcur", [P, 4])
        ovn = sb("ovn", [1, 1], I32)
        ove = sb("ove", [1, NOV], I32)

        def k(name):
            return kst[:, CONST[name][0]:CONST[name][1]]

        def at(start, n, parts=P):
            return area[0:parts, start:start + n]

        hT = at(HT0, KC * T).rearrange("p (c t) -> p c t", c=KC)
        qT = at(QT0, FH * T).rearrange("p (h t) -> p h t", h=FH)
        kT = at(KT0, FH * T).rearrange("p (h t) -> p h t", h=FH)
        fv = at(FV0, NT * 512).rearrange("p (t n) -> p t n", t=NT)
        rq = at(RQ0, RH * T).rearrange("p (h t) -> p h t", h=RH)
        rk = at(RK0, RH * T).rearrange("p (h t) -> p h t", h=RH)
        rv = at(RV0, NT * 512).rearrange("p (t n) -> p t n", t=NT)
        rg = at(RG0, RH * T).rearrange("p (h t) -> p h t", h=RH)
        dk = at(DK0, RH * T).rearrange("p (h t) -> p h t", h=RH)
        slab = [at(WR0 + i * SLAB, SLAB).rearrange("p (c n) -> p c n", c=KC) for i in range(3)]
        mixed = at(MX0, KC * T).rearrange("p (c t) -> p c t", c=KC)
        xn_mix = at(MX0, NT * D).rearrange("p (t n) -> p t n", t=NT)
        prob = [at(PB0 + i * PLEN, PLEN) for i in range(2)]
        probT = at(PT0, PLEN)
        tmp = [at(TA0 + i * T, T) for i in range(2)]
        cos, sin = at(CS0, T), at(CS0 + T, T)
        hT2 = [at(PB0 + i * D, D).rearrange("p (c t) -> p c t", c=KC) for i in range(2)]
        xn2 = [at(XN0 + i * D, D) for i in range(2)]
        wexp = [(at(s * EXPERT, 2 * KC * DE).rearrange("p (g c n) -> p g c n", g=2, c=KC),
                 at(s * EXPERT + 2 * KC * DE, (DE // P) * D).rearrange("p (c n) -> p c n", n=D))
                for s in range(RING)]
        xg = [at(XG0 + i * 512, 512) for i in range(3)]
        xT = at(XT0, 512).rearrange("p (j h s) -> p j h s", j=4, h=2)
        sg, hh = at(SG0, 256), at(HH0, 256)
        hx = at(HX0, 256).rearrange("p (j h s) -> p j h s", j=2, h=2)
        yy = [at(YY0 + i * 512, 512) for i in range(3)]
        wbig = at(WB0, 512).rearrange("p (j h s) -> p j h s", j=4, h=2)
        yc = [at(YC0 + i * 2 * D, 2 * D) for i in range(NT)]
        negc = at(TA0, T, FH)

        free = [MX0]

        def rt(*shape):
            n = int(np.prod(shape))
            v = at(free[0], n)
            free[0] += n
            if len(shape) == 1:
                return v
            names = "abcd"[:len(shape)]
            return v.rearrange(f"p ({' '.join(names)}) -> p {' '.join(names)}",
                               **{c: s for c, s in zip(names, shape)})

        lgt = rt(NT, NG + NE)
        gs, gf, og = rt(NT, NG), rt(NT, NG), rt(NT, NG)
        em = rt(NT, NG, EPG)
        ein, ef, o1, o2 = rt(NT, EPG), rt(NT, EPG), rt(NT, EPG), rt(NT, EPG)
        a1, a2, asum = rt(NT, NG, EPG), rt(NT, NG, EPG), rt(NT, NE)
        col1 = [rt(NT) for _ in range(8)]
        gmax, gsum, gidx, m1, m2, i1, ed, wden = col1
        wk = rt(NT, TOPK)
        rank, cnt = rt(NT, NE), rt(NE)
        ovc, cum, ovb, onesE = rt(NE), rt(NE), rt(NE), rt(NE)
        cmp_ov = rt(NE, MAXBLK - 1)
        cmp_blk = rt(NOV, NE)
        rsel = rt(NT, NE)
        pick = rt(3, NT, TOPK)
        cmp_st = rt(NT, TOPK, MAXBLK - 1)
        blkno, rmod, colno, morethan = rt(NT, TOPK), rt(NT, TOPK), rt(NT, TOPK), rt(NT, TOPK)
        ovef = rt(NOV)
        tabs = rt(3 * NCOL)
        assert free[0] <= PB0
        routing_end = free[0]
        hotR = at(PB0, NT * TOPK * P).rearrange("p (t k s) -> p t k s", t=NT, k=TOPK)
        hotC = at(PB0 + NT * TOPK * P, 3 * NT * TOPK * NCOL).rearrange(
            "p (t k v c) -> p t k v c", t=NT, k=TOPK, v=3)
        assert PB0 + NT * TOPK * (P + 3 * NCOL) <= WB0

        bank = [ctx.enter_context(nc.psum_tensor(f"bank{i}", [P, 512], F32)) for i in range(8)]

        full = [sem(f"bank{i}_full") for i in range(8)]
        freed = [sem(f"bank{i}_free") for i in range(8)]
        s_const, s_small, s_x = sem("const_loaded"), sem("small_loaded"), sem("x_loaded")
        s_slab = [sem(f"slab{i}_loaded") for i in range(3)]
        s_decay = sem("decay_loaded")
        s_fz = sem("forget_gate_abs_ready")
        s_fl = sem("forget_gate_ln_ready")
        s_ffc = sem("forget_sums_ready")
        s_kaug = sem("forget_sums_in_keys")
        s_ones = sem("query_ones_set")
        s_xready = sem("x_ready")
        s_rstd = sem("rstd_ready")
        s_xn = sem("xn_ready")
        s_max = sem("row_max_ready")
        s_exp = sem("exp_done")
        s_prob = sem("prob_ready")
        s_swap = sem("rope_swapped")
        s_rot = sem("rope_done")
        s_gexp = sem("gate_exp_done")
        s_gate = sem("gate_done")
        s_sd = sem("decayed_scores_ready")
        s_ro = sem("retention_out_ready")
        s_sq = sem("retention_square_ready")
        s_rln = sem("retention_rstd_ready")
        s_ret = sem("retention_done")
        s_xmid = sem("x_after_mixer")
        s_rstd2 = sem("ffn_rstd_ready")
        s_xn2 = sem("ffn_xn_ready")
        s_rows = [sem(f"rows{i}_saved") for i in range(2)]
        s_rin = sem("router_exp_asked")
        s_rexp = sem("router_exp_done")
        s_hot = sem("choices_ready")
        s_tabin = sem("one_hots_ready")
        s_tab = sem("tables_ready")
        s_wb = sem("ffn_weight_spread")
        s_w = [[sem(f"slot{s}_{n}_loaded") for n in ("gate_up", "down")] for s in range(RING)]
        s_idx, s_gat = sem("block_indices_ready"), [sem(f"rows_gathered{i}") for i in range(3)]
        s_xtf, s_xt = sem("block_transposed"), sem("block_input_ready")
        s_gu, s_sg, s_h = sem("gate_up_done"), sem("silu_done"), sem("hidden_ready")
        s_hxf, s_hx = sem("hidden_transposed"), sem("hidden_t_ready")
        s_yf, s_y = sem("down_done"), sem("block_output_ready")
        s_sc = [sem(f"rows_scattered{i}") for i in range(3)]
        s_moe = sem("all_blocks_scattered")
        s_yc = [sem(f"pairs{i}_loaded") for i in range(NT)]
        s_passed = sem("gpsimd_waits_passed")
        s_act = sem("scalar_chain")
        s_dve = sem("vector_chain")
        s_fw = sem("final_weight_loaded")
        s_fin = sem("final_rows_ready")
        s_out = sem("out_stored")
        ov = [{n: sem(f"further{l}_{n}") for n in (
            "idx", "gathered", "weights", "xt_full", "xt", "gate_up", "silu", "hidden", "hx_full", "hx",
            "down", "out", "scattered")} for l in range(DEPTH)]

        def result(name, layer):
            b, n = WHERE[name]
            return b, layer * USES[b] + n + 1

        def is_full(eng, name, layer):
            b, n = result(name, layer)
            eng.wait_ge(full[b], n)

        def is_taken(eng, name, layer):
            b, n = result(name, layer)
            eng.wait_ge(freed[b], 2 * n)

        def may_fill(eng, name, layer):
            b, n = result(name, layer)
            if not isinstance(n, int) or n > 1:
                eng.wait_ge(freed[b], 2 * (n - 1))

        block = ctx.enter_context(nc.Block())

        @block.sync
        def _(sp):
            sp.dma_start(kst[:, :], const).then_inc(s_const, 16)
            for t in range(NT):
                sp.dma_start(xres[:, t, :], x[0, t * P:(t + 1) * P, :]).then_inc(s_x, 16)
            for l in range(DEPTH):
                sp.dma_start(nmw[:, l, :], norm_mix_w[l].rearrange("(c p) -> p c", p=P),
                             allow_slow_non_contiguous=True).then_inc(s_small, 16)
                sp.dma_start(nfw[:, l, :], norm_ffn_w[l].rearrange("(c p) -> p c", p=P),
                             allow_slow_non_contiguous=True).then_inc(s_small, 16)
                sp.dma_start(ffw[:, l, :, :], w_in[l, :, FF_COL:FF_COL + FH].rearrange("(c p) n -> p c n", p=P)
                             ).then_inc(s_small, 16)
                sp.dma_start(fgb[:, l:l + 1], fox_forget_b[l].rearrange("(h a) -> h a", a=1)).then_inc(s_small, 16)
            for l in range(DEPTH):
                sp.dma_start(rtw[:, l, :, 0:NG], w_router_group[l].rearrange("(c p) n -> p c n", p=P)
                             ).then_inc(s_small, 16)
                sp.dma_start(rtw[:, l, :, NG:], w_router_expert[l].rearrange("(c p) n -> p c n", p=P)
                             ).then_inc(s_small, 16)
                sp.dma_start(rtb[:, l, 0:NG], b_router_group[l:l + 1, :].broadcast_to([P, NG])
                             ).then_inc(s_small, 16)
                sp.dma_start(rtb[:, l, NG:], b_router_expert[l:l + 1, :].broadcast_to([P, NE])
                             ).then_inc(s_small, 16)

            def load_slab(layer, n):
                if n < 7:
                    src = w_in[layer, :, SLAB_COL[n]:SLAB_COL[n] + 512]
                else:
                    src = w_out[layer, :, 512 * (n - 7):512 * (n - 6)]
                sp.dma_start(slab[n % 3], src.rearrange("(c p) n -> p c n", p=P)).then_inc(s_slab[n % 3], 16)

            slab_last = {0: ("fq", 3), 1: ("fk", 3), 2: ("fv", 3), 3: ("rq", 3), 4: ("rk", 3), 5: ("rv", 3)}

            def load_gate_up(layer, e, slot):
                sp.dma_start(wexp[slot][0][:, 0, :, :], w_expert_gate[layer, bass.ds(e, 1), :, :]
                             .rearrange("a (c p) n -> p (a c) n", p=P)).then_inc(s_w[slot][0], 16)
                sp.dma_start(wexp[slot][0][:, 1, :, :], w_expert_up[layer, bass.ds(e, 1), :, :]
                             .rearrange("a (c p) n -> p (a c) n", p=P)).then_inc(s_w[slot][0], 16)

            def load_down(layer, e, slot):
                sp.dma_start(wexp[slot][1], w_expert_down[layer, bass.ds(e, 1), :, :]
                             .rearrange("a (c p) n -> p (a c) n", p=P)).then_inc(s_w[slot][1], 16)

            for layer in range(DEPTH):
                if layer == 0:
                    for n in range(3):
                        load_slab(layer, n)
                    sp.dma_start(at(CS0, 2 * T), rope).then_inc(s_decay, 16)
                if layer > 0:
                    sp.wait_ge(s_yf, layer * NE)
                sp.dma_start(at(DK0, RH * T), decay).then_inc(s_decay, 16)
                sp.wait_ge(s_ffc, layer + 1)
                sp.dma_start(kT[FD:FD + 1, :, :], negc).then_inc(s_kaug, 16)
                for n in range(3, NSLAB):
                    is_full(sp, slab_last[n - 3], layer)
                    load_slab(layer, n)
                is_full(sp, ("RS", 0, 0), layer)
                load_gate_up(layer, 0, 0)
                load_down(layer, 0, 0)
                sp.wait_ge(s_ret, RH * (layer + 1))
                load_gate_up(layer, 1, 1)
                load_down(layer, 1, 1)
                is_full(sp, ("wo", 3, 1), layer)
                load_gate_up(layer, 2, 2)
                load_down(layer, 2, 2)

                def load_expert(e, slot):
                    sp.wait_ge(s_gu, e + (layer * NE - RING + 1))
                    load_gate_up(layer, e, slot)
                    sp.wait_ge(s_yf, e + (layer * NE - RING + 1))
                    load_down(layer, e, slot)

                with sp.Fori(RING, NE - NE % RING, RING) as e0:
                    for i in range(RING):
                        load_expert(e0 + i, i)
                for e in range(NE - NE % RING, NE):
                    load_expert(e, e % RING)

                sp.wait_ge(s_tab, layer + 1)
                n_more = sp.value_load(ovn[0:1, 0:1], min_val=0, max_val=NOV)
                sp.wait_ge(s_yf, (layer + 1) * NE - 1)
                o = ov[layer]
                with sp.Fori(0, NOV) as j:
                    with sp.If(n_more > j):
                        ex = sp.value_load(ove[0:1, bass.ds(j, 1)], min_val=0, max_val=NE - 1)
                        sp.wait_ge(o["idx"], j + 1)
                        sp.dma_start(wexp[0][0][:, 0, :, :], w_expert_gate[layer, bass.ds(ex, 1), :, :]
                                     .rearrange("a (c p) n -> p (a c) n", p=P)).then_inc(o["weights"], 16)
                        sp.dma_start(wexp[0][0][:, 1, :, :], w_expert_up[layer, bass.ds(ex, 1), :, :]
                                     .rearrange("a (c p) n -> p (a c) n", p=P)).then_inc(o["weights"], 16)
                        sp.dma_start(wexp[0][1], w_expert_down[layer, bass.ds(ex, 1), :, :]
                                     .rearrange("a (c p) n -> p (a c) n", p=P)).then_inc(o["weights"], 16)
                if layer + 1 < DEPTH:
                    for n in range(3):
                        load_slab(layer + 1, n)
                sp.wait_ge(s_moe, layer + 1)
                for t in range(NT):
                    src = pair_dram[4 * t * P:4 * (t + 1) * P, :].rearrange("(p a) n -> p (a n)", a=4)
                    sp.dma_start(yc[t], src).then_inc(s_yc[t], 16)

            fw = at(EXPERT, D)
            sp.wait_ge(s_yf, DEPTH * NE)
            sp.dma_start(fw, norm_final_w.rearrange("(a n) -> a n", a=1).broadcast_to([P, D])).then_inc(s_fw, 16)
            for t in range(NT):
                sp.wait_ge(s_fin, t + 1)
                sp.dma_start(out[0, t * P:(t + 1) * P, :], at(MX0 + t * D, D)).then_inc(s_out, 16)
            sp.wait_ge(s_out, 16 * NT)

        @block.gpsimd
        def _(pool):
            for layer in range(DEPTH):
                if layer > 0:
                    pool.wait_ge(s_xready, NT * (layer + 1))
                nc.gpsimd.memset(qT[FD:FD + 1, :, :], 1.0).then_inc(s_ones, 1)
                for t in range(NT):
                    pool.wait_ge(s_xn2, layer * NT + t + 1)
                    pool.dma_start(rows_dram[2 * t * P:2 * (t + 1) * P, :].rearrange("(p a) n -> p (a n)", a=2),
                                   xn2[t % 2]).then_inc(s_rows[t % 2], 16)
                pool.wait_ge(s_tab, layer + 1)
                for i in range(2):
                    pool.wait_ge(s_rows[i], 16 * (NT // 2) * (layer + 1))

                def move(e, i):
                    nc.gpsimd.tensor_copy(gcur[:, i:i + 1], gath[:, bass.ds(e, 1)])
                    nc.gpsimd.tensor_copy(scur[:, i:i + 1], scat[:, bass.ds(e, 1)])
                    nc.gpsimd.tensor_copy(wcur[:, i:i + 1], wgt[:, bass.ds(e, 1)]).then_inc(s_idx, 1)
                    pool.wait_ge(s_idx, e + (layer * NE + 1))
                    pool.sem_inc(s_passed, 1)
                    pool.indirect_dma_start(out=xg[i], out_offset=None, in_=rows_dram,
                                            in_offset=bass.IndirectOffsetOnAxis(ap=gcur[:, i:i + 1], axis=0)
                                            ).then_inc(s_gat[i], 16)

                def scatter(e, i):
                    pool.wait_ge(s_y, e + (layer * NE + 1))
                    pool.sem_inc(s_passed, 1)
                    pool.indirect_dma_start(out=pair_dram,
                                            out_offset=bass.IndirectOffsetOnAxis(ap=scur[:, i:i + 1], axis=0),
                                            in_=yy[i], in_offset=None, bounds_check=2 * TOPK * T - 1,
                                            oob_is_err=False).then_inc(s_sc[i], 16)

                for e in range(RING - 1):
                    move(e, e)

                def step(e, i, full_step, turns):
                    if full_step:
                        g = (i + 2) % RING
                        if turns is not None:
                            pool.wait_ge(s_xtf, e + layer * NE)
                            pool.wait_ge(s_sc[g], turns)
                        move(e + 2, g)
                    scatter(e, i)

                def per(i):
                    return len(range(i, NE, RING))

                step(0, 0, True, None)
                step(1, 1, True, 16 * (layer * per(0) + 1))
                step(2, 2, True, 16 * (layer * per(1) + 1))
                with pool.Fori(1, (NE - RING + 1) // RING) as q:
                    for i in range(RING):
                        g = (i + 2) % RING
                        step(q * RING + i, i, True, (q + (layer * per(g) + (1 if i else 0))) * 16)
                for e in range(RING * ((NE - RING + 1) // RING), NE):
                    i = e % RING
                    g = (i + 2) % RING
                    step(e, i, e + 2 < NE, 16 * (layer * per(g) + e // RING + (1 if i else 0)))

                o = ov[layer]
                n_more = pool.value_load(ovn[0:1, 0:1], min_val=0, max_val=NOV)
                pool.wait_ge(s_sc[0], 16 * (layer + 1) * per(0))
                with pool.Fori(0, NOV) as j:
                    with pool.If(n_more > j):
                        nc.gpsimd.tensor_copy(gcur[:, 3:4], gath[:, bass.ds(j + NE, 1)])
                        nc.gpsimd.tensor_copy(scur[:, 3:4], scat[:, bass.ds(j + NE, 1)])
                        nc.gpsimd.tensor_copy(wcur[:, 3:4], wgt[:, bass.ds(j + NE, 1)]).then_inc(o["idx"], 1)
                        pool.wait_ge(o["idx"], j + 1)
                        pool.sem_inc(s_passed, 1)
                        pool.indirect_dma_start(out=xg[0], out_offset=None, in_=rows_dram,
                                                in_offset=bass.IndirectOffsetOnAxis(ap=gcur[:, 3:4], axis=0)
                                                ).then_inc(o["gathered"], 16)
                        pool.wait_ge(o["out"], j + 1)
                        pool.sem_inc(s_passed, 1)
                        pool.indirect_dma_start(out=pair_dram,
                                                out_offset=bass.IndirectOffsetOnAxis(ap=scur[:, 3:4], axis=0),
                                                in_=yy[0], in_offset=None, bounds_check=2 * TOPK * T - 1,
                                                oob_is_err=False).then_inc(o["scattered"], 16)
                        pool.wait_ge(o["scattered"], (j + 1) * 16)
                        pool.sem_inc(s_passed, 1)
                for i in range(RING):
                    pool.wait_ge(s_sc[i], 16 * (layer + 1) * per(i))
                pool.sem_inc(s_moe, 1)

        @block.scalar
        def _(act):
            chain = [0]

            def link(ins):
                chain[0] += 1
                ins.then_inc(s_act, 1)
                act.wait_ge(s_act, chain[0])

            def rstd(src, t, junk, sig):
                link(nc.scalar.activation(junk, src, ACT.Square, accum_out=stat[:, t:t + 1]))
                link(nc.scalar.activation(stat[:, 8 + t:9 + t], stat[:, t:t + 1], ACT.Ln, bias=k("eps"),
                                          scale=1.0 / D))
                nc.scalar.activation(stat[:, 16 + t:17 + t], stat[:, 8 + t:9 + t], ACT.Exp, scale=-0.5
                                     ).then_inc(sig, 1)

            act.wait_ge(s_const, 16)
            for layer in range(DEPTH):
                act.preload_act_table_set("natural_log_exp_and_others")
                for t in range(NT):
                    if layer == 0:
                        act.wait_ge(s_x, 16 * NT)
                    else:
                        act.wait_ge(s_xready, layer * NT + t + 1)
                    rstd(xres[:, t, :], t, at(PB0, D), s_rstd)
                if layer == 0:
                    act.wait_ge(s_small, 16 * 4 * DEPTH * 2)
                rot = layer * 2 * RH
                gate = layer * RH
                srow = layer * FH * NT
                for s in STEPS:
                    kind = s[0]
                    if kind == "normT":
                        c = s[1]
                        if c % 2 == 0:
                            b, n = result(s, layer)
                            is_full(act, s, layer)
                            nc.scalar.activation(hT[:, c, :], bank[b][:, :], ACT.Copy,
                                                 scale=nmw[:, layer, c:c + 1]).then_inc(freed[b], 2)
                    elif kind == "ff":
                        act.wait_ge(s_fz, layer + 1)
                        link(nc.scalar.activation(at(TA0 + T, T, FH), at(PB0 + T, T, FH), ACT.Exp, scale=-1.0))
                        nc.scalar.activation(at(PB0 + 2 * T, T, FH), at(TA0 + T, T, FH), ACT.Ln,
                                             bias=k("one")[0:FH, :]).then_inc(s_fl, 1)
                    elif kind == "fq":
                        b, n = result(s, layer)
                        is_full(act, s, layer)
                        for i in range(2):
                            nc.scalar.activation(qT[0:FD, 2 * s[1] + i, :], bank[b][i * FD:(i + 1) * FD, :], ACT.Copy,
                                                 scale=FD ** -0.5).then_inc(freed[b], 1)
                    elif kind in ("fv", "rv"):
                        b, n = result(s, layer)
                        is_full(act, s, layer)
                        dst = fv if kind == "fv" else rv
                        nc.scalar.activation(dst[:, s[1], :], bank[b][:, :], ACT.Copy).then_inc(freed[b], 2)
                    elif kind in ("rq", "rk"):
                        b, n = result(s, layer)
                        is_full(act, s, layer)
                        if rot >= 2:
                            act.wait_ge(s_rot, rot - 1)
                        half = RD // 2
                        nc.scalar.activation(tmp[rot % 2][0:half, :], bank[b][half:RD, :], ACT.Copy
                                             ).then_inc(s_swap, 1)
                        nc.scalar.activation(tmp[rot % 2][half:RD, :], bank[b][0:half, :], ACT.Copy
                                             ).then_inc(s_swap, 1)
                        rot += 1
                    elif kind == "rg":
                        b, n = result(s, layer)
                        is_full(act, s, layer)
                        if s[1] == 0:
                            act.wait_ge(s_rot, rot)
                        if gate:
                            act.wait_ge(s_gate, gate)
                        nc.scalar.activation(tmp[0], bank[b][:, :], ACT.Exp, scale=-1.0).then_inc(s_gexp, 1)
                        gate += 1
                    elif kind == "S":
                        h, qb = s[1], s[2]
                        srow += 1
                        b, n = result(s, layer)
                        act.wait_ge(s_max, srow)
                        if srow > 2:
                            act.wait_ge(s_prob, srow - 2)
                        nc.scalar.activation(prob[h % 2][:, pblk(qb):pblk(qb) + P * (qb + 1)],
                                             bank[b][:, 0:P * (qb + 1)], ACT.Exp,
                                             bias=rowsum[:, srow % 2:srow % 2 + 1],
                                             accum_out=rowsum[:, 2 + srow % 2:3 + srow % 2]).then_inc(s_exp, 1)
                    elif kind == "PT":
                        h, j = s[1], s[2]
                        b, n = result(s, layer)
                        is_full(act, s, layer)
                        nc.scalar.activation(probT[:, tblk(j):tblk(j) + T - P * j], bank[b][:, P * j:T], ACT.Copy
                                             ).then_inc(freed[b], 2)
                    elif kind == "PV" and s[1] % 2 and s[2] == NT - 1:
                        m = s[1] // 2
                        b, n = result(("O", m), layer)
                        is_full(act, ("O", m), layer)
                        nc.scalar.activation(mixed[:, m, :], bank[b][:, :], ACT.Copy).then_inc(freed[b], 2)
                    elif kind == "RV":
                        r = s[1]
                        b, n = result(s, layer)
                        is_full(act, s, layer)
                        if r < 2:
                            act.wait_ge(s_gate, gate)
                        else:
                            act.wait_ge(s_ret, layer * RH + r - 1)
                        nc.scalar.activation(tmp[r % 2], bank[b][:, :], ACT.Square).then_inc(s_sq, 1)
                        nc.scalar.activation(probT[:, T * (r % 2):T * (r % 2 + 1)], bank[b][:, :], ACT.Copy
                                             ).then_inc(freed[b], 2)
                    elif kind == "RN":
                        r = s[1]
                        b, n = result(s, layer)
                        is_full(act, s, layer)
                        m = mixed[:, RH + r, :]
                        link(nc.scalar.activation(m, bank[b][:, :], ACT.Ln, bias=k("eps"), scale=1.0 / RD))
                        nc.scalar.activation(m, m, ACT.Exp, scale=-0.5).then_inc(s_rln, 1)
                    elif kind == "wo" and s[2] == 1:
                        t = s[1]
                        act.wait_ge(s_xmid, layer * NT + t + 1)
                        if t >= 2:
                            is_full(act, ("fT", t - 2, 1), layer)
                            act.wait_ge(s_rows[t % 2], 16 * (layer * (NT // 2) + t // 2))
                        rstd(xres[:, t, :], t, xn2[t % 2], s_rstd2)

                act.wait_ge(s_rin, 2 * layer + 1)
                nc.scalar.activation(gs, gs, ACT.Exp).then_inc(s_rexp, 1)
                act.wait_ge(s_rin, 2 * layer + 2)
                nc.scalar.activation(ed, ed, ACT.Exp).then_inc(s_rexp, 1)
                act.preload_act_table_set("silu_and_others")

                act.wait_ge(s_tab, layer + 1)

                def expert(e, i, scattered):
                    act.wait_ge(s_gu, e + (layer * NE + 1))
                    nc.scalar.activation(sg, bank[1][:, 0:256], ACT.Silu).then_inc(s_sg, 1)
                    act.wait_ge(s_yf, e + (layer * NE + 1))
                    act.wait_ge(s_idx, e + (layer * NE + 1))
                    if scattered is not None:
                        act.wait_ge(s_sc[i], scattered)
                    nc.scalar.activation(yy[i], bank[3][:, :], ACT.Copy, scale=wcur[:, i:i + 1]).then_inc(s_y, 1)

                def per(i):
                    return len(range(i, NE, RING))

                for e in range(RING):
                    expert(e, e, None)
                with act.Fori(1, NE // RING) as q:
                    for i in range(RING):
                        expert(q * RING + i, i, (q + layer * per(i)) * 16)
                for e in range(RING * (NE // RING), NE):
                    expert(e, e % RING, 16 * (e // RING + layer * per(e % RING)))

                o = ov[layer]
                n_more = act.value_load(ovn[0:1, 0:1], min_val=0, max_val=NOV)
                act.wait_ge(s_sc[0], 16 * (layer + 1) * per(0))
                with act.Fori(0, NOV) as j:
                    with act.If(n_more > j):
                        act.wait_ge(o["gate_up"], j + 1)
                        nc.scalar.activation(sg, bank[1][:, 0:256], ACT.Silu).then_inc(o["silu"], 1)
                        act.wait_ge(o["down"], j + 1)
                        nc.scalar.activation(yy[0], bank[3][:, :], ACT.Copy, scale=wcur[:, 3:4]).then_inc(o["out"], 1)

            act.preload_act_table_set("natural_log_exp_and_others")
            for t in range(NT):
                act.wait_ge(s_xready, DEPTH * NT + t + 1)
                rstd(xres[:, t, :], t, at(PB0, D), s_rstd)

        @block.vector
        def _(dve):
            chain = [0]

            def link(ins):
                chain[0] += 1
                ins.then_inc(s_dve, 1)
                dve.wait_ge(s_dve, chain[0])

            tt, ts, red = nc.vector.tensor_tensor, nc.vector.tensor_scalar, nc.vector.tensor_reduce

            def ffn_rows(layer, t):
                dve.wait_ge(s_rstd2, layer * NT + t + 1)
                ts(xn2[t % 2], xres[:, t, :], stat[:, 16 + t:17 + t], None, ALU.mult).then_inc(s_xn2, 1)

            def over(v, n):
                return v.unsqueeze(1).broadcast_to([P, n, v.shape[1]])

            def each(v, n):
                return v.unsqueeze(len(v.shape)).broadcast_to([*v.shape, n])

            def first_of(scores, best, index, onehot, scratch, n):
                link(tt(scratch, scores, each(best, n), ALU.is_equal))
                link(tt(scratch, scratch, over(index, NT), ALU.mult))
                link(red(i1, scratch, AX.X, ALU.min))
                link(tt(onehot, over(index, NT), each(i1, n), ALU.is_equal))

            def route(layer):
                b, n = result(("lg",), layer)
                is_full(dve, ("lg",), layer)
                tt(lgt, bank[b][:, 0:NT * (NG + NE)].rearrange("p (t n) -> p t n", t=NT), over(rtb[:, layer, :], NT),
                   ALU.add).then_inc(freed[b], 2)
                is_taken(dve, ("lg",), layer)
                g_log = lgt[:, :, 0:NG]
                e_log = lgt[:, :, NG:].rearrange("p t (g e) -> p t g e", g=NG)
                link(red(gmax, g_log, AX.X, ALU.max))
                tt(gs, g_log, each(gmax, NG), ALU.subtract).then_inc(s_rin, 1)
                first_of(g_log, gmax, k("g"), og, gf, NG)
                link(tt(em, e_log, each(og, EPG), ALU.mult))
                link(red(ein, em.rearrange("p t g e -> p t e g"), AX.X, ALU.add))
                link(red(m1, ein, AX.X, ALU.max))
                first_of(ein, m1, k("o"), o1, ef, EPG)
                link(nc.vector.scalar_tensor_tensor(out=ein, in0=o1, scalar=NEG, in1=ein, op0=ALU.mult, op1=ALU.add))
                link(red(m2, ein, AX.X, ALU.max))
                tt(ed, m2, m1, ALU.subtract).then_inc(s_rin, 1)
                first_of(ein, m2, k("o"), o2, ef, EPG)
                for a, o_ in ((a1, o1), (a2, o2)):
                    link(tt(a, each(og, EPG), o_.unsqueeze(2).broadcast_to([P, NT, NG, EPG]), ALU.mult))
                ak = [a.rearrange("p t g e -> p t (g e)") for a in (a1, a2)]
                tt(asum, ak[0], ak[1], ALU.add).then_inc(s_hot, 1)
                dve.wait_ge(s_rexp, 2 * layer + 2)
                link(red(gsum, gs, AX.X, ALU.add))
                link(nc.vector.scalar_tensor_tensor(out=wden, in0=ed, scalar=1.0, in1=gsum, op0=ALU.add, op1=ALU.mult))
                link(nc.vector.reciprocal(wk[:, :, 0], wden))
                link(tt(wk[:, :, 1], wk[:, :, 0], ed, ALU.mult))
                b, n = result(("rank",), layer)
                is_full(dve, ("rank",), layer)
                link(nc.vector.tensor_copy(rank, bank[b][:, 0:NT * NE].rearrange("p (t e) -> p t e", t=NT)))
                nc.vector.tensor_copy(cnt, bank[b][:, NT * NE:(NT + 1) * NE]).then_inc(freed[b], 2)
                is_taken(dve, ("rank",), layer)
                link(tt(cmp_ov, each(cnt, MAXBLK - 1), over(k("over"), NE), ALU.is_ge))
                link(red(ovc, cmp_ov, AX.X, ALU.add))
                link(nc.vector.tensor_tensor_scan(cum, k("ones")[:, 0:NE], ovc, 0.0, ALU.mult, ALU.add))
                link(tt(ovb, cum, ovc, ALU.subtract))
                link(tt(cmp_blk, over(cum, NOV), each(k("blk"), NE), ALU.is_le))
                link(red(ovef, cmp_blk, AX.X, ALU.add))
                link(nc.vector.tensor_copy(ove[:, :], ovef[0:1, :]))
                link(nc.vector.tensor_copy(ovn[:, :], cum[0:1, NE - 1:NE]))
                for c in range(TOPK):
                    for i, v in enumerate((rank, over(ovb, NT), over(k("exp"), NT))):
                        link(tt(rsel, ak[c], v, ALU.mult))
                        link(red(pick[:, i, :, c], rsel, AX.X, ALU.add))
                flat = lambda v: v.rearrange("p t k -> p (t k)")
                p_rank, p_ovb, p_exp = (flat(pick[:, i, :, :]) for i in range(3))
                n_, r_, c_, m_ = flat(blkno), flat(rmod), flat(colno), flat(morethan)
                link(tt(cmp_st.rearrange("p t k m -> p (t k) m"), each(p_rank, MAXBLK - 1),
                        over(k("step"), NT * TOPK), ALU.is_ge))
                link(red(n_, cmp_st.rearrange("p t k m -> p (t k) m"), AX.X, ALU.add))
                link(nc.vector.scalar_tensor_tensor(out=r_, in0=n_, scalar=-float(SLOTS), in1=p_rank, op0=ALU.mult,
                                                    op1=ALU.add))
                link(tt(c_, p_ovb, n_, ALU.add))
                link(tt(c_, c_, p_exp, ALU.subtract))
                link(ts(m_, n_, 1.0, None, ALU.is_ge))
                link(nc.vector.scalar_tensor_tensor(out=c_, in0=c_, scalar=float(NE - 1), in1=m_, op0=ALU.add,
                                                    op1=ALU.mult))
                link(tt(c_, c_, p_exp, ALU.add))
                link(tt(hotR.rearrange("p t k s -> p (t k) s"), over(k("slot"), NT * TOPK), each(r_, P), ALU.is_equal))
                hc = [hotC[:, :, :, i, :].rearrange("p t k c -> p (t k) c") for i in range(3)]
                link(tt(hc[0], over(k("col"), NT * TOPK), each(c_, NCOL), ALU.is_equal))
                for c in range(TOPK):
                    link(tt(hotC[:, :, c, 1, :], hotC[:, :, c, 0, :], each(k("tok"), NCOL), ALU.mult))
                link(tt(hc[2], hc[0], each(flat(wk), NCOL), ALU.mult))
                tt(hc[0], hc[0], each(k("val"), NCOL), ALU.mult).then_inc(s_tabin, 1)
                for i in range(2):
                    dve.wait_ge(s_rows[i], 16 * (NT // 2) * (layer + 1))
                link(nc.vector.tensor_copy(wbig, each(nfw[:, layer, :].rearrange("p (h j) -> p j h", h=2), SLOTS)))
                b, n = result(("table",), layer)
                is_full(dve, ("table",), layer)
                val, tok, w_ = (bank[b][:, NCOL * i:NCOL * (i + 1)] for i in range(3))
                link(ts(gath[:, :], tok, 2.0, k("half"), ALU.mult, ALU.add))
                link(ts(tabs[:, 0:NCOL], val, 0.0, 1.0e6, ALU.is_equal, ALU.mult))
                link(ts(tabs[:, NCOL:2 * NCOL], val, 2.0, k("half"), ALU.mult, ALU.add))
                link(nc.vector.scalar_tensor_tensor(out=scat[:, :], in0=tabs[:, 0:NCOL], scalar=-2.0,
                                                    in1=tabs[:, NCOL:2 * NCOL], op0=ALU.add, op1=ALU.add))
                nc.vector.tensor_copy(wgt[:, :], w_).then_inc(freed[b], 2)
                is_taken(dve, ("table",), layer)
                dve.sem_inc(s_tab, 1)

            dve.wait_ge(s_const, 16)
            dve.wait_ge(s_x, 16 * NT)
            dve.wait_ge(s_small, 16 * 4 * DEPTH * 2)
            for layer in range(DEPTH):
                for t in range(NT):
                    dve.wait_ge(s_rstd, layer * NT + t + 1)
                    ts(xn_mix[:, t, :], xres[:, t, :], stat[:, 16 + t:17 + t], None, ALU.mult).then_inc(s_xn, 1)
                rot = layer * 2 * RH
                gate = layer * RH
                srow = layer * FH * NT
                for s in STEPS:
                    kind = s[0]
                    if kind == "normT" and s[1] % 2:
                        c = s[1]
                        b, n = result(s, layer)
                        is_full(dve, s, layer)
                        ts(hT[:, c, :], bank[b][:, :], nmw[:, layer, c:c + 1], None, ALU.mult).then_inc(freed[b], 2)
                    elif kind == "ff":
                        b, n = result(s, layer)
                        is_full(dve, s, layer)
                        z, az, ln = at(PB0, T, FH), at(PB0 + T, T, FH), at(PB0 + 2 * T, T, FH)
                        ts(z, bank[b][0:FH, :], fgb[:, layer:layer + 1], None, ALU.add).then_inc(freed[b], 2)
                        is_taken(dve, s, layer)
                        link(ts(at(PB0 + 3 * T, T, FH), z, -1.0, None, ALU.mult))
                        tt(az, z, at(PB0 + 3 * T, T, FH), ALU.max).then_inc(s_fz, 1)
                        link(ts(z, z, 0.0, None, ALU.min))
                        dve.wait_ge(s_fl, layer + 1)
                        link(tt(ln, ln, z, ALU.subtract))
                        dve.wait_ge(s_fz, layer + 1)
                        link(nc.vector.memset(az, 1.0))
                        nc.vector.tensor_tensor_scan(negc, az, ln, 0.0, ALU.mult, ALU.add).then_inc(s_ffc, 1)
                    elif kind == "fk":
                        b, n = result(s, layer)
                        is_full(dve, s, layer)
                        for i in range(2):
                            nc.vector.tensor_copy(kT[0:FD, 2 * s[1] + i, :], bank[b][i * FD:(i + 1) * FD, :]
                                                  ).then_inc(freed[b], 1)
                    elif kind in ("rq", "rk"):
                        b, n = result(s, layer)
                        if rot == 0:
                            dve.wait_ge(s_decay, 16 * 2)
                        dst = (rq if kind == "rq" else rk)[:, s[1], :]
                        is_full(dve, s, layer)
                        dve.wait_ge(s_swap, 2 * (rot + 1))
                        tt(dst, bank[b][:, :], cos, ALU.mult).then_inc(freed[b], 2)
                        link(tt(tmp[rot % 2], tmp[rot % 2], sin, ALU.mult))
                        is_taken(dve, s, layer)
                        tt(dst, dst, tmp[rot % 2], ALU.add).then_inc(s_rot, 1)
                        rot += 1
                    elif kind == "rg":
                        b, n = result(s, layer)
                        gate += 1
                        dve.wait_ge(s_gexp, gate)
                        link(ts(tmp[0], tmp[0], 1.0, None, ALU.add))
                        link(nc.vector.reciprocal(tmp[0], tmp[0]))
                        tt(rg[:, s[1], :], bank[b][:, :], tmp[0], ALU.mult).then_inc(s_gate, 1)
                        dve.wait_ge(s_gate, gate)
                        dve.sem_inc(freed[b], 2)
                    elif kind == "S":
                        h, qb = s[1], s[2]
                        srow += 1
                        b, n = result(s, layer)
                        is_full(dve, s, layer)
                        diag = bank[b][:, P * qb:P * (qb + 1)]
                        link(tt(diag, diag, k("mask"), ALU.add))
                        red(rowsum[:, srow % 2:srow % 2 + 1], bank[b][:, 0:P * (qb + 1)], AX.X, ALU.max, negate=True
                            ).then_inc(s_max, 1)
                        dve.wait_ge(s_exp, srow)
                        dve.sem_inc(freed[b], 2)
                        link(nc.vector.reciprocal(rowsum[:, 4:5], rowsum[:, 2 + srow % 2:3 + srow % 2]))
                        pr = prob[h % 2][:, pblk(qb):pblk(qb) + P * (qb + 1)]
                        ts(pr, pr, rowsum[:, 4:5], None, ALU.mult).then_inc(s_prob, 1)
                    elif kind == "RS":
                        r, j = s[1], s[2]
                        b, n = result(s, layer)
                        if r == 0 and j == 0:
                            dve.wait_ge(s_decay, 16 * (layer + 2))
                        is_full(dve, s, layer)
                        tt(prob[r % 2][:, tblk(j):tblk(j) + T - P * j], bank[b][:, P * j:T], dk[:, r, 0:T - P * j],
                           ALU.mult).then_inc(freed[b], 2)
                    elif kind == "RN":
                        r = s[1]
                        b, n = result(s, layer)
                        dve.wait_ge(s_rln, layer * RH + r + 1)
                        dve.sem_inc(freed[b], 2)
                        y, m = probT[:, T * (r % 2):T * (r % 2 + 1)], mixed[:, RH + r, :]
                        link(tt(y, y, rg[:, r, :], ALU.mult))
                        tt(m, m, y, ALU.mult).then_inc(s_ret, 1)
                    elif kind == "wo":
                        t, half = s[1], s[2]
                        if t and half:
                            ffn_rows(layer, t - 1)
                        b, n = result(s, layer)
                        is_full(dve, s, layer)
                        xs = xres[:, t, 512 * half:512 * (half + 1)]
                        tt(xs, xs, bank[b][:, :], ALU.add).then_inc(freed[b], 2)
                        if half:
                            is_taken(dve, ("wo", t, 0), layer)
                            is_taken(dve, s, layer)
                            dve.sem_inc(s_xmid, 1)
                    elif kind == "fT":
                        t, half = s[1], s[2]
                        if t == NT - 1 and half == 0:
                            ffn_rows(layer, t)
                        b, n = result(s, layer)
                        is_full(dve, s, layer)
                        w = nfw[:, layer, 4 * half:4 * (half + 1)].unsqueeze(2).broadcast_to([P, 4, P])
                        tt(hT2[t % 2][:, 4 * half:4 * (half + 1), :],
                           bank[b][:, :].rearrange("p (c t) -> p c t", c=4), w, ALU.mult).then_inc(freed[b], 2)

                route(layer)

                def expert(e, last):
                    dve.wait_ge(s_sg, e + (layer * NE + 1))
                    tt(hh, sg, bank[1][:, 256:512], ALU.mult).then_inc(s_h, 1)
                    if not last:
                        take_input(e + 1)
                    dve.wait_ge(s_hxf, e + (layer * NE + 1))
                    nc.vector.tensor_copy(at(HX0, 256), bank[2][:, 0:256]).then_inc(s_hx, 1)

                def take_input(e):
                    dve.wait_ge(s_xtf, e + (layer * NE + 1))
                    tt(at(XT0, 512), bank[0][:, :], at(WB0, 512), ALU.mult).then_inc(s_xt, 1)

                take_input(0)
                with dve.Fori(0, NE - 1) as e:
                    expert(e, False)
                expert(NE - 1, True)

                o = ov[layer]
                n_more = dve.value_load(ovn[0:1, 0:1], min_val=0, max_val=NOV)
                with dve.Fori(0, NOV) as j:
                    with dve.If(n_more > j):
                        dve.wait_ge(o["xt_full"], j + 1)
                        tt(at(XT0, 512), bank[0][:, :], at(WB0, 512), ALU.mult).then_inc(o["xt"], 1)
                        dve.wait_ge(o["silu"], j + 1)
                        tt(hh, sg, bank[1][:, 256:512], ALU.mult).then_inc(o["hidden"], 1)
                        dve.wait_ge(o["hx_full"], j + 1)
                        nc.vector.tensor_copy(at(HX0, 256), bank[2][:, 0:256]).then_inc(o["hx"], 1)

                if layer == 0:
                    dve.sem_inc(s_xready, NT)
                for t in range(NT):
                    dve.wait_ge(s_yc[t], 16 * (layer + 1))
                    link(tt(xres[:, t, :], xres[:, t, :], yc[t][:, 0:D], ALU.add))
                    tt(xres[:, t, :], xres[:, t, :], yc[t][:, D:2 * D], ALU.add).then_inc(s_xready, 1)
                    dve.wait_ge(s_xready, (layer + 1) * NT + t + 1)

            dve.wait_ge(s_fw, 16)
            for t in range(NT):
                dve.wait_ge(s_rstd, DEPTH * NT + t + 1)
                link(ts(at(MX0 + t * D, D), xres[:, t, :], stat[:, 16 + t:17 + t], None, ALU.mult))
                tt(at(MX0 + t * D, D), at(MX0 + t * D, D), at(EXPERT, D), ALU.mult).then_inc(s_fin, 1)

        @block.tensor
        def _(pe):
            mm, tr = nc.tensor.matmul, nc.tensor.transpose
            ident = k("ident")

            pe.wait_ge(s_const, 16)
            for layer in range(DEPTH):
                def slab_ready(n):
                    pe.wait_ge(s_slab[n % 3], 16 * (layer * (NSLAB // 3) + n // 3 + 1))

                srow = layer * FH * NT
                for s in STEPS:
                    kind = s[0]
                    if kind in ("PV", "lg"):
                        name = ("O", s[1] // 2) if kind == "PV" else ("lg",)
                        first = s[1] % 2 == 0 and s[2] == 0 if kind == "PV" else s[1] == 0
                    else:
                        name, first = s, True
                    b, n = result(name, layer)
                    o = bank[b]
                    if first:
                        may_fill(pe, name, layer)
                    if kind == "normT":
                        if s[1] == 0:
                            pe.wait_ge(s_xn, NT * (layer + 1))
                        for t in range(NT):
                            last = tr(o[:, P * t:P * (t + 1)], xn_mix[:, t, P * s[1]:P * (s[1] + 1)], ident)
                    elif kind == "ff":
                        if layer == 0:
                            pe.wait_ge(s_small, 16 * 4 * DEPTH * 2)
                        is_taken(pe, ("normT", KC - 2), layer)
                        is_taken(pe, ("normT", KC - 1), layer)
                        for c in range(KC):
                            last = mm(o[0:FH, :], ffw[:, layer, c, :], hT[:, c, :], start=(c == 0), stop=(c == KC - 1))
                    elif kind in ("fq", "fk", "rq", "rk", "rg"):
                        w = SLAB_OF[kind]
                        slab_ready(w)
                        for c in range(KC):
                            last = mm(o[:, :], slab[w % 3][:, c, P * s[1]:P * (s[1] + 1)], hT[:, c, :],
                                      start=(c == 0), stop=(c == KC - 1))
                    elif kind in ("fv", "rv"):
                        w = SLAB_OF[kind]
                        slab_ready(w)
                        for c in range(KC):
                            last = mm(o[:, :], hT[:, c, P * s[1]:P * (s[1] + 1)], slab[w % 3][:, c, :],
                                      start=(c == 0), stop=(c == KC - 1))
                    elif kind == "S":
                        h, qb = s[1], s[2]
                        if h == 0 and qb == 0:
                            pe.wait_ge(s_kaug, 16 * (layer + 1))
                            pe.wait_ge(s_ones, layer + 1)
                            for i in range(4):
                                is_taken(pe, ("fq", i), layer)
                                is_taken(pe, ("fk", i), layer)
                        last = mm(o[:, 0:P * (qb + 1)], qT[0:FD + 1, h, P * qb:P * (qb + 1)],
                                  kT[0:FD + 1, h, 0:P * (qb + 1)], start=True, stop=True)
                    elif kind == "PT":
                        h, j = s[1], s[2]
                        if j == 0:
                            pe.wait_ge(s_prob, layer * FH * NT + NT * (h + 1))
                        for qb in range(j, NT):
                            last = tr(o[:, P * qb:P * (qb + 1)],
                                      prob[h % 2][:, pblk(qb) + P * j:pblk(qb) + P * (j + 1)], ident)
                    elif kind == "PV":
                        h, j = s[1], s[2]
                        is_taken(pe, ("PT", h, j), layer)
                        if h == 0 and j == 0:
                            for t in range(NT):
                                is_taken(pe, ("fv", t), layer)
                        lo = FD * (h % 2)
                        last = mm(o[lo:lo + FD, P * j:T], fv[:, j, FD * h:FD * (h + 1)],
                                  probT[:, tblk(j):tblk(j) + T - P * j], start=(j == 0), stop=(j == NT - 1))
                    elif kind == "RS":
                        r, j = s[1], s[2]
                        pe.wait_ge(s_rot, layer * 2 * RH + RH + r + 1)
                        last = mm(o[:, P * j:T], rk[:, r, P * j:P * (j + 1)], rq[:, r, P * j:T], start=True, stop=True)
                    elif kind == "RV":
                        r = s[1]
                        for t in range(NT):
                            is_taken(pe, ("rv", t), layer)
                            is_taken(pe, ("RS", r, t), layer)
                        for j in range(NT):
                            last = mm(o[:, P * j:T], rv[:, j, RD * r:RD * (r + 1)],
                                      prob[r % 2][:, tblk(j):tblk(j) + T - P * j], start=(j == 0), stop=(j == NT - 1))
                    elif kind == "RN":
                        pe.wait_ge(s_sq, layer * RH + s[1] + 1)
                        last = mm(o[:, :], k("ones"), tmp[s[1] % 2], start=True, stop=True)
                    elif kind == "wo":
                        t, half = s[1], s[2]
                        if t == 0 and half == 0:
                            pe.wait_ge(s_ret, RH * (layer + 1))
                            for m in range(FH // 2):
                                is_taken(pe, ("O", m), layer)
                        slab_ready(7 + half)
                        for c in range(KC):
                            last = mm(o[:, :], mixed[:, c, P * t:P * (t + 1)], slab[(7 + half) % 3][:, c, :],
                                      start=(c == 0), stop=(c == KC - 1))
                    elif kind == "fT":
                        t, half = s[1], s[2]
                        pe.wait_ge(s_xn2, layer * NT + t + 1)
                        for c in range(4):
                            cc = 4 * half + c
                            last = tr(o[:, P * c:P * (c + 1)], xn2[t % 2][:, P * cc:P * (cc + 1)], ident)
                    elif kind == "lg":
                        t = s[1]
                        for half in range(2):
                            is_taken(pe, ("fT", t, half), layer)
                        w = NG + NE
                        for c in range(KC):
                            last = mm(o[:, w * t:w * (t + 1)], hT2[t % 2][:, c, :], rtw[:, layer, c, :],
                                      start=(c == 0), stop=(c == KC - 1))
                    elif kind == "rank":
                        pe.wait_ge(s_hot, layer + 1)
                        for t in range(NT):
                            dst = o[:, NE * t:NE * (t + 1)]
                            for u in range(t):
                                mm(dst, k("ones"), asum[:, u, :], start=(u == 0), stop=False)
                            mm(dst, k("lower"), asum[:, t, :], start=(t == 0), stop=True)
                        for t in range(NT):
                            last = mm(o[:, NE * NT:NE * (NT + 1)], k("ones"), asum[:, t, :], start=(t == 0),
                                      stop=(t == NT - 1))
                    elif kind == "table":
                        pe.wait_ge(s_tabin, layer + 1)
                        i = 0
                        for t in range(NT):
                            for c in range(TOPK):
                                last = mm(o[:, 0:3 * NCOL], hotR[:, t, c, :],
                                          hotC[:, t, c, :, :].rearrange("p v c -> p (v c)"),
                                          start=(i == 0), stop=(i == NT * TOPK - 1))
                                i += 1
                    if kind == "PV":
                        done = s[1] % 2 and s[2] == NT - 1
                    elif kind == "lg":
                        done = s[1] == NT - 1
                    else:
                        done = True
                    if done:
                        last.then_inc(full[b], 1)

                pe.wait_ge(s_tab, layer + 1)

                def input_transpose(e, i, gathered):
                    pe.wait_ge(s_gat[i], gathered)
                    for j in range(4):
                        last = tr(bank[0][:, P * j:P * (j + 1)], xg[i][:, P * j:P * (j + 1)], ident)
                    last.then_inc(s_xtf, 1)

                def gate_up(slot):
                    w = wexp[slot][0]
                    for c in range(KC):
                        for half in range(2):
                            last = mm(bank[1][SLOTS * half:SLOTS * (half + 1), :], xT[:, c % 4, c // 4, :],
                                      w[:, :, c, 256 * half:256 * (half + 1)], start=(c == 0), stop=(c == KC - 1))
                    return last

                def hidden_transpose():
                    for j in range(2):
                        last = tr(bank[2][:, P * j:P * (j + 1)], hh[:, P * j:P * (j + 1)], ident)
                    return last

                def down(slot):
                    w = wexp[slot][1]
                    for c in range(4):
                        for half in range(2):
                            last = mm(bank[3][SLOTS * half:SLOTS * (half + 1), :], hx[:, c % 2, c // 2, :],
                                      w[:, c, 512 * half:512 * (half + 1)], start=(c == 0), stop=(c == 3))
                    return last

                def expert(e, i, loads, next_gathered):
                    g = e + (layer * NE + 1)
                    pe.wait_ge(s_xt, g)
                    pe.wait_ge(s_w[i][0], loads * 2)
                    gate_up(i).then_inc(s_gu, 1)
                    if next_gathered is not None:
                        input_transpose(e + 1, (i + 1) % RING, next_gathered)
                    pe.wait_ge(s_h, g)
                    hidden_transpose().then_inc(s_hxf, 1)
                    pe.wait_ge(s_hx, g)
                    pe.wait_ge(s_w[i][1], loads)
                    down(i).then_inc(s_yf, 1)

                def per(i):
                    return len(range(i, NE, RING))

                input_transpose(0, 0, 16 * (layer * per(0) + 1))
                with pe.Fori(0, NE // RING) as q:
                    for i in range(RING):
                        nxt = (q + (layer * per((i + 1) % RING) + 1 + (1 if i == RING - 1 else 0))) * 16
                        expert(q * RING + i, i, (q + (layer * per(i) + 1)) * 16, nxt)
                for e in range(RING * (NE // RING), NE):
                    i = e % RING
                    nxt = None if e == NE - 1 else 16 * (layer * per((i + 1) % RING) + (e + 1) // RING + 1)
                    expert(e, i, 16 * (layer * per(i) + e // RING + 1), nxt)

                o = ov[layer]
                n_more = pe.value_load(ovn[0:1, 0:1], min_val=0, max_val=NOV)
                pe.wait_ge(s_y, (layer + 1) * NE)
                with pe.Fori(0, NOV) as j:
                    with pe.If(n_more > j):
                        pe.wait_ge(o["gathered"], (j + 1) * 16)
                        for c in range(4):
                            last = tr(bank[0][:, P * c:P * (c + 1)], xg[0][:, P * c:P * (c + 1)], ident)
                        last.then_inc(o["xt_full"], 1)
                        pe.wait_ge(o["xt"], j + 1)
                        pe.wait_ge(o["weights"], (j + 1) * 48)
                        gate_up(0).then_inc(o["gate_up"], 1)
                        pe.wait_ge(o["hidden"], j + 1)
                        hidden_transpose().then_inc(o["hx_full"], 1)
                        pe.wait_ge(o["hx"], j + 1)
                        down(0).then_inc(o["down"], 1)


_INS = ["x", "norm_mix_w", "w_in", "fox_forget_b", "w_out", "norm_ffn_w", "w_router_group", "b_router_group",
        "w_router_expert", "b_router_expert", "w_expert_gate", "w_expert_up", "w_expert_down", "norm_final_w"]


def kernel(**inputs):
    import numpy as _np
    import concourse.bacc as _bacc
    from concourse import mybir as _mybir
    from concourse.bass_utils import run_bass_kernel_spmd as _run

    nc = _bacc.Bacc("TRN2", target_bir_lowering=False, num_devices=1)
    arrays, args = {}, {}
    for name, a in [(n, _np.ascontiguousarray(inputs[n])) for n in _INS] + list(constants().items()):
        arrays[f"in_{name}_dram"] = a
        args[name] = nc.dram_tensor(f"in_{name}_dram", a.shape, _mybir.dt.from_np(a.dtype), kind="ExternalInput").ap()
    args["out"] = nc.dram_tensor("out_dram", (1, T, D), F32, kind="ExternalOutput").ap()
    trunk_kernel(nc, **args)
    r = _run(nc, [arrays], core_ids=[0])
    return r.results[0]["out_dram"]
```

```python
import numpy as np
import concourse.bass as bass
from concourse import mybir
from contextlib import ExitStack

F32 = mybir.dt.float32
F32R = mybir.dt.float32r
I32 = mybir.dt.int32
ALU = mybir.AluOpType
ACT = mybir.ActivationFunctionType
AX = mybir.AxisListType

P = 128
DEPTH, T, D = 2, 512, 1024
NT = T // P
KC = D // P
FH, FD = 8, 64
RH, RD = 4, 128
CHUNK = 64
NG, EPG, TOPK = 4, 8, 2
NE = NG * EPG
DE = D // 2
EPS = 1e-6
ROPE_BASE = 10000.0
NEG = -3.0e38

SLOTS = 64
MAXBLK = T // SLOTS
NOV = max(k for k in range(NE * MAXBLK)
          if min(k, NE) * (SLOTS + 1) + max(k - NE, 0) * SLOTS <= T * TOPK)
NCOL = NE + NOV + 1

EXPERT = 2 * KC * DE + (DE // P) * D
RING = 3
SLAB = KC * P
HT0 = 0
KT0 = HT0 + 2 * KC * T
FV0 = EXPERT
RQ0 = FV0 + NT * 512
RK0 = RQ0 + RH * T
RV0 = RK0 + RH * T
RG0 = RV0 + NT * 512
DK0 = RG0 + RH * T
RAW, CUT = 2, 3
WR0 = 2 * EXPERT
WS0 = WR0 + RAW * SLAB
QT0 = 3 * EXPERT - FH * T
WO0 = WR0
WK0 = RING * EXPERT
MX0 = WK0
PB0 = MX0 + KC * T
PLEN = P * NT * (NT + 1) // 2
PT0 = PB0 + 2 * PLEN
TA0 = PT0 + PLEN
CS0 = TA0 + 2 * T
AREA = CS0 + 2 * T
XN0 = PT0
XG0 = PB0
XT0 = XG0 + 3 * 512
SG0 = XT0 + 512
HH0 = SG0 + 256
HX0 = HH0 + 256
YY0 = HX0 + 256
WB0 = YY0 + 3 * 512
assert WB0 + 512 <= CS0 and DK0 + RH * T <= 2 * EXPERT and KT0 + FH * T <= EXPERT
assert WS0 + 2 * CUT * SLAB <= QT0 and WO0 + KC * D <= QT0
YC0 = EXPERT - NT * 2 * D


def pblk(qb):
    return P * qb * (qb + 1) // 2


def tblk(j):
    return sum(T - P * i for i in range(j))


def const_layout():
    parts = [("ident", P), ("mask", P), ("ones", P), ("lower", P), ("slot", P), ("col", NCOL), ("exp", NE),
             ("g", NG), ("o", EPG), ("over", MAXBLK - 1), ("step", MAXBLK - 1), ("blk", NOV),
             ("val", NT * TOPK), ("tok", NT), ("half", 1), ("eps", 1), ("one", 1)]
    at, out = 0, {}
    for name, n in parts:
        out[name] = (at, at + n)
        at += n
    return out, at


CONST, NCONST = const_layout()


def constants():
    p = np.arange(P)
    c = np.zeros((P, NCONST), np.float32)

    def put(name, v):
        c[:, CONST[name][0]:CONST[name][1]] = v

    put("ident", np.eye(P))
    put("mask", np.where(p[:, None] >= p[None, :], 0.0, NEG))
    put("ones", 1.0)
    put("lower", p[:, None] < p[None, :])
    put("slot", p % SLOTS)
    put("col", np.arange(NCOL))
    put("exp", np.arange(NE))
    put("g", np.arange(NG) - NG)
    put("o", np.arange(EPG) - EPG)
    put("over", SLOTS * np.arange(1, MAXBLK) + 1)
    put("step", SLOTS * np.arange(1, MAXBLK))
    put("blk", np.arange(NOV))
    tok = p[:, None] + P * np.arange(NT)[None]
    put("val", (TOPK * tok[:, None, :] + np.arange(TOPK)[:, None] + 1).reshape(P, -1))
    put("tok", tok)
    put("half", (p >= SLOTS)[:, None])
    put("eps", EPS)
    put("one", 1.0)
    half = RD // 2
    inv = (np.float32(1.0) / (np.float32(ROPE_BASE) ** (np.arange(half, dtype=np.float32) / np.float32(half)))).astype(np.float32)
    ang = inv[:, None] * np.arange(T, dtype=np.float32)[None, :]
    cos, sin = np.cos(ang), np.sin(ang)
    cs = np.concatenate([np.concatenate([cos, cos]), np.concatenate([-sin, sin])], axis=1).astype(np.float32)
    lg = np.log(1.0 - 2.0 ** (-5.0 - np.arange(RH)))
    l, j = np.arange(P)[:, None], np.arange(T)[None, :]
    power = np.where(l // CHUNK == j // CHUNK, np.abs(j - l), j - l)
    live = (l // CHUNK) <= (j // CHUNK)
    decay = np.where(live[None], np.exp(lg[:, None, None] * power[None]), 0.0) * RD ** -0.5
    decay = decay.transpose(1, 0, 2).reshape(P, RH * T).astype(np.float32)
    return {"const": c, "rope": cs, "decay": decay}


KINDS = ("fq", "fk", "fv", "rq", "rk", "rv", "rg")
FF_COL = 3 * FH * FD
UNITS = [("ff",)] + [(kind, i) for kind in KINDS for i in range(4)]
COLUMN = {("ff",): FF_COL}
COLUMN.update({(kind, i): 512 * n + P * i + (FH if n >= 3 else 0) for n, kind in enumerate(KINDS) for i in range(4)})
NU = len(UNITS)


def steps():
    out = [("normT", c) for c in range(KC)]
    groups = []
    for n, u in enumerate(UNITS):
        before = UNITS[n - 1]
        groups.append([u] + ([("vT", *before)] if before[0] in ("fv", "rv") else []))
    fox, ret = groups[:13], groups[13:]
    for g in fox:
        out += g
    for h in range(FH + 1):
        if h < FH:
            out += [("S", h, 0), ("S", h, 1)]
        if h:
            out += [("PT", h - 1, 0), ("PT", h - 1, 1)]
        if h < FH:
            out += ret[2 * h]
        else:
            out += [("RS", 0, 0), ("RS", 0, 1)]
        if h:
            out += [("PV", h - 1, 0), ("PV", h - 1, 1), ("PT", h - 1, 2), ("PT", h - 1, 3)]
        if h < FH:
            out += [("S", h, 2), ("S", h, 3)] + ret[2 * h + 1]
        if h:
            out += [("PV", h - 1, 2), ("PV", h - 1, 3)]
    out += [("RS", 0, 2), ("RS", 0, 3)]
    for r in range(RH):
        if r + 1 < RH:
            out += [("RS", r + 1, j) for j in range(NT)]
        out += [("RV", r)]
        if r:
            out += [("RN", r - 1)]
    out += [("RN", RH - 1)]
    out += [("wo", 0, 0), ("wo", 0, 1), ("wo", 1, 0), ("wo", 1, 1), ("fT", 0, 0), ("fT", 0, 1),
            ("wo", 2, 0), ("wo", 2, 1), ("lg", 0), ("fT", 1, 0), ("fT", 1, 1), ("wo", 3, 0), ("wo", 3, 1),
            ("lg", 1), ("fT", 2, 0), ("fT", 2, 1), ("lg", 2), ("fT", 3, 0), ("fT", 3, 1), ("lg", 3),
            ("rank",), ("table",)]
    return out


STEPS = steps()


def banks():
    acc, uses, where = 0, [0] * 8, {}
    for s in STEPS:
        kind = s[0]
        if kind == "S":
            b = 2 + s[2] % 2
        elif kind == "PT":
            b = 4 + s[2] % 2
        elif kind == "PV":
            s = ("O", s[1] // 2)
            b = 6
        elif kind == "vT":
            b = 7
        elif kind == "normT":
            b = s[1]
        elif kind == "RS":
            b = 2 + s[2]
        elif kind == "RV":
            b = 6 + s[1] % 2
        elif kind == "lg":
            s, b = ("lg",), 2
        elif kind == "rank":
            b = 3
        elif kind == "table":
            b = 4
        else:
            b = acc % 2
            acc += 1
        if s not in where:
            where[s] = (b, uses[b])
            uses[b] += 1
    return where, uses


WHERE, USES = banks()


def trunk_kernel(nc, x, norm_mix_w, w_in, fox_forget_b, w_out, norm_ffn_w, w_router_group, b_router_group,
                 w_router_expert, b_router_expert, w_expert_gate, w_expert_up, w_expert_down, norm_final_w,
                 const, rope, decay, out):
    with ExitStack() as ctx:
        def sb(name, shape, dt=F32):
            return ctx.enter_context(nc.sbuf_tensor(name, shape, dt))

        def sem(name):
            return ctx.enter_context(nc.semaphore(name))

        rows_dram = nc.dram_tensor("rows", [2 * T, 512], F32, kind="Internal").ap()
        pair_dram = nc.dram_tensor("pairs", [2 * TOPK * T, 512], F32, kind="Internal").ap()

        area = sb("area", [P, AREA])
        area_base = nc.sbuf_base - 4 * AREA
        xres = sb("xres", [P, NT, D])
        kst = sb("kst", [P, NCONST])
        rtw = sb("rtw", [P, DEPTH, KC, NG + NE])
        rtb = sb("rtb", [P, DEPTH, NG + NE])
        nmw = sb("nmw", [P, DEPTH, KC])
        nfw = sb("nfw", [P, DEPTH, KC])
        fgb = sb("fgb", [FH, DEPTH])
        stat = sb("stat", [P, 32])
        rowsum = sb("rowsum", [P, 16])
        gath = sb("gath", [P, NCOL], I32)
        scat = sb("scat", [P, NCOL], I32)
        wgt = sb("wgt", [P, NCOL])
        gcur = sb("gcur", [P, 4], I32)
        scur = sb("scur", [P, 4], I32)
        wcur = sb("wcur", [P, 4])
        ovn = sb("ovn", [1, 1], I32)
        ove = sb("ove", [1, NOV], I32)

        def k(name):
            return kst[:, CONST[name][0]:CONST[name][1]]

        def at(start, n, parts=P):
            return area[0:parts, start:start + n]


        def split(name, start, shape):
            return nc.alloc_sbuf_tensor_at(name, [P, *shape], F32R, offset=area_base + 4 * start)

        h_hi = split("h_hi", HT0, [KC, T])
        h_lo = split("h_lo", HT0 + KC * T, [KC, T])
        w_hi = [split(f"w_hi{i}", WS0 + 2 * i * SLAB, [KC, P]) for i in range(CUT)]
        w_lo = [split(f"w_lo{i}", WS0 + (2 * i + 1) * SLAB, [KC, P]) for i in range(CUT)]
        qT = at(QT0, FH * T).rearrange("p (h t) -> p h t", h=FH)
        kT = at(KT0, FH * T).rearrange("p (h t) -> p h t", h=FH)
        fv = at(FV0, NT * 512).rearrange("p (t n) -> p t n", t=NT)
        rq = at(RQ0, RH * T).rearrange("p (h t) -> p h t", h=RH)
        rk = at(RK0, RH * T).rearrange("p (h t) -> p h t", h=RH)
        rv = at(RV0, NT * 512).rearrange("p (t n) -> p t n", t=NT)
        rg = at(RG0, RH * T).rearrange("p (h t) -> p h t", h=RH)
        dk = at(DK0, RH * T).rearrange("p (h t) -> p h t", h=RH)
        slab = [at(WR0 + i * SLAB, SLAB).rearrange("p (c n) -> p c n", c=KC) for i in range(RAW)]
        wo = [at(WO0 + i * KC * 512, KC * 512).rearrange("p (c n) -> p c n", c=KC) for i in range(2)]
        mixed = at(MX0, KC * T).rearrange("p (c t) -> p c t", c=KC)
        xn_mix = at(MX0, NT * D).rearrange("p (t n) -> p t n", t=NT)
        prob = [at(PB0 + i * PLEN, PLEN) for i in range(2)]
        probT = at(PT0, PLEN)
        tmp = [at(TA0 + i * T, T) for i in range(2)]
        cos, sin = at(CS0, T), at(CS0 + T, T)
        hT2 = [at(PB0 + i * D, D).rearrange("p (c t) -> p c t", c=KC) for i in range(2)]
        xn2 = [at(XN0 + i * D, D) for i in range(2)]
        wexp = [(at(s * EXPERT, 2 * KC * DE).rearrange("p (g c n) -> p g c n", g=2, c=KC),
                 at(s * EXPERT + 2 * KC * DE, (DE // P) * D).rearrange("p (c n) -> p c n", n=D))
                for s in range(RING)]
        xg = [at(XG0 + i * 512, 512) for i in range(3)]
        xT = at(XT0, 512).rearrange("p (j h s) -> p j h s", j=4, h=2)
        sg, hh = at(SG0, 256), at(HH0, 256)
        hx = at(HX0, 256).rearrange("p (j h s) -> p j h s", j=2, h=2)
        yy = [at(YY0 + i * 512, 512) for i in range(3)]
        wbig = at(WB0, 512).rearrange("p (j h s) -> p j h s", j=4, h=2)
        yc = [at(YC0 + i * 2 * D, 2 * D) for i in range(NT)]
        negc = at(TA0, T, FH)

        free = [MX0]

        def rt(*shape):
            n = int(np.prod(shape))
            v = at(free[0], n)
            free[0] += n
            if len(shape) == 1:
                return v
            names = "abcd"[:len(shape)]
            return v.rearrange(f"p ({' '.join(names)}) -> p {' '.join(names)}",
                               **{c: s for c, s in zip(names, shape)})

        lgt = rt(NT, NG + NE)
        gs, gf, og = rt(NT, NG), rt(NT, NG), rt(NT, NG)
        em = rt(NT, NG, EPG)
        ein, ef, o1, o2 = rt(NT, EPG), rt(NT, EPG), rt(NT, EPG), rt(NT, EPG)
        a12 = rt(TOPK, NT, NG, EPG)
        a1, a2 = a12[:, 0, :, :, :], a12[:, 1, :, :, :]
        ASUM0 = free[0]
        asum = rt(NT + 1, NE)
        col1 = [rt(NT) for _ in range(8)]
        gmax, gsum, gidx, m1, m2, i1, ed, wden = col1
        wk = rt(TOPK, NT)
        rank, cnt = rt(NT, NE), rt(NE)
        ovc, cum, ovb = rt(NE), rt(NE), rt(NE)
        cmp_ov = rt(NE, MAXBLK - 1)
        cmp_blk = rt(NOV, NE)
        rsel = rt(TOPK, NT, NE)
        pick = rt(3, TOPK, NT)
        cmp_st = rt(TOPK * NT, MAXBLK - 1)
        blkno, rmod, colno, morethan = (rt(TOPK * NT) for _ in range(4))
        ovef = rt(NOV)
        tabs = rt(3 * NCOL)
        assert free[0] <= PB0
        routing_end = free[0]
        hotR = at(PB0, NT * TOPK * P).rearrange("p (k t s) -> p k t s", t=NT, k=TOPK)
        hotC = at(PB0 + NT * TOPK * P, 3 * NT * TOPK * NCOL).rearrange(
            "p (k t v c) -> p k t v c", t=NT, k=TOPK, v=3)
        assert PB0 + NT * TOPK * (P + 3 * NCOL) <= WB0

        bank = [ctx.enter_context(nc.psum_tensor(f"bank{i}", [P, 512], F32)) for i in range(8)]

        full = [sem(f"bank{i}_full") for i in range(8)]
        freed = [sem(f"bank{i}_free") for i in range(8)]
        s_const, s_small = sem("const_loaded"), sem("small_loaded")
        s_x = [sem(f"x{t}_loaded") for t in range(NT)]
        s_slab = [sem(f"slab{i}_loaded") for i in range(RAW)]
        s_whi, s_wlo = sem("slab_hi_ready"), sem("slab_lo_ready")
        s_hhi = sem("input_hi_ready")
        s_wo = [sem(f"w_out{i}_loaded") for i in range(2)]
        s_decay = sem("decay_loaded")
        s_fz = sem("forget_gate_abs_ready")
        s_fl = sem("forget_gate_ln_ready")
        s_ffc = sem("forget_sums_ready")
        s_kaug = sem("forget_sums_in_keys")
        s_ones = sem("query_ones_set")
        s_xready = sem("x_ready")
        s_rstd = sem("rstd_ready")
        s_xn = sem("xn_ready")
        s_max = sem("row_max_ready")
        s_exp = sem("exp_done")
        s_prob = sem("prob_ready")
        s_swap = sem("rope_swapped")
        s_rot = sem("rope_done")
        s_gexp = sem("gate_exp_done")
        s_gate = sem("gate_done")
        s_sd = sem("decayed_scores_ready")
        s_ro = sem("retention_out_ready")
        s_sq = sem("retention_square_ready")
        s_rln = sem("retention_rstd_ready")
        s_ret = sem("retention_done")
        s_xmid = sem("x_after_mixer")
        s_rstd2 = sem("ffn_rstd_ready")
        s_xn2 = sem("ffn_xn_ready")
        s_rows = [sem(f"rows{i}_saved") for i in range(2)]
        s_rin = sem("router_exp_asked")
        s_rexp = sem("router_exp_done")
        s_hot = sem("choices_ready")
        s_tabin = sem("one_hots_ready")
        s_tab = sem("tables_ready")
        s_wb = sem("ffn_weight_spread")
        s_w = [[sem(f"slot{s}_{n}_loaded") for n in ("gate_up", "down")] for s in range(RING)]
        s_idx, s_gat = sem("block_indices_ready"), [sem(f"rows_gathered{i}") for i in range(3)]
        s_xtf, s_xt = sem("block_transposed"), sem("block_input_ready")
        s_gu, s_sg, s_h = sem("gate_up_done"), sem("silu_done"), sem("hidden_ready")
        s_hxf, s_hx = sem("hidden_transposed"), sem("hidden_t_ready")
        s_yf, s_y = sem("down_done"), sem("block_output_ready")
        s_sc = [sem(f"rows_scattered{i}") for i in range(3)]
        s_moe = sem("all_blocks_scattered")
        s_yc = [sem(f"pairs{i}_loaded") for i in range(NT)]
        s_passed = sem("gpsimd_waits_passed")
        s_act = sem("scalar_chain")
        s_dve = sem("vector_chain")
        s_fw = sem("final_weight_loaded")
        s_fin = sem("final_rows_ready")
        s_out = sem("out_stored")
        ov = [{n: sem(f"further{l}_{n}") for n in (
            "idx", "gathered", "weights", "xt_full", "xt", "gate_up", "silu", "hidden", "hx_full", "hx",
            "down", "out", "scattered")} for l in range(DEPTH)]

        def result(name, layer):
            b, n = WHERE[name]
            return b, layer * USES[b] + n + 1

        def is_full(eng, name, layer):
            b, n = result(name, layer)
            eng.wait_ge(full[b], n)

        def is_taken(eng, name, layer):
            b, n = result(name, layer)
            eng.wait_ge(freed[b], 2 * n)

        def may_fill(eng, name, layer):
            b, n = result(name, layer)
            if not isinstance(n, int) or n > 1:
                eng.wait_ge(freed[b], 2 * (n - 1))

        block = ctx.enter_context(nc.Block())

        @block.sync
        def _(sp):
            sp.dma_start(kst[:, :], const).then_inc(s_const, 16)
            for t in range(NT):
                sp.dma_start(xres[:, t, :], x[0, t * P:(t + 1) * P, :]).then_inc(s_x[t], 16)
            def load_slab(layer, n):
                g = layer * NU + n
                if g >= RAW:
                    sp.wait_ge(s_wlo, g - RAW + 1)
                c = COLUMN[UNITS[n]]
                sp.dma_start(slab[g % RAW], w_in[layer, :, c:c + P].rearrange("(c p) n -> p c n", p=P)
                             ).then_inc(s_slab[g % RAW], 16)

            def load_gate_up(layer, e, slot):
                sp.dma_start(wexp[slot][0][:, 0, :, :], w_expert_gate[layer, bass.ds(e, 1), :, :]
                             .rearrange("a (c p) n -> p (a c) n", p=P)).then_inc(s_w[slot][0], 16)
                sp.dma_start(wexp[slot][0][:, 1, :, :], w_expert_up[layer, bass.ds(e, 1), :, :]
                             .rearrange("a (c p) n -> p (a c) n", p=P)).then_inc(s_w[slot][0], 16)

            def load_down(layer, e, slot):
                sp.dma_start(wexp[slot][1], w_expert_down[layer, bass.ds(e, 1), :, :]
                             .rearrange("a (c p) n -> p (a c) n", p=P)).then_inc(s_w[slot][1], 16)

            for layer in range(DEPTH):
                if layer == 0:
                    for n in range(RAW):
                        load_slab(layer, n)
                    for l in range(DEPTH):
                        sp.dma_start(nmw[:, l, :], norm_mix_w[l].rearrange("(c p) -> p c", p=P),
                                     allow_slow_non_contiguous=True).then_inc(s_small, 16)
                        sp.dma_start(nfw[:, l, :], norm_ffn_w[l].rearrange("(c p) -> p c", p=P),
                                     allow_slow_non_contiguous=True).then_inc(s_small, 16)
                        sp.dma_start(fgb[:, l:l + 1], fox_forget_b[l].rearrange("(h a) -> h a", a=1)).then_inc(s_small, 16)
                    for l in range(DEPTH):
                        sp.dma_start(rtw[:, l, :, 0:NG], w_router_group[l].rearrange("(c p) n -> p c n", p=P)
                                     ).then_inc(s_small, 16)
                        sp.dma_start(rtw[:, l, :, NG:], w_router_expert[l].rearrange("(c p) n -> p c n", p=P)
                                     ).then_inc(s_small, 16)
                        sp.dma_start(rtb[:, l, 0:NG], b_router_group[l:l + 1, :].broadcast_to([P, NG])
                                     ).then_inc(s_small, 16)
                        sp.dma_start(rtb[:, l, NG:], b_router_expert[l:l + 1, :].broadcast_to([P, NE])
                                     ).then_inc(s_small, 16)
                    sp.dma_start(at(CS0, 2 * T), rope).then_inc(s_decay, 16)
                if layer > 0:
                    sp.wait_ge(s_yf, layer * NE)
                sp.dma_start(at(DK0, RH * T), decay).then_inc(s_decay, 16)
                for n in range(RAW, RAW + CUT):
                    load_slab(layer, n)
                sp.wait_ge(s_ffc, layer + 1)
                sp.dma_start(kT[FD:FD + 1, :, :], negc).then_inc(s_kaug, 16)
                for n in range(RAW + CUT, NU):
                    load_slab(layer, n)
                is_full(sp, UNITS[-1], layer)
                for i in range(2):
                    sp.dma_start(wo[i], w_out[layer, :, 512 * i:512 * (i + 1)].rearrange("(c p) n -> p c n", p=P)
                                 ).then_inc(s_wo[i], 16)
                is_full(sp, ("RS", 0, 0), layer)
                load_gate_up(layer, 0, 0)
                load_down(layer, 0, 0)
                sp.wait_ge(s_ret, RH * (layer + 1))
                load_gate_up(layer, 1, 1)
                load_down(layer, 1, 1)
                is_full(sp, ("wo", 3, 1), layer)
                load_gate_up(layer, 2, 2)
                load_down(layer, 2, 2)

                def load_expert(e, slot):
                    sp.wait_ge(s_gu, e + (layer * NE - RING + 1))
                    load_gate_up(layer, e, slot)
                    sp.wait_ge(s_yf, e + (layer * NE - RING + 1))
                    load_down(layer, e, slot)

                with sp.Fori(RING, NE - NE % RING, RING) as e0:
                    for i in range(RING):
                        load_expert(e0 + i, i)
                for e in range(NE - NE % RING, NE):
                    load_expert(e, e % RING)

                sp.wait_ge(s_tab, layer + 1)
                n_more = sp.value_load(ovn[0:1, 0:1], min_val=0, max_val=NOV)
                sp.wait_ge(s_yf, (layer + 1) * NE - 1)
                o = ov[layer]
                with sp.Fori(0, NOV) as j:
                    with sp.If(n_more > j):
                        ex = sp.value_load(ove[0:1, bass.ds(j, 1)], min_val=0, max_val=NE - 1)
                        sp.wait_ge(o["idx"], j + 1)
                        sp.dma_start(wexp[0][0][:, 0, :, :], w_expert_gate[layer, bass.ds(ex, 1), :, :]
                                     .rearrange("a (c p) n -> p (a c) n", p=P)).then_inc(o["weights"], 16)
                        sp.dma_start(wexp[0][0][:, 1, :, :], w_expert_up[layer, bass.ds(ex, 1), :, :]
                                     .rearrange("a (c p) n -> p (a c) n", p=P)).then_inc(o["weights"], 16)
                        sp.dma_start(wexp[0][1], w_expert_down[layer, bass.ds(ex, 1), :, :]
                                     .rearrange("a (c p) n -> p (a c) n", p=P)).then_inc(o["weights"], 16)
                if layer + 1 < DEPTH:
                    for n in range(RAW):
                        load_slab(layer + 1, n)
                sp.wait_ge(s_moe, layer + 1)
                for t in range(NT):
                    src = pair_dram[4 * t * P:4 * (t + 1) * P, :].rearrange("(p a) n -> p (a n)", a=4)
                    sp.dma_start(yc[t], src).then_inc(s_yc[t], 16)

            fw = at(EXPERT, D)
            sp.wait_ge(s_yf, DEPTH * NE)
            sp.dma_start(fw, norm_final_w.rearrange("(a n) -> a n", a=1).broadcast_to([P, D])).then_inc(s_fw, 16)
            for t in range(NT):
                sp.wait_ge(s_fin, t + 1)
                sp.dma_start(out[0, t * P:(t + 1) * P, :], at(MX0 + t * D, D)).then_inc(s_out, 16)
            sp.wait_ge(s_out, 16 * NT)

        @block.gpsimd
        def _(pool):
            for layer in range(DEPTH):
                for n in range(NU):
                    g = layer * NU + n
                    pool.wait_ge(s_whi, g + 1)
                    nc.gpsimd.tensor_tensor(w_lo[g % CUT][:, :, :], slab[g % RAW], w_hi[g % CUT][:, :, :].bitcast(F32),
                                            ALU.subtract).then_inc(s_wlo, 1)
                    if n == 2:
                        pool.wait_ge(s_wlo, g + 1)
                        nc.gpsimd.memset(qT[FD:FD + 1, :, :], 1.0).then_inc(s_ones, 1)
                        pool.wait_ge(s_ones, layer + 1)
                for t in range(NT):
                    pool.wait_ge(s_xn2, layer * NT + t + 1)
                    pool.dma_start(rows_dram[2 * t * P:2 * (t + 1) * P, :].rearrange("(p a) n -> p (a n)", a=2),
                                   xn2[t % 2]).then_inc(s_rows[t % 2], 16)
                pool.wait_ge(s_tab, layer + 1)
                for i in range(2):
                    pool.wait_ge(s_rows[i], 16 * (NT // 2) * (layer + 1))

                def move(e, i):
                    nc.gpsimd.tensor_copy(gcur[:, i:i + 1], gath[:, bass.ds(e, 1)])
                    nc.gpsimd.tensor_copy(scur[:, i:i + 1], scat[:, bass.ds(e, 1)])
                    nc.gpsimd.tensor_copy(wcur[:, i:i + 1], wgt[:, bass.ds(e, 1)]).then_inc(s_idx, 1)
                    pool.wait_ge(s_idx, e + (layer * NE + 1))
                    pool.sem_inc(s_passed, 1)
                    pool.indirect_dma_start(out=xg[i], out_offset=None, in_=rows_dram,
                                            in_offset=bass.IndirectOffsetOnAxis(ap=gcur[:, i:i + 1], axis=0),
                                            bounds_check=2 * T - 1, oob_is_err=False).then_inc(s_gat[i], 16)

                def scatter(e, i):
                    pool.wait_ge(s_y, e + (layer * NE + 1))
                    pool.sem_inc(s_passed, 1)
                    pool.indirect_dma_start(out=pair_dram,
                                            out_offset=bass.IndirectOffsetOnAxis(ap=scur[:, i:i + 1], axis=0),
                                            in_=yy[i], in_offset=None, bounds_check=2 * TOPK * T - 1,
                                            oob_is_err=False).then_inc(s_sc[i], 16)

                for e in range(RING - 1):
                    move(e, e)

                def step(e, i, full_step, turns):
                    if full_step:
                        g = (i + 2) % RING
                        if turns is not None:
                            pool.wait_ge(s_xtf, e + layer * NE)
                            pool.wait_ge(s_sc[g], turns)
                        move(e + 2, g)
                    scatter(e, i)

                def per(i):
                    return len(range(i, NE, RING))

                step(0, 0, True, None)
                step(1, 1, True, 16 * (layer * per(0) + 1))
                step(2, 2, True, 16 * (layer * per(1) + 1))
                with pool.Fori(1, (NE - RING + 1) // RING) as q:
                    for i in range(RING):
                        g = (i + 2) % RING
                        step(q * RING + i, i, True, (q + (layer * per(g) + (1 if i else 0))) * 16)
                for e in range(RING * ((NE - RING + 1) // RING), NE):
                    i = e % RING
                    g = (i + 2) % RING
                    step(e, i, e + 2 < NE, 16 * (layer * per(g) + e // RING + (1 if i else 0)))

                o = ov[layer]
                n_more = pool.value_load(ovn[0:1, 0:1], min_val=0, max_val=NOV)
                pool.wait_ge(s_sc[0], 16 * (layer + 1) * per(0))
                with pool.Fori(0, NOV) as j:
                    with pool.If(n_more > j):
                        nc.gpsimd.tensor_copy(gcur[:, 3:4], gath[:, bass.ds(j + NE, 1)])
                        nc.gpsimd.tensor_copy(scur[:, 3:4], scat[:, bass.ds(j + NE, 1)])
                        nc.gpsimd.tensor_copy(wcur[:, 3:4], wgt[:, bass.ds(j + NE, 1)]).then_inc(o["idx"], 1)
                        pool.wait_ge(o["idx"], j + 1)
                        pool.sem_inc(s_passed, 1)
                        pool.indirect_dma_start(out=xg[0], out_offset=None, in_=rows_dram,
                                                in_offset=bass.IndirectOffsetOnAxis(ap=gcur[:, 3:4], axis=0),
                                                bounds_check=2 * T - 1, oob_is_err=False).then_inc(o["gathered"], 16)
                        pool.wait_ge(o["out"], j + 1)
                        pool.sem_inc(s_passed, 1)
                        pool.indirect_dma_start(out=pair_dram,
                                                out_offset=bass.IndirectOffsetOnAxis(ap=scur[:, 3:4], axis=0),
                                                in_=yy[0], in_offset=None, bounds_check=2 * TOPK * T - 1,
                                                oob_is_err=False).then_inc(o["scattered"], 16)
                        pool.wait_ge(o["scattered"], (j + 1) * 16)
                        pool.sem_inc(s_passed, 1)
                for i in range(RING):
                    pool.wait_ge(s_sc[i], 16 * (layer + 1) * per(i))
                pool.sem_inc(s_moe, 1)

        @block.scalar
        def _(act):
            chain = [0]

            def link(ins):
                chain[0] += 1
                ins.then_inc(s_act, 1)
                act.wait_ge(s_act, chain[0])

            def rstd(src, t, junk, sig):
                link(nc.scalar.activation(junk, src, ACT.Square, accum_out=stat[:, t:t + 1]))
                link(nc.scalar.activation(stat[:, 8 + t:9 + t], stat[:, t:t + 1], ACT.Ln, bias=k("eps"),
                                          scale=1.0 / D))
                nc.scalar.activation(stat[:, 16 + t:17 + t], stat[:, 8 + t:9 + t], ACT.Exp, scale=-0.5
                                     ).then_inc(sig, 1)

            act.wait_ge(s_const, 16)
            for layer in range(DEPTH):
                act.preload_act_table_set("natural_log_exp_and_others")

                def split_slab(n):
                    g = layer * NU + n
                    act.wait_ge(s_slab[g % RAW], 16 * (g // RAW + 1))
                    nc.scalar.activation(w_hi[g % CUT][:, :, :], slab[g % RAW], ACT.Copy).then_inc(s_whi, 1)

                if layer > 0:
                    for n in range(RAW):
                        split_slab(n)
                for t in range(NT):
                    if layer == 0:
                        act.wait_ge(s_x[t], 16)
                    else:
                        act.wait_ge(s_xready, layer * NT + t + 1)
                    rstd(xres[:, t, :], t, at(PB0, D), s_rstd)
                for n in range(RAW if layer else 0, CUT):
                    split_slab(n)
                if layer == 0:
                    act.wait_ge(s_small, 16 * 7 * DEPTH)
                rot = layer * 2 * RH
                gate = layer * RH
                srow = layer * FH * NT
                for s in STEPS:
                    kind = s[0]
                    if kind == "normT":
                        c = s[1]
                        b, n = result(s, layer)
                        is_full(act, s, layer)
                        nc.scalar.activation(h_hi[:, c, :], bank[b][:, :], ACT.Copy,
                                             scale=nmw[:, layer, c:c + 1]).then_inc(s_hhi, 1)
                    elif kind == "ff":
                        act.wait_ge(s_fz, layer + 1)
                        link(nc.scalar.activation(at(TA0 + T, T, FH), at(PB0 + T, T, FH), ACT.Exp, scale=-1.0))
                        nc.scalar.activation(at(PB0 + 2 * T, T, FH), at(TA0 + T, T, FH), ACT.Ln,
                                             bias=k("one")[0:FH, :]).then_inc(s_fl, 1)
                    elif kind == "fq":
                        b, n = result(s, layer)
                        is_full(act, s, layer)
                        for i in range(2):
                            nc.scalar.activation(qT[0:FD, 2 * s[1] + i, :], bank[b][i * FD:(i + 1) * FD, :], ACT.Copy,
                                                 scale=FD ** -0.5).then_inc(freed[b], 1)
                    elif kind in ("fv", "rv"):
                        b, n = result(s, layer)
                        is_full(act, s, layer)
                        if kind == "fv":
                            act.wait_ge(s_kaug, 16 * (layer + 1))
                        else:
                            act.wait_ge(s_rot, rot)
                        nc.scalar.activation(tmp[s[1] % 2], bank[b][:, :], ACT.Copy).then_inc(freed[b], 2)
                    elif kind == "vT":
                        b, n = result(s, layer)
                        is_full(act, s, layer)
                        dst = fv if s[1] == "fv" else rv
                        nc.scalar.activation(dst[:, :, P * s[2]:P * (s[2] + 1)],
                                             bank[b][:, :].rearrange("p (t c) -> p t c", t=NT), ACT.Copy
                                             ).then_inc(freed[b], 2)
                    elif kind in ("rq", "rk"):
                        b, n = result(s, layer)
                        is_full(act, s, layer)
                        if rot >= 2:
                            act.wait_ge(s_rot, rot - 1)
                        half = RD // 2
                        nc.scalar.activation(tmp[rot % 2][0:half, :], bank[b][half:RD, :], ACT.Copy
                                             ).then_inc(s_swap, 1)
                        nc.scalar.activation(tmp[rot % 2][half:RD, :], bank[b][0:half, :], ACT.Copy
                                             ).then_inc(s_swap, 1)
                        rot += 1
                    elif kind == "rg":
                        b, n = result(s, layer)
                        is_full(act, s, layer)
                        if gate:
                            act.wait_ge(s_gate, gate)
                        nc.scalar.activation(tmp[0], bank[b][:, :], ACT.Exp, scale=-1.0).then_inc(s_gexp, 1)
                        gate += 1
                    elif kind == "S":
                        h, qb = s[1], s[2]
                        srow += 1
                        b, n = result(s, layer)
                        act.wait_ge(s_max, srow)
                        if srow > 2:
                            act.wait_ge(s_prob, srow - 2)
                        nc.scalar.activation(prob[h % 2][:, pblk(qb):pblk(qb) + P * (qb + 1)],
                                             bank[b][:, 0:P * (qb + 1)], ACT.Exp,
                                             bias=rowsum[:, srow % 2:srow % 2 + 1],
                                             accum_out=rowsum[:, 2 + srow % 2:3 + srow % 2]).then_inc(s_exp, 1)
                    elif kind == "PT":
                        h, j = s[1], s[2]
                        b, n = result(s, layer)
                        is_full(act, s, layer)
                        nc.scalar.activation(probT[:, tblk(j):tblk(j) + T - P * j], bank[b][:, P * j:T], ACT.Copy
                                             ).then_inc(freed[b], 2)
                    elif kind == "PV" and s[1] % 2 and s[2] == NT - 1:
                        m = s[1] // 2
                        b, n = result(("O", m), layer)
                        is_full(act, ("O", m), layer)
                        nc.scalar.activation(mixed[:, m, :], bank[b][:, :], ACT.Copy).then_inc(freed[b], 2)
                    elif kind == "RV":
                        r = s[1]
                        b, n = result(s, layer)
                        is_full(act, s, layer)
                        if r < 2:
                            act.wait_ge(s_gate, gate)
                        else:
                            act.wait_ge(s_ret, layer * RH + r - 1)
                        nc.scalar.activation(tmp[r % 2], bank[b][:, :], ACT.Square).then_inc(s_sq, 1)
                        nc.scalar.activation(probT[:, T * (r % 2):T * (r % 2 + 1)], bank[b][:, :], ACT.Copy
                                             ).then_inc(freed[b], 2)
                    elif kind == "RN":
                        r = s[1]
                        b, n = result(s, layer)
                        is_full(act, s, layer)
                        m = mixed[:, RH + r, :]
                        link(nc.scalar.activation(m, bank[b][:, :], ACT.Ln, bias=k("eps"), scale=1.0 / RD))
                        nc.scalar.activation(m, m, ACT.Exp, scale=-0.5).then_inc(s_rln, 1)
                    elif kind == "wo" and s[2] == 1:
                        t = s[1]
                        act.wait_ge(s_xmid, layer * NT + t + 1)
                        if t >= 2:
                            is_full(act, ("fT", t - 2, 1), layer)
                            act.wait_ge(s_rows[t % 2], 16 * (layer * (NT // 2) + t // 2))
                        rstd(xres[:, t, :], t, xn2[t % 2], s_rstd2)
                    if s in UNITS and UNITS.index(s) + CUT < NU:
                        is_full(act, s, layer)
                        split_slab(UNITS.index(s) + CUT)

                act.wait_ge(s_rin, 2 * layer + 1)
                nc.scalar.activation(gs, gs, ACT.Exp).then_inc(s_rexp, 1)
                act.wait_ge(s_rin, 2 * layer + 2)
                nc.scalar.activation(ed, ed, ACT.Exp).then_inc(s_rexp, 1)
                act.preload_act_table_set("silu_and_others")

                act.wait_ge(s_tab, layer + 1)

                def expert(e, i, scattered):
                    act.wait_ge(s_gu, e + (layer * NE + 1))
                    nc.scalar.activation(sg, bank[1][:, 0:256], ACT.Silu).then_inc(s_sg, 1)
                    act.wait_ge(s_yf, e + (layer * NE + 1))
                    act.wait_ge(s_idx, e + (layer * NE + 1))
                    if scattered is not None:
                        act.wait_ge(s_sc[i], scattered)
                    nc.scalar.activation(yy[i], bank[3][:, :], ACT.Copy, scale=wcur[:, i:i + 1]).then_inc(s_y, 1)

                def per(i):
                    return len(range(i, NE, RING))

                for e in range(RING):
                    expert(e, e, None)
                with act.Fori(1, NE // RING) as q:
                    for i in range(RING):
                        expert(q * RING + i, i, (q + layer * per(i)) * 16)
                for e in range(RING * (NE // RING), NE):
                    expert(e, e % RING, 16 * (e // RING + layer * per(e % RING)))

                o = ov[layer]
                n_more = act.value_load(ovn[0:1, 0:1], min_val=0, max_val=NOV)
                act.wait_ge(s_sc[0], 16 * (layer + 1) * per(0))
                with act.Fori(0, NOV) as j:
                    with act.If(n_more > j):
                        act.wait_ge(o["gate_up"], j + 1)
                        nc.scalar.activation(sg, bank[1][:, 0:256], ACT.Silu).then_inc(o["silu"], 1)
                        act.wait_ge(o["down"], j + 1)
                        nc.scalar.activation(yy[0], bank[3][:, :], ACT.Copy, scale=wcur[:, 3:4]).then_inc(o["out"], 1)

            act.preload_act_table_set("natural_log_exp_and_others")
            for t in range(NT):
                act.wait_ge(s_xready, DEPTH * NT + t + 1)
                rstd(xres[:, t, :], t, at(PB0, D), s_rstd)

        @block.vector
        def _(dve):
            chain = [0]

            def link(ins):
                chain[0] += 1
                ins.then_inc(s_dve, 1)
                dve.wait_ge(s_dve, chain[0])

            tt, ts, red = nc.vector.tensor_tensor, nc.vector.tensor_scalar, nc.vector.tensor_reduce

            def ffn_rows(layer, t):
                dve.wait_ge(s_rstd2, layer * NT + t + 1)
                ts(xn2[t % 2], xres[:, t, :], stat[:, 16 + t:17 + t], None, ALU.mult).then_inc(s_xn2, 1)

            def over(v, n):
                return v.unsqueeze(1).broadcast_to([P, n, v.shape[1]])

            def each(v, n):
                return v.unsqueeze(len(v.shape)).broadcast_to([*v.shape, n])

            def first_of(scores, best, index, onehot, scratch, n):
                link(tt(scratch, scores, each(best, n), ALU.is_equal))
                link(tt(scratch, scratch, over(index, NT), ALU.mult))
                link(red(i1, scratch, AX.X, ALU.min))
                link(tt(onehot, over(index, NT), each(i1, n), ALU.is_equal))

            def route(layer):
                b, n = result(("lg",), layer)
                is_full(dve, ("lg",), layer)
                tt(lgt, bank[b][:, 0:NT * (NG + NE)].rearrange("p (t n) -> p t n", t=NT), over(rtb[:, layer, :], NT),
                   ALU.add).then_inc(freed[b], 2)
                is_taken(dve, ("lg",), layer)
                g_log = lgt[:, :, 0:NG]
                e_log = lgt[:, :, NG:].rearrange("p t (g e) -> p t g e", g=NG)
                link(red(gmax, g_log, AX.X, ALU.max))
                tt(gs, g_log, each(gmax, NG), ALU.subtract).then_inc(s_rin, 1)
                first_of(g_log, gmax, k("g"), og, gf, NG)
                link(tt(em, e_log, each(og, EPG), ALU.mult))
                link(red(ein, em.rearrange("p t g e -> p t e g"), AX.X, ALU.add))
                link(red(m1, ein, AX.X, ALU.max))
                first_of(ein, m1, k("o"), o1, ef, EPG)
                link(nc.vector.scalar_tensor_tensor(out=ein, in0=o1, scalar=NEG, in1=ein, op0=ALU.mult, op1=ALU.add))
                link(red(m2, ein, AX.X, ALU.max))
                tt(ed, m2, m1, ALU.subtract).then_inc(s_rin, 1)
                first_of(ein, m2, k("o"), o2, ef, EPG)
                for a, o_ in ((a1, o1), (a2, o2)):
                    link(tt(a, each(og, EPG), o_.unsqueeze(2).broadcast_to([P, NT, NG, EPG]), ALU.mult))
                ak = [a.rearrange("p t g e -> p t (g e)") for a in (a1, a2)]
                link(nc.vector.memset(asum[:, NT, :], 0.0))
                tt(asum[:, 0:NT, :], ak[0], ak[1], ALU.add).then_inc(s_hot, 1)
                dve.wait_ge(s_rexp, 2 * layer + 2)
                link(red(gsum, gs, AX.X, ALU.add))
                link(nc.vector.scalar_tensor_tensor(out=wden, in0=ed, scalar=1.0, in1=gsum, op0=ALU.add, op1=ALU.mult))
                link(nc.vector.reciprocal(wk[:, 0, :], wden))
                link(tt(wk[:, 1, :], wk[:, 0, :], ed, ALU.mult))
                def picked(i, v):
                    link(tt(rsel, a12.rearrange("p k t g e -> p k t (g e)"), v, ALU.mult))
                    link(red(pick[:, i, :, :], rsel, AX.X, ALU.add))
                    return pick[:, i, :, :].rearrange("p k t -> p (k t)")

                p_exp = picked(2, k("exp").unsqueeze(1).unsqueeze(1).broadcast_to([P, TOPK, NT, NE]))
                for i in range(2):
                    dve.wait_ge(s_rows[i], 16 * (NT // 2) * (layer + 1))
                link(nc.vector.tensor_copy(wbig, each(nfw[:, layer, :].rearrange("p (h j) -> p j h", h=2), SLOTS)))
                b, n = result(("rank",), layer)
                is_full(dve, ("rank",), layer)
                link(nc.vector.tensor_copy(rank, bank[b][:, 0:NT * NE].rearrange("p (t e) -> p t e", t=NT)))
                nc.vector.tensor_copy(cnt, bank[b][:, NT * NE:(NT + 1) * NE]).then_inc(freed[b], 2)
                is_taken(dve, ("rank",), layer)
                link(tt(cmp_ov, each(cnt, MAXBLK - 1), over(k("over"), NE), ALU.is_ge))
                link(red(ovc, cmp_ov, AX.X, ALU.add))
                link(nc.vector.tensor_tensor_scan(cum, k("ones")[:, 0:NE], ovc, 0.0, ALU.mult, ALU.add))
                link(tt(ovb, cum, ovc, ALU.subtract))
                p_rank = picked(0, rank.unsqueeze(1).broadcast_to([P, TOPK, NT, NE]))
                p_ovb = picked(1, ovb.unsqueeze(1).unsqueeze(1).broadcast_to([P, TOPK, NT, NE]))
                n_, r_, c_, m_ = blkno, rmod, colno, morethan
                link(tt(cmp_st, each(p_rank, MAXBLK - 1), over(k("step"), NT * TOPK), ALU.is_ge))
                link(red(n_, cmp_st, AX.X, ALU.add))
                link(nc.vector.scalar_tensor_tensor(out=r_, in0=n_, scalar=-float(SLOTS), in1=p_rank, op0=ALU.mult,
                                                    op1=ALU.add))
                link(tt(c_, p_ovb, n_, ALU.add))
                link(tt(c_, c_, p_exp, ALU.subtract))
                link(ts(m_, n_, 1.0, None, ALU.is_ge))
                link(nc.vector.scalar_tensor_tensor(out=c_, in0=c_, scalar=float(NE - 1), in1=m_, op0=ALU.add,
                                                    op1=ALU.mult))
                link(tt(c_, c_, p_exp, ALU.add))
                link(tt(hotR.rearrange("p k t s -> p (k t) s"), over(k("slot"), NT * TOPK), each(r_, P), ALU.is_equal))
                hc = [hotC[:, :, :, i, :].rearrange("p k t c -> p (k t) c") for i in range(3)]
                link(tt(hc[0], over(k("col"), NT * TOPK), each(c_, NCOL), ALU.is_equal))
                for c in range(TOPK):
                    link(tt(hotC[:, c, :, 1, :], hotC[:, c, :, 0, :], each(k("tok"), NCOL), ALU.mult))
                link(tt(hc[2], hc[0], each(wk.rearrange("p k t -> p (k t)"), NCOL), ALU.mult))
                tt(hc[0], hc[0], each(k("val"), NCOL), ALU.mult).then_inc(s_tabin, 1)
                link(tt(cmp_blk, over(cum, NOV), each(k("blk"), NE), ALU.is_le))
                link(red(ovef, cmp_blk, AX.X, ALU.add))
                link(nc.vector.tensor_copy(ove[:, :], ovef[0:1, :]))
                link(nc.vector.tensor_copy(ovn[:, :], cum[0:1, NE - 1:NE]))
                b, n = result(("table",), layer)
                is_full(dve, ("table",), layer)
                val, tok, w_ = (bank[b][:, NCOL * i:NCOL * (i + 1)] for i in range(3))
                link(ts(tabs[:, 0:NCOL], val, 0.0, 1.0e6, ALU.is_equal, ALU.mult))
                link(ts(tabs[:, NCOL:2 * NCOL], val, 2.0, k("half"), ALU.mult, ALU.add))
                link(ts(tabs[:, 2 * NCOL:], tok, 2.0, k("half"), ALU.mult, ALU.add))
                link(tt(gath[:, :], tabs[:, 2 * NCOL:], tabs[:, 0:NCOL], ALU.add))
                link(nc.vector.scalar_tensor_tensor(out=scat[:, :], in0=tabs[:, 0:NCOL], scalar=-2.0,
                                                    in1=tabs[:, NCOL:2 * NCOL], op0=ALU.add, op1=ALU.add))
                nc.vector.tensor_copy(wgt[:, :], w_).then_inc(freed[b], 2)
                is_taken(dve, ("table",), layer)
                dve.sem_inc(s_tab, 1)

            dve.wait_ge(s_const, 16)
            dve.wait_ge(s_small, 16 * 7 * DEPTH)
            for layer in range(DEPTH):
                for t in range(NT):
                    dve.wait_ge(s_rstd, layer * NT + t + 1)
                    ts(xn_mix[:, t, :], xres[:, t, :], stat[:, 16 + t:17 + t], None, ALU.mult).then_inc(s_xn, 1)
                rot = layer * 2 * RH
                gate = layer * RH
                srow = layer * FH * NT
                for s in STEPS:
                    kind = s[0]
                    if kind == "normT":
                        c = s[1]
                        b, n = result(s, layer)
                        dve.wait_ge(s_hhi, layer * KC + c + 1)
                        nc.vector.scalar_tensor_tensor(out=h_lo[:, c, :], in0=bank[b][:, :],
                                                       scalar=nmw[:, layer, c:c + 1], in1=h_hi[:, c, :].bitcast(F32),
                                                       op0=ALU.mult, op1=ALU.subtract).then_inc(freed[b], 2)
                    elif kind == "ff":
                        b, n = result(s, layer)
                        is_full(dve, s, layer)
                        z, az, ln = at(PB0, T, FH), at(PB0 + T, T, FH), at(PB0 + 2 * T, T, FH)
                        ts(z, bank[b][0:FH, :], fgb[:, layer:layer + 1], None, ALU.add).then_inc(freed[b], 2)
                        is_taken(dve, s, layer)
                        link(ts(at(PB0 + 3 * T, T, FH), z, -1.0, None, ALU.mult))
                        tt(az, z, at(PB0 + 3 * T, T, FH), ALU.max).then_inc(s_fz, 1)
                        link(ts(z, z, 0.0, None, ALU.min))
                        dve.wait_ge(s_fl, layer + 1)
                        link(tt(ln, ln, z, ALU.subtract))
                        dve.wait_ge(s_fz, layer + 1)
                        link(nc.vector.memset(az, 1.0))
                        nc.vector.tensor_tensor_scan(negc, az, ln, 0.0, ALU.mult, ALU.add).then_inc(s_ffc, 1)
                    elif kind == "fk":
                        b, n = result(s, layer)
                        is_full(dve, s, layer)
                        for i in range(2):
                            nc.vector.tensor_copy(kT[0:FD, 2 * s[1] + i, :], bank[b][i * FD:(i + 1) * FD, :]
                                                  ).then_inc(freed[b], 1)
                    elif kind in ("rq", "rk"):
                        b, n = result(s, layer)
                        if rot == 0:
                            dve.wait_ge(s_decay, 16 * 2)
                        dst = (rq if kind == "rq" else rk)[:, s[1], :]
                        is_full(dve, s, layer)
                        dve.wait_ge(s_swap, 2 * (rot + 1))
                        tt(dst, bank[b][:, :], cos, ALU.mult).then_inc(freed[b], 2)
                        link(tt(tmp[rot % 2], tmp[rot % 2], sin, ALU.mult))
                        is_taken(dve, s, layer)
                        tt(dst, dst, tmp[rot % 2], ALU.add).then_inc(s_rot, 1)
                        rot += 1
                    elif kind == "rg":
                        b, n = result(s, layer)
                        gate += 1
                        dve.wait_ge(s_gexp, gate)
                        link(ts(tmp[0], tmp[0], 1.0, None, ALU.add))
                        link(nc.vector.reciprocal(tmp[0], tmp[0]))
                        tt(rg[:, s[1], :], bank[b][:, :], tmp[0], ALU.mult).then_inc(s_gate, 1)
                        dve.wait_ge(s_gate, gate)
                        dve.sem_inc(freed[b], 2)
                    elif kind == "S":
                        h, qb = s[1], s[2]
                        srow += 1
                        b, n = result(s, layer)
                        is_full(dve, s, layer)
                        diag = bank[b][:, P * qb:P * (qb + 1)]
                        link(tt(diag, diag, k("mask"), ALU.add))
                        red(rowsum[:, srow % 2:srow % 2 + 1], bank[b][:, 0:P * (qb + 1)], AX.X, ALU.max, negate=True
                            ).then_inc(s_max, 1)
                        dve.wait_ge(s_exp, srow)
                        dve.sem_inc(freed[b], 2)
                        link(nc.vector.reciprocal(rowsum[:, 4:5], rowsum[:, 2 + srow % 2:3 + srow % 2]))
                        pr = prob[h % 2][:, pblk(qb):pblk(qb) + P * (qb + 1)]
                        ts(pr, pr, rowsum[:, 4:5], None, ALU.mult).then_inc(s_prob, 1)
                    elif kind == "RS":
                        r, j = s[1], s[2]
                        b, n = result(s, layer)
                        if r == 0 and j == 0:
                            dve.wait_ge(s_decay, 16 * (layer + 2))
                        is_full(dve, s, layer)
                        tt(prob[r % 2][:, tblk(j):tblk(j) + T - P * j], bank[b][:, P * j:T], dk[:, r, 0:T - P * j],
                           ALU.mult).then_inc(freed[b], 2)
                    elif kind == "RN":
                        r = s[1]
                        b, n = result(s, layer)
                        dve.wait_ge(s_rln, layer * RH + r + 1)
                        dve.sem_inc(freed[b], 2)
                        y, m = probT[:, T * (r % 2):T * (r % 2 + 1)], mixed[:, RH + r, :]
                        link(tt(y, y, rg[:, r, :], ALU.mult))
                        tt(m, m, y, ALU.mult).then_inc(s_ret, 1)
                    elif kind == "wo":
                        t, half = s[1], s[2]
                        if t and half:
                            ffn_rows(layer, t - 1)
                        b, n = result(s, layer)
                        is_full(dve, s, layer)
                        xs = xres[:, t, 512 * half:512 * (half + 1)]
                        tt(xs, xs, bank[b][:, :], ALU.add).then_inc(freed[b], 2)
                        if half:
                            is_taken(dve, ("wo", t, 0), layer)
                            is_taken(dve, s, layer)
                            dve.sem_inc(s_xmid, 1)
                    elif kind == "fT":
                        t, half = s[1], s[2]
                        if t == NT - 1 and half == 0:
                            ffn_rows(layer, t)
                        b, n = result(s, layer)
                        is_full(dve, s, layer)
                        w = nfw[:, layer, 4 * half:4 * (half + 1)].unsqueeze(2).broadcast_to([P, 4, P])
                        tt(hT2[t % 2][:, 4 * half:4 * (half + 1), :],
                           bank[b][:, :].rearrange("p (c t) -> p c t", c=4), w, ALU.mult).then_inc(freed[b], 2)

                route(layer)

                def expert(e, last):
                    dve.wait_ge(s_sg, e + (layer * NE + 1))
                    tt(hh, sg, bank[1][:, 256:512], ALU.mult).then_inc(s_h, 1)
                    if not last:
                        take_input(e + 1)
                    dve.wait_ge(s_hxf, e + (layer * NE + 1))
                    nc.vector.tensor_copy(at(HX0, 256), bank[2][:, 0:256]).then_inc(s_hx, 1)

                def take_input(e):
                    dve.wait_ge(s_xtf, e + (layer * NE + 1))
                    tt(at(XT0, 512), bank[0][:, :], at(WB0, 512), ALU.mult).then_inc(s_xt, 1)

                take_input(0)
                with dve.Fori(0, NE - 1) as e:
                    expert(e, False)
                expert(NE - 1, True)

                o = ov[layer]
                n_more = dve.value_load(ovn[0:1, 0:1], min_val=0, max_val=NOV)
                with dve.Fori(0, NOV) as j:
                    with dve.If(n_more > j):
                        dve.wait_ge(o["xt_full"], j + 1)
                        tt(at(XT0, 512), bank[0][:, :], at(WB0, 512), ALU.mult).then_inc(o["xt"], 1)
                        dve.wait_ge(o["silu"], j + 1)
                        tt(hh, sg, bank[1][:, 256:512], ALU.mult).then_inc(o["hidden"], 1)
                        dve.wait_ge(o["hx_full"], j + 1)
                        nc.vector.tensor_copy(at(HX0, 256), bank[2][:, 0:256]).then_inc(o["hx"], 1)

                if layer == 0:
                    dve.sem_inc(s_xready, NT)
                for t in range(NT):
                    dve.wait_ge(s_yc[t], 16 * (layer + 1))
                    link(tt(xres[:, t, :], xres[:, t, :], yc[t][:, 0:D], ALU.add))
                    tt(xres[:, t, :], xres[:, t, :], yc[t][:, D:2 * D], ALU.add).then_inc(s_xready, 1)
                    dve.wait_ge(s_xready, (layer + 1) * NT + t + 1)

            dve.wait_ge(s_fw, 16)
            for t in range(NT):
                dve.wait_ge(s_rstd, DEPTH * NT + t + 1)
                link(ts(at(MX0 + t * D, D), xres[:, t, :], stat[:, 16 + t:17 + t], None, ALU.mult))
                tt(at(MX0 + t * D, D), at(MX0 + t * D, D), at(EXPERT, D), ALU.mult).then_inc(s_fin, 1)

        @block.tensor
        def _(pe):
            mm, tr = nc.tensor.matmul, nc.tensor.transpose
            ident = k("ident")

            pe.wait_ge(s_const, 16)
            for layer in range(DEPTH):
                srow = layer * FH * NT
                for s in STEPS:
                    kind = s[0]
                    if kind in ("PV", "lg"):
                        name = ("O", s[1] // 2) if kind == "PV" else ("lg",)
                        first = s[1] % 2 == 0 and s[2] == 0 if kind == "PV" else s[1] == 0
                    else:
                        name, first = s, True
                    b, n = result(name, layer)
                    o = bank[b]
                    if first:
                        may_fill(pe, name, layer)
                    if kind == "normT":
                        if s[1] == 0:
                            pe.wait_ge(s_xn, NT * (layer + 1))
                        for t in range(NT):
                            last = tr(o[:, P * t:P * (t + 1)], xn_mix[:, t, P * s[1]:P * (s[1] + 1)], ident)
                    elif s in UNITS:
                        g = layer * NU + UNITS.index(s)
                        if kind == "ff":
                            for c in range(KC):
                                is_taken(pe, ("normT", c), layer)
                        pe.wait_ge(s_wlo, g + 1)
                        hi, lo = w_hi[g % CUT], w_lo[g % CUT]
                        for c in range(KC):
                            mm(o[:, :], hi[:, c, :], h_hi[:, c, :], start=(c == 0), stop=False)
                            mm(o[:, :], hi[:, c, :], h_lo[:, c, :], start=False, stop=False)
                            last = mm(o[:, :], lo[:, c, :], h_hi[:, c, :], start=False, stop=(c == KC - 1))
                    elif kind == "vT":
                        is_taken(pe, s[1:], layer)
                        for t in range(NT):
                            last = tr(o[:, P * t:P * (t + 1)], tmp[s[2] % 2][:, P * t:P * (t + 1)], ident)
                    elif kind == "S":
                        h, qb = s[1], s[2]
                        if h == 0 and qb == 0:
                            pe.wait_ge(s_kaug, 16 * (layer + 1))
                            pe.wait_ge(s_ones, layer + 1)
                            for i in range(4):
                                is_taken(pe, ("fq", i), layer)
                                is_taken(pe, ("fk", i), layer)
                        last = mm(o[:, 0:P * (qb + 1)], qT[0:FD + 1, h, P * qb:P * (qb + 1)],
                                  kT[0:FD + 1, h, 0:P * (qb + 1)], start=True, stop=True)
                    elif kind == "PT":
                        h, j = s[1], s[2]
                        if j == 0:
                            pe.wait_ge(s_prob, layer * FH * NT + NT * (h + 1))
                        for qb in range(j, NT):
                            last = tr(o[:, P * qb:P * (qb + 1)],
                                      prob[h % 2][:, pblk(qb) + P * j:pblk(qb) + P * (j + 1)], ident)
                    elif kind == "PV":
                        h, j = s[1], s[2]
                        is_taken(pe, ("PT", h, j), layer)
                        if h == 0 and j == 0:
                            for t in range(NT):
                                is_taken(pe, ("vT", "fv", t), layer)
                        lo = FD * (h % 2)
                        last = mm(o[lo:lo + FD, P * j:T], fv[:, j, FD * h:FD * (h + 1)],
                                  probT[:, tblk(j):tblk(j) + T - P * j], start=(j == 0), stop=(j == NT - 1))
                    elif kind == "RS":
                        r, j = s[1], s[2]
                        pe.wait_ge(s_rot, layer * 2 * RH + RH + r + 1)
                        last = mm(o[:, P * j:T], rk[:, r, P * j:P * (j + 1)], rq[:, r, P * j:T], start=True, stop=True)
                    elif kind == "RV":
                        r = s[1]
                        for t in range(NT):
                            is_taken(pe, ("vT", "rv", t), layer)
                            is_taken(pe, ("RS", r, t), layer)
                        for j in range(NT):
                            last = mm(o[:, P * j:T], rv[:, j, RD * r:RD * (r + 1)],
                                      prob[r % 2][:, tblk(j):tblk(j) + T - P * j], start=(j == 0), stop=(j == NT - 1))
                    elif kind == "RN":
                        pe.wait_ge(s_sq, layer * RH + s[1] + 1)
                        last = mm(o[:, :], k("ones"), tmp[s[1] % 2], start=True, stop=True)
                    elif kind == "wo":
                        t, half = s[1], s[2]
                        if t == 0 and half == 0:
                            pe.wait_ge(s_ret, RH * (layer + 1))
                            for m in range(FH // 2):
                                is_taken(pe, ("O", m), layer)
                        pe.wait_ge(s_wo[half], 16 * (layer + 1))
                        for c in range(KC):
                            last = mm(o[:, :], mixed[:, c, P * t:P * (t + 1)], wo[half][:, c, :],
                                      start=(c == 0), stop=(c == KC - 1))
                    elif kind == "fT":
                        t, half = s[1], s[2]
                        pe.wait_ge(s_xn2, layer * NT + t + 1)
                        for c in range(4):
                            cc = 4 * half + c
                            last = tr(o[:, P * c:P * (c + 1)], xn2[t % 2][:, P * cc:P * (cc + 1)], ident)
                    elif kind == "lg":
                        t = s[1]
                        for half in range(2):
                            is_taken(pe, ("fT", t, half), layer)
                        w = NG + NE
                        for c in range(KC):
                            last = mm(o[:, w * t:w * (t + 1)], hT2[t % 2][:, c, :], rtw[:, layer, c, :],
                                      start=(c == 0), stop=(c == KC - 1))
                    elif kind == "rank":
                        pe.wait_ge(s_hot, layer + 1)
                        rows = at(ASUM0, (NT + 1) * NE)
                        mm(o[:, 0:NE * (NT + 1)], k("lower"), rows, start=True, stop=False)
                        for u in range(1, NT + 1):
                            last = mm(o[:, NE * u:NE * (NT + 1)], k("ones"), rows[:, 0:NE * (NT + 1 - u)],
                                      start=False, stop=(u == NT))
                    elif kind == "table":
                        pe.wait_ge(s_tabin, layer + 1)
                        i = 0
                        for t in range(NT):
                            for c in range(TOPK):
                                last = mm(o[:, 0:3 * NCOL], hotR[:, c, t, :],
                                          hotC[:, c, t, :, :].rearrange("p v c -> p (v c)"),
                                          start=(i == 0), stop=(i == NT * TOPK - 1))
                                i += 1
                    if kind == "PV":
                        done = s[1] % 2 and s[2] == NT - 1
                    elif kind == "lg":
                        done = s[1] == NT - 1
                    else:
                        done = True
                    if done:
                        last.then_inc(full[b], 1)

                pe.wait_ge(s_tab, layer + 1)

                def input_transpose(e, i, gathered):
                    pe.wait_ge(s_gat[i], gathered)
                    for j in range(4):
                        last = tr(bank[0][:, P * j:P * (j + 1)], xg[i][:, P * j:P * (j + 1)], ident)
                    last.then_inc(s_xtf, 1)

                def gate_up(slot):
                    w = wexp[slot][0]
                    for c in range(KC):
                        for half in range(2):
                            last = mm(bank[1][SLOTS * half:SLOTS * (half + 1), :], xT[:, c % 4, c // 4, :],
                                      w[:, :, c, 256 * half:256 * (half + 1)], start=(c == 0), stop=(c == KC - 1))
                    return last

                def hidden_transpose():
                    for j in range(2):
                        last = tr(bank[2][:, P * j:P * (j + 1)], hh[:, P * j:P * (j + 1)], ident)
                    return last

                def down(slot):
                    w = wexp[slot][1]
                    for c in range(4):
                        for half in range(2):
                            last = mm(bank[3][SLOTS * half:SLOTS * (half + 1), :], hx[:, c % 2, c // 2, :],
                                      w[:, c, 512 * half:512 * (half + 1)], start=(c == 0), stop=(c == 3))
                    return last

                def expert(e, i, loads, next_gathered):
                    g = e + (layer * NE + 1)
                    pe.wait_ge(s_xt, g)
                    pe.wait_ge(s_w[i][0], loads * 2)
                    gate_up(i).then_inc(s_gu, 1)
                    if next_gathered is not None:
                        input_transpose(e + 1, (i + 1) % RING, next_gathered)
                    pe.wait_ge(s_h, g)
                    hidden_transpose().then_inc(s_hxf, 1)
                    pe.wait_ge(s_hx, g)
                    pe.wait_ge(s_w[i][1], loads)
                    down(i).then_inc(s_yf, 1)

                def per(i):
                    return len(range(i, NE, RING))

                input_transpose(0, 0, 16 * (layer * per(0) + 1))
                with pe.Fori(0, NE // RING) as q:
                    for i in range(RING):
                        nxt = (q + (layer * per((i + 1) % RING) + 1 + (1 if i == RING - 1 else 0))) * 16
                        expert(q * RING + i, i, (q + (layer * per(i) + 1)) * 16, nxt)
                for e in range(RING * (NE // RING), NE):
                    i = e % RING
                    nxt = None if e == NE - 1 else 16 * (layer * per((i + 1) % RING) + (e + 1) // RING + 1)
                    expert(e, i, 16 * (layer * per(i) + e // RING + 1), nxt)

                o = ov[layer]
                n_more = pe.value_load(ovn[0:1, 0:1], min_val=0, max_val=NOV)
                pe.wait_ge(s_y, (layer + 1) * NE)
                with pe.Fori(0, NOV) as j:
                    with pe.If(n_more > j):
                        pe.wait_ge(o["gathered"], (j + 1) * 16)
                        for c in range(4):
                            last = tr(bank[0][:, P * c:P * (c + 1)], xg[0][:, P * c:P * (c + 1)], ident)
                        last.then_inc(o["xt_full"], 1)
                        pe.wait_ge(o["xt"], j + 1)
                        pe.wait_ge(o["weights"], (j + 1) * 48)
                        gate_up(0).then_inc(o["gate_up"], 1)
                        pe.wait_ge(o["hidden"], j + 1)
                        hidden_transpose().then_inc(o["hx_full"], 1)
                        pe.wait_ge(o["hx"], j + 1)
                        down(0).then_inc(o["down"], 1)


_INS = ["x", "norm_mix_w", "w_in", "fox_forget_b", "w_out", "norm_ffn_w", "w_router_group", "b_router_group",
        "w_router_expert", "b_router_expert", "w_expert_gate", "w_expert_up", "w_expert_down", "norm_final_w"]


def kernel(**inputs):
    import numpy as _np
    import concourse.bacc as _bacc
    from concourse import mybir as _mybir
    from concourse.bass_utils import run_bass_kernel_spmd as _run

    nc = _bacc.Bacc("TRN2", target_bir_lowering=False, num_devices=1)
    arrays, args = {}, {}
    for name, a in [(n, _np.ascontiguousarray(inputs[n])) for n in _INS] + list(constants().items()):
        arrays[f"in_{name}_dram"] = a
        args[name] = nc.dram_tensor(f"in_{name}_dram", a.shape, _mybir.dt.from_np(a.dtype), kind="ExternalInput").ap()
    args["out"] = nc.dram_tensor("out_dram", (1, T, D), F32, kind="ExternalOutput").ap()
    trunk_kernel(nc, **args)
    r = _run(nc, [arrays], core_ids=[0])
    return r.results[0]["out_dram"]
```

```python
import numpy as np
import concourse.bass as bass
from concourse import mybir
from contextlib import ExitStack

F32 = mybir.dt.float32
F32R = mybir.dt.float32r
I32 = mybir.dt.int32
ALU = mybir.AluOpType
ACT = mybir.ActivationFunctionType
AX = mybir.AxisListType

P = 128
DEPTH, T, D = 2, 512, 1024
NT = T // P
KC = D // P
FH, FD = 8, 64
RH, RD = 4, 128
CHUNK = 64
NG, EPG, TOPK = 4, 8, 2
NE = NG * EPG
DE = D // 2
EPS = 1e-6
ROPE_BASE = 10000.0
NEG = -3.0e38

SLOTS = 64
MAXBLK = T // SLOTS
NOV = max(k for k in range(NE * MAXBLK)
          if min(k, NE) * (SLOTS + 1) + max(k - NE, 0) * SLOTS <= T * TOPK)
NMORE = NOV + NOV % 2
NCOL = NE + NMORE
EMPTY = 2 * TOPK * T
assert T & (T - 1) == 0

EXPERT = 2 * KC * DE + (DE // P) * D
RING = 3
TAIL = NE % RING or RING
SLAB = KC * P
HT0 = 0
KT0 = HT0 + 2 * KC * T
FV0 = EXPERT
RQ0 = FV0 + NT * 512
RK0 = RQ0 + RH * T
RV0 = RK0 + RH * T
RG0 = RV0 + NT * 512
DK0 = RG0 + RH * T
RAW, CUT = 2, 3
WR0 = 2 * EXPERT
WS0 = WR0 + RAW * SLAB
QT0 = 3 * EXPERT - FH * T
WO0 = WR0
WK0 = RING * EXPERT
MX0 = WK0
PB0 = MX0 + KC * T
PLEN = P * NT * (NT + 1) // 2
PT0 = PB0 + 2 * PLEN
TA0 = PT0 + PLEN
CS0 = TA0 + 2 * T
AREA = CS0 + 2 * T
XN0 = PT0
XG0 = PB0
XT0 = XG0 + 3 * 512
SG0 = XT0 + 512
HH0 = SG0 + 256
HX0 = HH0 + 256
YY0 = HX0 + 256
WB0 = YY0 + 3 * 512
assert PLEN <= (RH - 1) * T and WB0 + 512 <= CS0 and DK0 + RH * T <= 2 * EXPERT and KT0 + FH * T <= EXPERT
assert KC * T <= FH * T and KC * 512 <= KC * T
assert WS0 + 2 * CUT * SLAB <= QT0 and WO0 + KC * D <= QT0
FN0 = EXPERT
assert D <= 2 * T
YC0 = EXPERT - NT * 2 * D


def pblk(qb):
    return P * qb * (qb + 1) // 2


def tblk(j):
    return sum(T - P * i for i in range(j))


def const_layout():
    parts = [("ident", P), ("mask", P), ("ones", P), ("lower", P), ("slot", P),
             ("g", NG), ("o", EPG), ("over", MAXBLK - 1), ("step", MAXBLK - 1), ("blk", NMORE),
             ("row", TOPK * NT), ("off", 1), ("eps", 1), ("one", 1)]
    at, out = 0, {}
    for name, n in parts:
        out[name] = (at, at + n)
        at += n
    return out, at


CONST, NCONST = const_layout()


def constants():
    p = np.arange(P)
    c = np.zeros((P, NCONST), np.float32)

    def put(name, v):
        c[:, CONST[name][0]:CONST[name][1]] = v

    put("ident", np.eye(P))
    put("mask", np.where(p[:, None] >= p[None, :], 0.0, NEG))
    put("ones", 1.0)
    put("lower", p[:, None] < p[None, :])
    put("slot", p % SLOTS)
    put("g", np.arange(NG) - NG)
    put("o", np.arange(EPG) - EPG)
    put("over", SLOTS * np.arange(1, MAXBLK) + 1)
    put("step", SLOTS * np.arange(1, MAXBLK))
    put("blk", np.arange(NMORE) + 1)
    tok = p[:, None] + P * np.arange(NT)[None]
    put("row", (2 * T * np.arange(TOPK)[:, None] + tok[:, None, :]).reshape(P, -1) - EMPTY)
    put("off", (EMPTY + T * (p >= SLOTS))[:, None])
    put("eps", EPS)
    put("one", 1.0)
    half = RD // 2
    inv = (np.float32(1.0) / (np.float32(ROPE_BASE) ** (np.arange(half, dtype=np.float32) / np.float32(half)))).astype(np.float32)
    ang = inv[:, None] * np.arange(T, dtype=np.float32)[None, :]
    cos, sin = np.cos(ang), np.sin(ang)
    cs = np.concatenate([np.concatenate([cos, cos]), np.concatenate([-sin, sin])], axis=1).astype(np.float32)
    lg = np.log(1.0 - 2.0 ** (-5.0 - np.arange(RH)))
    l, j = np.arange(P)[:, None], np.arange(T)[None, :]
    power = np.where(l // CHUNK == j // CHUNK, np.abs(j - l), j - l)
    live = (l // CHUNK) <= (j // CHUNK)
    decay = np.where(live[None], np.exp(lg[:, None, None] * power[None]), 0.0) * RD ** -0.5
    decay = decay.transpose(1, 0, 2).reshape(P, RH * T).astype(np.float32)
    return {"const": c, "rope": cs, "decay": decay}


KINDS = ("fq", "fk", "fv", "rq", "rk", "rv", "rg")
FF_COL = 3 * FH * FD
UNITS = [("ff",)] + [(kind, i) for kind in KINDS for i in range(4)]
COLUMN = {("ff",): FF_COL}
COLUMN.update({(kind, i): 512 * n + P * i + (FH if n >= 3 else 0) for n, kind in enumerate(KINDS) for i in range(4)})
NU = len(UNITS)


def steps():
    out = [("normT", c) for c in range(KC)]
    groups = []
    for n, u in enumerate(UNITS):
        before = UNITS[n - 1]
        groups.append([u] + ([("vT", *before)] if before[0] in ("fv", "rv") else []))
    fox, ret = groups[:13], groups[13:]
    for g in fox:
        out += g
    for h in range(FH + 1):
        if h < FH:
            out += [("S", h, 0), ("S", h, 1)]
        if h:
            out += [("PT", h - 1, 0), ("PT", h - 1, 1)]
        if h < FH:
            out += ret[2 * h]
        else:
            out += [("RS", 0, 0), ("RS", 0, 1)]
        pair = [("PV", (h - 1) // 2, j) for j in range(NT)] if h and h % 2 == 0 else []
        out += pair[:2]
        if h:
            out += [("PT", h - 1, 2), ("PT", h - 1, 3)]
        if h < FH:
            out += [("S", h, 2), ("S", h, 3)] + ret[2 * h + 1]
        out += pair[2:]
    out += [("RS", 0, 2), ("RS", 0, 3)]
    leading = [[("mh", 0), ("ws", 0), ("ws", 1)], [("mh", 1), ("mh", 2), ("ws", 2), ("ws", 3)],
               [("mh", 3), ("mh", 4), ("ws", 4), ("ws", 5)], [("mh", 5), ("ws", 6), ("ws", 7)]]
    rest = [[], [("ml", 0)], [("ml", 1), ("ml", 2)], [("ml", 3), ("ml", 4)]]
    for r in range(RH):
        if r + 1 < RH:
            out += [("RS", r + 1, j) for j in range(NT)]
        out += rest[r] + [("RV", r)]
        if r:
            out += [("RN", r - 1)]
        out += leading[r]
    for i in range(4):
        for stage in range(3):
            at = out.index(("gate", i, stage - 1) if stage else ("rg", i)) + 2
            while out[at][0] not in ("S", "PT", "RS") or out[at][2] % 2:
                at += 1
            out.insert(at, ("gate", i, stage))
    out += [("begin", 0, 0), ("ml", 5), ("RN", RH - 1), ("mh", 6), ("ml", 6), ("begin", 0, 1), ("mh", 7), ("ml", 7)]
    out += [("wo", 0, 0), ("wo", 0, 1), ("wo", 1, 0), ("wo", 1, 1), ("fT", 0, 0), ("fT", 0, 1),
            ("wo", 2, 0), ("wo", 2, 1), ("lg", 0, 0), ("lg", 0, 1), ("fT", 1, 0), ("fT", 1, 1), ("wo", 3, 0),
            ("fT", 2, 0), ("fT", 2, 1), ("lg", 1, 0), ("lg", 1, 1), ("fT", 3, 0), ("lg", 2, 0), ("lg", 2, 1),
            ("lg", 3, 0), ("wo", 3, 1), ("fT", 3, 1), ("lg", 3, 1), ("rank",), ("table",)]
    return out


STEPS = steps()


def banks():
    acc, uses, where = 0, [0] * 8, {}
    for s in STEPS + [("more",)]:
        kind = s[0]
        if kind in ("gate", "mh", "ml", "ws"):
            continue
        if kind == "begin":
            s = ("wo", *s[1:])
        if kind == "S":
            b = 2 + s[2] % 2
        elif kind == "PT":
            b = 4 + s[2] % 2
        elif kind == "PV":
            s = ("O", s[1])
            b = 6
        elif kind == "vT":
            b = 7
        elif kind == "normT":
            b = s[1]
        elif kind == "RS":
            b = 2 + s[2]
        elif kind == "RV":
            b = 6 + s[1] % 2
        elif kind == "RN":
            b = 4 + s[1] % 2
        elif kind == "lg":
            s, b = s[:2], 2 + s[1] % 2
        elif kind == "fT":
            b = 4 + (2 * s[1] + s[2]) % 4
        elif kind == "rank":
            b = 5
        elif kind == "table":
            b = 4
        elif kind == "more":
            b = 6
        elif s not in where:
            b = acc % 2
            acc += 1
        if s not in where:
            where[s] = (b, uses[b])
            uses[b] += 1
    return where, uses


WHERE, USES = banks()


def trunk_kernel(nc, x, norm_mix_w, w_in, fox_forget_b, w_out, norm_ffn_w, w_router_group, b_router_group,
                 w_router_expert, b_router_expert, w_expert_gate, w_expert_up, w_expert_down, norm_final_w,
                 const, rope, decay, out):
    with ExitStack() as ctx:
        def sb(name, shape, dt=F32):
            return ctx.enter_context(nc.sbuf_tensor(name, shape, dt))

        def sem(name):
            return ctx.enter_context(nc.semaphore(name))

        rows_dram = nc.dram_tensor("rows", [2 * T, 512], F32, kind="Internal").ap()
        pair_dram = nc.dram_tensor("pairs", [2 * TOPK * T, 512], F32, kind="Internal").ap()

        area = sb("area", [P, AREA])
        area_base = nc.sbuf_base - 4 * AREA
        xres = sb("xres", [P, NT, D])
        kst = sb("kst", [P, NCONST])
        rtw = sb("rtw", [P, DEPTH, KC, NG + NE])
        rtb = sb("rtb", [P, DEPTH, NG + NE])
        nmw = sb("nmw", [P, DEPTH, KC])
        nfw = sb("nfw", [P, DEPTH, KC])
        fgb = sb("fgb", [FH, DEPTH])
        stat = sb("stat", [P, 32])
        sums = sb("sums", [P, 2, P], F32R)
        rowsum = sb("rowsum", [P, 16])
        gath = sb("gath", [P, NCOL], I32)
        scat = sb("scat", [P, NCOL], I32)
        gcur = sb("gcur", [P, 4], I32)
        scur = sb("scur", [P, 4], I32)
        ovn = sb("ovn", [1, 1], I32)
        ove = sb("ove", [1, NOV], I32)

        def k(name):
            return kst[:, CONST[name][0]:CONST[name][1]]

        def at(start, n, parts=P):
            return area[0:parts, start:start + n]


        def split(name, start, shape):
            return nc.alloc_sbuf_tensor_at(name, [P, *shape], F32R, offset=area_base + 4 * start)

        h_hi = split("h_hi", HT0, [KC, T])
        h_lo = split("h_lo", HT0 + KC * T, [KC, T])
        w_hi = [split(f"w_hi{i}", WS0 + 2 * i * SLAB, [KC, P]) for i in range(CUT)]
        w_lo = [split(f"w_lo{i}", WS0 + (2 * i + 1) * SLAB, [KC, P]) for i in range(CUT)]
        qT = at(QT0, FH * T).rearrange("p (h t) -> p h t", h=FH)
        kT = at(KT0, FH * T).rearrange("p (h t) -> p h t", h=FH)
        fv = at(FV0, NT * 512).rearrange("p (t n) -> p t n", t=NT)
        rq = at(RQ0, RH * T).rearrange("p (h t) -> p h t", h=RH)
        rk = at(RK0, RH * T).rearrange("p (h t) -> p h t", h=RH)
        rv = at(RV0, NT * 512).rearrange("p (t n) -> p t n", t=NT)
        rg = at(RG0, RH * T).rearrange("p (h t) -> p h t", h=RH)
        dk = at(DK0, RH * T).rearrange("p (h t) -> p h t", h=RH)
        slab = [at(WR0 + i * SLAB, SLAB).rearrange("p (c n) -> p c n", c=KC) for i in range(RAW)]
        mix_hi, mix_lo = split("mix_hi", KT0, [KC, T]), split("mix_lo", MX0, [KC, T])
        wo_hi = [split("wo_hi0", QT0, [KC, 512]), split("wo_hi1", HT0, [KC, 512])]
        wo_lo = [split(f"wo_lo{i}", WO0 + i * KC * 512, [KC, 512]) for i in range(2)]
        wo = [at(WO0 + i * KC * 512, KC * 512).rearrange("p (c n) -> p c n", c=KC) for i in range(2)]
        mixed = at(MX0, KC * T).rearrange("p (c t) -> p c t", c=KC)
        xn_mix = at(MX0, NT * D).rearrange("p (t n) -> p t n", t=NT)
        prob = [at(PB0 + i * PLEN, PLEN) for i in range(2)]
        probT = [at(PT0, PLEN), at(DK0 + T, PLEN)]
        tmp = [at(TA0 + i * T, T) for i in range(2)]
        cos, sin = at(CS0, T), at(CS0 + T, T)
        hT2 = [at(PB0 + i * D, D).rearrange("p (c t) -> p c t", c=KC) for i in range(2)]
        xn2 = [at(XN0 + i * D, D) for i in range(2)]
        wexp = [(at(s * EXPERT, 2 * KC * DE).rearrange("p (g c n) -> p g c n", g=2, c=KC),
                 at(s * EXPERT + 2 * KC * DE, (DE // P) * D).rearrange("p (c n) -> p c n", n=D))
                for s in range(RING)]
        xg = [at(XG0 + i * 512, 512) for i in range(3)]
        xT = at(XT0, 512).rearrange("p (j h s) -> p j h s", j=4, h=2)
        sg, hh = at(SG0, 256), at(HH0, 256)
        hx = at(HX0, 256).rearrange("p (j h s) -> p j h s", j=2, h=2)
        yy = [at(YY0 + i * 512, 512) for i in range(3)]
        wbig = at(WB0, 512).rearrange("p (j h s) -> p j h s", j=4, h=2)
        yc = [at(YC0 + i * 2 * D, 2 * D) for i in range(NT)]
        negc = at(TA0, T, FH)

        free = [MX0]

        def rt(*shape):
            n = int(np.prod(shape))
            v = at(free[0], n)
            free[0] += n
            if len(shape) == 1:
                return v
            names = "abcd"[:len(shape)]
            return v.rearrange(f"p ({' '.join(names)}) -> p {' '.join(names)}",
                               **{c: s for c, s in zip(names, shape)})

        def rt_one_pass(name, *shape):
            start = -(-free[0] // 8) * 8
            free[0] = start + int(np.prod(shape))
            return split(name, start, list(shape))

        lgt = rt(NT, NG + NE)
        gs, gf, og = rt(NT, NG), rt(NT, NG), rt(NT, NG)
        em = rt(NT, NG, EPG)
        ein, ef, o1, o2 = rt(NT, EPG), rt(NT, EPG), rt(NT, EPG), rt(NT, EPG)
        a12 = rt(TOPK, NT, NG, EPG)
        a1, a2 = a12[:, 0, :, :, :], a12[:, 1, :, :, :]
        chosen = rt_one_pass("chosen", NT + 1, NE)
        gmax, gsum, m1, m2, i1, ed, wden = (rt(NT) for _ in range(7))
        wk = rt(TOPK, NT)
        cnt = rt(NE)
        ovc, cum, ovb = rt(NE), rt(NE), rt(NE)
        cmp_ov = rt(NE, MAXBLK - 1)
        cmp_blk = rt(NOV, NE)
        rsel = rt(TOPK, NT, NE)
        pick = rt(2, TOPK, NT)
        cmp_st = rt(TOPK * NT, MAXBLK - 1)
        blkno, rmod, colno, morethan = (rt(TOPK * NT) for _ in range(4))
        ovef = rt(NOV)
        cmp_col = rt(TOPK * NT, NMORE)
        hot_slot = rt_one_pass("hot_slot", TOPK * NT, P)
        hot_exp = rt_one_pass("hot_exp", TOPK * NT, NE)
        hot_more = rt_one_pass("hot_more", TOPK * NT, NMORE)
        assert free[0] <= PB0

        bank = [ctx.enter_context(nc.psum_tensor(f"bank{i}", [P, 512], F32)) for i in range(8)]

        full = [sem(f"bank{i}_full") for i in range(8)]
        freed = [sem(f"bank{i}_free") for i in range(8)]
        s_const, s_small = sem("const_loaded"), sem("small_loaded")
        s_x = [sem(f"x{t}_loaded") for t in range(NT)]
        s_slab = [sem(f"slab{i}_loaded") for i in range(RAW)]
        s_whi, s_wlo = sem("slab_hi_ready"), sem("slab_lo_ready")
        s_hhi = sem("input_hi_ready")
        s_wo = [sem(f"w_out{i}_loaded") for i in range(2)]
        s_woh, s_wol = sem("w_out_hi_ready"), sem("w_out_lo_ready")
        s_mh, s_ml = sem("mixed_hi_ready"), sem("mixed_lo_ready")
        s_decay = sem("decay_loaded")
        s_fz = sem("forget_gate_abs_ready")
        s_fl = sem("forget_gate_ln_ready")
        s_ffc = sem("forget_sums_ready")
        s_kaug = sem("forget_sums_in_keys")
        s_ones = sem("query_ones_set")
        s_xready = sem("x_ready")
        s_rstd = sem("rstd_ready")
        s_xn = sem("xn_ready")
        s_max = sem("row_max_ready")
        s_exp = sem("exp_done")
        s_prob = sem("prob_ready")
        s_swap = sem("rope_swapped")
        s_rot = sem("rope_done")
        s_gabs = sem("gate_abs_ready")
        s_gln = sem("gate_ln_ready")
        s_glog = sem("gate_log_sigmoid_ready")
        s_gexp = sem("gate_sigmoid_ready")
        s_gate = sem("gate_done")
        s_sq = sem("retention_square_ready")
        s_rln = sem("retention_rstd_ready")
        s_ret = sem("retention_done")
        s_xmid = sem("x_after_mixer")
        s_rstd2 = sem("ffn_rstd_ready")
        s_xn2 = sem("ffn_xn_ready")
        s_rows = [sem(f"rows{i}_saved") for i in range(2)]
        s_rtw = sem("router_weights_scaled")
        s_sums = sem("sums_rounded")
        s_rin = sem("router_exp_asked")
        s_rexp = sem("router_exp_done")
        s_hot = sem("choices_ready")
        s_tabin = sem("one_hots_of_experts_ready")
        s_hots = sem("one_hots_of_slots_ready")
        s_tab = sem("tables_ready")
        s_morein = sem("more_one_hots_ready")
        s_more = sem("further_tables_ready")
        s_w = [[sem(f"slot{s}_{n}_loaded") for n in ("gate_up_a", "gate_up_b", "down")] for s in range(RING)]
        s_idx, s_sidx = sem("gather_rows_ready"), sem("scatter_rows_ready")
        s_gat = [sem(f"rows_gathered{i}") for i in range(3)]
        s_xtf, s_xt = sem("block_transposed"), sem("block_input_ready")
        s_gh = sem("gate_up_half_done")
        s_gu, s_sg, s_h = sem("gate_up_done"), sem("silu_done"), sem("hidden_ready")
        s_hxf, s_hx = sem("hidden_transposed"), sem("hidden_t_ready")
        s_yf, s_y = sem("down_done"), sem("block_output_ready")
        s_sc = [sem(f"rows_scattered{i}") for i in range(3)]
        s_moe = sem("all_blocks_scattered")
        s_yc = [sem(f"pairs{i}_loaded") for i in range(NT)]
        s_passed = sem("gpsimd_waits_passed")
        s_act = sem("scalar_chain")
        s_dve = sem("vector_chain")
        s_fw = sem("final_weight_loaded")
        s_fin = sem("final_rows_ready")
        s_out = sem("out_stored")
        ov = [{n: sem(f"further{l}_{n}") for n in (
            "idx", "gathered", "weights", "xt_full", "xt", "gate_up", "silu", "hidden", "hx_full", "hx",
            "down", "out", "scattered")} for l in range(DEPTH)]

        def result(name, layer):
            b, n = WHERE[name]
            return b, layer * USES[b] + n + 1

        def is_full(eng, name, layer):
            b, n = result(name, layer)
            eng.wait_ge(full[b], n)

        def is_taken(eng, name, layer):
            b, n = result(name, layer)
            eng.wait_ge(freed[b], 2 * n)

        def may_fill(eng, name, layer):
            b, n = result(name, layer)
            if not isinstance(n, int) or n > 1:
                eng.wait_ge(freed[b], 2 * (n - 1))

        block = ctx.enter_context(nc.Block())

        @block.sync
        def _(sp):
            for t in range(NT):
                sp.dma_start(xres[:, t, :], x[0, t * P:(t + 1) * P, :]).then_inc(s_x[t], 16)
                if t == 0:
                    sp.dma_start(kst[:, :], const).then_inc(s_const, 16)

            def load_slab(layer, n):
                g = layer * NU + n
                if g >= RAW:
                    sp.wait_ge(s_wlo, g - RAW + 1)
                c = COLUMN[UNITS[n]]
                sp.dma_start(slab[g % RAW], w_in[layer, :, c:c + P].rearrange("(c p) n -> p c n", p=P)
                             ).then_inc(s_slab[g % RAW], 16)

            def load_rows(layer, e, slot, half, i):
                c0, c1 = KC // 2 * half, KC // 2 * (half + 1)
                weight = (w_expert_gate, w_expert_up)[i]
                sp.dma_start(wexp[slot][0][:, i, c0:c1, :], weight[layer, bass.ds(e, 1), P * c0:P * c1, :]
                             .rearrange("a (c p) n -> p (a c) n", p=P)).then_inc(s_w[slot][half], 16)

            def load_gate_up(layer, e, slot):
                for half in range(2):
                    for i in range(2):
                        load_rows(layer, e, slot, half, i)

            def load_down(layer, e, slot):
                sp.dma_start(wexp[slot][1], w_expert_down[layer, bass.ds(e, 1), :, :]
                             .rearrange("a (c p) n -> p (a c) n", p=P)).then_inc(s_w[slot][2], 16)

            for layer in range(DEPTH):
                if layer == 0:
                    for n in range(RAW):
                        load_slab(layer, n)
                    for l in range(DEPTH):
                        sp.dma_start(nmw[:, l, :], norm_mix_w[l].rearrange("(c p) -> p c", p=P),
                                     allow_slow_non_contiguous=True).then_inc(s_small, 16)
                        sp.dma_start(nfw[:, l, :], norm_ffn_w[l].rearrange("(c p) -> p c", p=P),
                                     allow_slow_non_contiguous=True).then_inc(s_small, 16)
                        sp.dma_start(fgb[:, l:l + 1], fox_forget_b[l].rearrange("(h a) -> h a", a=1)).then_inc(s_small, 16)
                    for l in range(DEPTH):
                        sp.dma_start(rtw[:, l, :, 0:NG], w_router_group[l].rearrange("(c p) n -> p c n", p=P)
                                     ).then_inc(s_small, 16)
                        sp.dma_start(rtw[:, l, :, NG:], w_router_expert[l].rearrange("(c p) n -> p c n", p=P)
                                     ).then_inc(s_small, 16)
                        sp.dma_start(rtb[:, l, 0:NG], b_router_group[l:l + 1, :].broadcast_to([P, NG])
                                     ).then_inc(s_small, 16)
                        sp.dma_start(rtb[:, l, NG:], b_router_expert[l:l + 1, :].broadcast_to([P, NE])
                                     ).then_inc(s_small, 16)
                    sp.dma_start(at(CS0, 2 * T), rope).then_inc(s_decay, 16)
                if layer > 0:
                    sp.wait_ge(s_yf, layer * NE)
                sp.dma_start(at(DK0, T), decay[:, 0:T]).then_inc(s_decay, 16)
                for n in range(RAW, RAW + CUT):
                    load_slab(layer, n)
                sp.wait_ge(s_ffc, layer + 1)
                sp.dma_start(kT[FD:FD + 1, :, :], negc).then_inc(s_kaug, 16)
                for n in range(RAW + CUT, NU):
                    load_slab(layer, n)

                def load_w_out(i):
                    sp.dma_start(wo[i], w_out[layer, :, 512 * i:512 * (i + 1)].rearrange("(c p) n -> p c n", p=P)
                                 ).then_inc(s_wo[i], 16)

                is_full(sp, UNITS[-1], layer)
                load_w_out(0)
                is_full(sp, ("O", FH // 2 - 1), layer)
                sp.dma_start(at(DK0 + T, (RH - 1) * T), decay[:, T:]).then_inc(s_decay, 16)
                load_w_out(1)
                for half in range(2):
                    load_rows(layer, 0, 0, half, 1)
                sp.wait_ge(s_ret, RH * (layer + 1))
                load_gate_up(layer, 1, 1)
                load_down(layer, 1, 1)
                if layer == DEPTH - 1:
                    sp.dma_start(at(CS0, D), norm_final_w.rearrange("(a n) -> a n", a=1).broadcast_to([P, D])
                                 ).then_inc(s_fw, 16)
                is_full(sp, ("wo", 3, 0), layer)
                load_down(layer, 2, 2)
                for half in range(2):
                    load_rows(layer, 2, 2, half, 0)
                is_full(sp, ("wo", 3, 1), layer)
                for i in range(2):
                    sp.wait_ge(s_rows[i], 16 * (NT // 2) * (layer + 1))
                for half in range(2):
                    load_rows(layer, 0, 0, half, 0)
                sp.wait_ge(s_idx, layer * NE + 2)
                load_down(layer, 0, 0)
                for half in range(2):
                    load_rows(layer, 2, 2, half, 1)

                def load_expert(e, slot):
                    for half, used in enumerate((s_gh, s_gu)):
                        sp.wait_ge(used, e + (layer * NE - RING + 1))
                        for i in range(2):
                            load_rows(layer, e, slot, half, i)
                    sp.wait_ge(s_yf, e + (layer * NE - RING + 1))
                    load_down(layer, e, slot)

                with sp.Fori(RING, NE - NE % RING, RING) as e0:
                    for i in range(RING):
                        load_expert(e0 + i, i)
                for e in range(NE - NE % RING, NE):
                    load_expert(e, e % RING)

                sp.wait_ge(s_more, layer + 1)
                n_more = sp.value_load(ovn[0:1, 0:1], min_val=0, max_val=NOV)
                sp.wait_ge(s_yf, (layer + 1) * NE - 1)
                o = ov[layer]
                with sp.If(n_more > 0):
                    with sp.Fori(0, NOV) as j:
                        with sp.If(n_more > j):
                            ex = sp.value_load(ove[0:1, bass.ds(j, 1)], min_val=0, max_val=NE - 1)
                            sp.wait_ge(o["idx"], j + 1)
                            sp.dma_start(wexp[0][0][:, 0, :, :], w_expert_gate[layer, bass.ds(ex, 1), :, :]
                                         .rearrange("a (c p) n -> p (a c) n", p=P)).then_inc(o["weights"], 16)
                            sp.dma_start(wexp[0][0][:, 1, :, :], w_expert_up[layer, bass.ds(ex, 1), :, :]
                                         .rearrange("a (c p) n -> p (a c) n", p=P)).then_inc(o["weights"], 16)
                            sp.dma_start(wexp[0][1], w_expert_down[layer, bass.ds(ex, 1), :, :]
                                         .rearrange("a (c p) n -> p (a c) n", p=P)).then_inc(o["weights"], 16)
                if layer + 1 < DEPTH:
                    for n in range(RAW):
                        load_slab(layer + 1, n)
                sp.wait_ge(s_moe, layer + 1)
                for t in range(NT):
                    src = pair_dram.rearrange("(a r) n -> r a n", a=2 * TOPK)[t * P:(t + 1) * P, :, :]
                    sp.dma_start(yc[t].rearrange("p (a n) -> p a n", a=2 * TOPK), src).then_inc(s_yc[t], 16)

            for t in range(NT):
                sp.wait_ge(s_fin, t + 1)
                sp.dma_start(out[0, t * P:(t + 1) * P, :], at(FN0 + t * D, D)).then_inc(s_out, 16)
            sp.wait_ge(s_out, 16 * NT)

        @block.gpsimd
        def _(pool):
            for layer in range(DEPTH):
                for n in range(NU):
                    g = layer * NU + n
                    pool.wait_ge(s_whi, g + 1)
                    nc.gpsimd.tensor_tensor(w_lo[g % CUT][:, :, :], slab[g % RAW], w_hi[g % CUT][:, :, :].bitcast(F32),
                                            ALU.subtract).then_inc(s_wlo, 1)
                    if n == 2:
                        pool.wait_ge(s_wlo, g + 1)
                        nc.gpsimd.memset(qT[FD:FD + 1, :, :], 1.0).then_inc(s_ones, 1)
                        pool.wait_ge(s_ones, layer + 1)
                for q in range(KC):
                    half, c = q // 4, 2 * (q % 4)
                    pool.wait_ge(s_woh, layer * KC + q + 1)
                    nc.gpsimd.tensor_tensor(wo_lo[half][:, c:c + 2, :], wo[half][:, c:c + 2, :],
                                            wo_hi[half][:, c:c + 2, :].bitcast(F32), ALU.subtract).then_inc(s_wol, 1)
                for t in range(NT):
                    pool.wait_ge(s_xn2, layer * NT + t + 1)
                    dst = rows_dram.rearrange("(h r) n -> r h n", h=2)[t * P:(t + 1) * P, :, :]
                    pool.dma_start(dst, xn2[t % 2].rearrange("p (h n) -> p h n", h=2)).then_inc(s_rows[t % 2], 16)
                pool.wait_ge(s_tab, layer + 1)
                for i in range(2):
                    pool.wait_ge(s_rows[i], 16 * (NT // 2) * (layer + 1))

                def gather(e, i):
                    nc.gpsimd.tensor_copy(gcur[:, i:i + 1], gath[:, bass.ds(e, 1)]).then_inc(s_idx, 1)
                    pool.wait_ge(s_idx, e + (layer * NE + 1))
                    pool.sem_inc(s_passed, 1)
                    pool.indirect_dma_start(out=xg[i], out_offset=None, in_=rows_dram,
                                            in_offset=bass.IndirectOffsetOnAxis(ap=gcur[:, i:i + 1], axis=0),
                                            bounds_check=2 * T - 1, oob_is_err=False).then_inc(s_gat[i], 16)

                def step(e, i, gather_more, scattered):
                    if gather_more:
                        pool.wait_ge(s_xtf, e + (layer * NE + 1))
                        gather(e + RING, i)
                    if scattered is not None:
                        pool.wait_ge(s_sc[i], scattered)
                    nc.gpsimd.tensor_copy(scur[:, i:i + 1], scat[:, bass.ds(e, 1)]).then_inc(s_sidx, 1)
                    pool.wait_ge(s_sidx, e + (layer * NE + 1))
                    pool.wait_ge(s_y, e + (layer * NE + 1))
                    pool.sem_inc(s_passed, 1)
                    pool.indirect_dma_start(out=pair_dram,
                                            out_offset=bass.IndirectOffsetOnAxis(ap=scur[:, i:i + 1], axis=0),
                                            in_=yy[i], in_offset=None, bounds_check=EMPTY - 1,
                                            oob_is_err=False).then_inc(s_sc[i], 16)

                def per(i):
                    return len(range(i, NE, RING))

                for e in range(RING):
                    gather(e, e)
                for e in range(RING):
                    step(e, e, True, None)
                with pool.Fori(1, (NE - RING) // RING) as q:
                    for i in range(RING):
                        step(q * RING + i, i, True, (q + layer * per(i)) * 16)
                for e in range(RING * ((NE - RING) // RING), NE):
                    step(e, e % RING, e + RING < NE, 16 * (layer * per(e % RING) + e // RING))

                o = ov[layer]
                pool.wait_ge(s_more, layer + 1)
                n_more = pool.value_load(ovn[0:1, 0:1], min_val=0, max_val=NOV)
                pool.wait_ge(s_sc[0], 16 * (layer + 1) * per(0))
                with pool.If(n_more > 0):
                    with pool.Fori(0, NOV) as j:
                        with pool.If(n_more > j):
                            nc.gpsimd.tensor_copy(gcur[:, 3:4], gath[:, bass.ds(j + NE, 1)])
                            nc.gpsimd.tensor_copy(scur[:, 3:4], scat[:, bass.ds(j + NE, 1)]).then_inc(o["idx"], 1)
                            pool.wait_ge(o["idx"], j + 1)
                            pool.sem_inc(s_passed, 1)
                            pool.indirect_dma_start(out=xg[0], out_offset=None, in_=rows_dram,
                                                    in_offset=bass.IndirectOffsetOnAxis(ap=gcur[:, 3:4], axis=0),
                                                    bounds_check=2 * T - 1, oob_is_err=False).then_inc(o["gathered"], 16)
                            pool.wait_ge(o["out"], j + 1)
                            pool.sem_inc(s_passed, 1)
                            pool.indirect_dma_start(out=pair_dram,
                                                    out_offset=bass.IndirectOffsetOnAxis(ap=scur[:, 3:4], axis=0),
                                                    in_=yy[0], in_offset=None, bounds_check=EMPTY - 1,
                                                    oob_is_err=False).then_inc(o["scattered"], 16)
                            pool.wait_ge(o["scattered"], (j + 1) * 16)
                            pool.sem_inc(s_passed, 1)
                for i in range(RING):
                    pool.wait_ge(s_sc[i], 16 * (layer + 1) * per(i))
                pool.sem_inc(s_moe, 1)

        @block.scalar
        def _(act):
            chain = [0]

            def link(ins):
                chain[0] += 1
                ins.then_inc(s_act, 1)
                act.wait_ge(s_act, chain[0])

            def rstd(src, t, junk, sig):
                link(nc.scalar.activation(junk, src, ACT.Square, accum_out=stat[:, t:t + 1]))
                link(nc.scalar.activation(stat[:, 8 + t:9 + t], stat[:, t:t + 1], ACT.Ln, bias=k("eps"),
                                          scale=1.0 / D))
                nc.scalar.activation(stat[:, 16 + t:17 + t], stat[:, 8 + t:9 + t], ACT.Exp, scale=-0.5
                                     ).then_inc(sig, 1)

            act.wait_ge(s_const, 16)
            for layer in range(DEPTH):
                act.preload_act_table_set("natural_log_exp_and_others")

                def split_slab(n):
                    g = layer * NU + n
                    act.wait_ge(s_slab[g % RAW], 16 * (g // RAW + 1))
                    nc.scalar.activation(w_hi[g % CUT][:, :, :], slab[g % RAW], ACT.Copy).then_inc(s_whi, 1)

                if layer > 0:
                    for n in range(RAW):
                        split_slab(n)
                for t in range(NT):
                    if layer == 0:
                        act.wait_ge(s_x[t], 16)
                    else:
                        act.wait_ge(s_xready, layer * NT + t + 1)
                    rstd(xres[:, t, :], t, at(PB0, D), s_rstd)
                if layer == 0:
                    for n in range(RAW):
                        split_slab(n)
                    for i, name in enumerate(("lower", "ones")):
                        nc.scalar.activation(sums[:, i, :], k(name), ACT.Copy).then_inc(s_sums, 1)
                    act.wait_ge(s_small, 16 * 7 * DEPTH)
                rot = layer * 2 * RH
                srow = layer * FH * NT
                for s in STEPS:
                    kind = s[0]
                    if kind == "normT":
                        c = s[1]
                        b, n = result(s, layer)
                        is_full(act, s, layer)
                        nc.scalar.activation(h_hi[:, c, :], bank[b][:, :], ACT.Copy,
                                             scale=nmw[:, layer, c:c + 1]).then_inc(s_hhi, 1)
                    elif kind == "ff":
                        for n in range(RAW, CUT):
                            split_slab(n)
                        act.wait_ge(s_fz, layer + 1)
                        link(nc.scalar.activation(at(TA0 + T, T, FH), at(PB0 + T, T, FH), ACT.Exp, scale=-1.0))
                        nc.scalar.activation(at(PB0 + 2 * T, T, FH), at(TA0 + T, T, FH), ACT.Ln,
                                             bias=k("one")[0:FH, :]).then_inc(s_fl, 1)
                    elif kind == "fq":
                        b, n = result(s, layer)
                        is_full(act, s, layer)
                        for i in range(2):
                            nc.scalar.activation(qT[0:FD, 2 * s[1] + i, :], bank[b][i * FD:(i + 1) * FD, :], ACT.Copy,
                                                 scale=FD ** -0.5).then_inc(freed[b], 1)
                    elif kind in ("fv", "rv"):
                        b, n = result(s, layer)
                        is_full(act, s, layer)
                        if kind == "fv":
                            act.wait_ge(s_kaug, 16 * (layer + 1))
                        else:
                            act.wait_ge(s_rot, rot)
                        nc.scalar.activation(tmp[s[1] % 2], bank[b][:, :], ACT.Copy).then_inc(freed[b], 2)
                    elif kind == "vT":
                        b, n = result(s, layer)
                        is_full(act, s, layer)
                        dst = fv if s[1] == "fv" else rv
                        nc.scalar.activation(dst[:, :, P * s[2]:P * (s[2] + 1)],
                                             bank[b][:, :].rearrange("p (t c) -> p t c", t=NT), ACT.Copy
                                             ).then_inc(freed[b], 2)
                    elif kind in ("rq", "rk"):
                        b, n = result(s, layer)
                        is_full(act, s, layer)
                        if rot >= 2:
                            act.wait_ge(s_rot, rot - 1)
                        half = RD // 2
                        nc.scalar.activation(tmp[rot % 2][0:half, :], bank[b][half:RD, :], ACT.Copy
                                             ).then_inc(s_swap, 1)
                        nc.scalar.activation(tmp[rot % 2][half:RD, :], bank[b][0:half, :], ACT.Copy
                                             ).then_inc(s_swap, 1)
                        rot += 1
                    elif kind == "rg":
                        b, n = result(s, layer)
                        is_full(act, s, layer)
                        nc.scalar.activation(rg[:, s[1], :], bank[b][:, :], ACT.Copy).then_inc(freed[b], 2)
                    elif kind == "gate" and s[2] == 0:
                        buf = tmp[s[1] % 2]
                        act.wait_ge(s_gabs, layer * RH + s[1] + 1)
                        link(nc.scalar.activation(buf, buf, ACT.Exp))
                        nc.scalar.activation(buf, buf, ACT.Ln, bias=k("one")).then_inc(s_gln, 1)
                    elif kind == "gate" and s[2] == 1:
                        buf = tmp[s[1] % 2]
                        act.wait_ge(s_glog, layer * RH + s[1] + 1)
                        nc.scalar.activation(buf, buf, ACT.Exp).then_inc(s_gexp, 1)
                    elif kind == "S":
                        h, qb = s[1], s[2]
                        srow += 1
                        b, n = result(s, layer)
                        act.wait_ge(s_max, srow)
                        if srow > 2:
                            act.wait_ge(s_prob, srow - 2)
                        nc.scalar.activation(prob[h % 2][:, pblk(qb):pblk(qb) + P * (qb + 1)],
                                             bank[b][:, 0:P * (qb + 1)], ACT.Exp,
                                             bias=rowsum[:, srow % 2:srow % 2 + 1],
                                             accum_out=rowsum[:, 2 + srow % 2:3 + srow % 2]).then_inc(s_exp, 1)
                    elif kind == "PT":
                        h, j = s[1], s[2]
                        b, n = result(s, layer)
                        is_full(act, s, layer)
                        nc.scalar.activation(probT[h % 2][:, tblk(j):tblk(j) + T - P * j], bank[b][:, P * j:T], ACT.Copy
                                             ).then_inc(freed[b], 2)
                    elif kind == "PV" and s[2] == NT - 1:
                        m = s[1]
                        b, n = result(("O", m), layer)
                        is_full(act, ("O", m), layer)
                        nc.scalar.activation(mixed[:, m, :], bank[b][:, :], ACT.Copy).then_inc(freed[b], 2)
                    elif kind == "ws":
                        half, c = s[1] // 4, 2 * (s[1] % 4)
                        act.wait_ge(s_wo[half], 16 * (layer + 1))
                        nc.scalar.activation(wo_hi[half][:, c:c + 2, :], wo[half][:, c:c + 2, :], ACT.Copy
                                             ).then_inc(s_woh, 1)
                    elif kind == "mh":
                        m = s[1]
                        if m < FH // 2:
                            is_taken(act, ("O", m), layer)
                        else:
                            act.wait_ge(s_ret, RH * layer + m - FH // 2 + 1)
                        nc.scalar.activation(mix_hi[:, m, :], mixed[:, m, :], ACT.Copy).then_inc(s_mh, 1)
                    elif kind == "RV":
                        r = s[1]
                        b, n = result(s, layer)
                        is_full(act, s, layer)
                        if r < 2:
                            act.wait_ge(s_gate, RH * (layer + 1))
                        else:
                            act.wait_ge(s_ret, layer * RH + r - 1)
                        nc.scalar.activation(tmp[r % 2], bank[b][:, :], ACT.Square).then_inc(s_sq, 1)
                        nc.scalar.activation(probT[0][:, T * (r % 2):T * (r % 2 + 1)], bank[b][:, :], ACT.Copy
                                             ).then_inc(freed[b], 2)
                    elif kind == "RN":
                        r = s[1]
                        b, n = result(s, layer)
                        is_full(act, s, layer)
                        m = mixed[:, RH + r, :]
                        link(nc.scalar.activation(m, bank[b][:, :], ACT.Ln, bias=k("eps"), scale=1.0 / RD))
                        nc.scalar.activation(m, m, ACT.Exp, scale=-0.5).then_inc(s_rln, 1)
                    elif kind == "wo" and s[2] == 1:
                        t = s[1]
                        act.wait_ge(s_xmid, layer * NT + t + 1)
                        if t >= 2:
                            act.wait_ge(s_rows[t % 2], 16 * (layer * (NT // 2) + t // 2))
                        rstd(xres[:, t, :], t, xn2[t % 2], s_rstd2)
                    if s in UNITS and UNITS.index(s) + CUT < NU:
                        is_full(act, s, layer)
                        split_slab(UNITS.index(s) + CUT)

                act.wait_ge(s_rin, 2 * layer + 1)
                nc.scalar.activation(ed, ed, ACT.Exp).then_inc(s_rexp, 1)
                act.wait_ge(s_rin, 2 * layer + 2)
                nc.scalar.activation(gs, gs, ACT.Exp).then_inc(s_rexp, 1)
                act.preload_act_table_set("silu_and_others")

                act.wait_ge(s_tab, layer + 1)

                def expert(e, i, scattered):
                    act.wait_ge(s_gu, e + (layer * NE + 1))
                    nc.scalar.activation(sg, bank[1][:, 0:256], ACT.Silu).then_inc(s_sg, 1)
                    act.wait_ge(s_yf, e + (layer * NE + 1))
                    if scattered is not None:
                        act.wait_ge(s_sc[i], scattered)
                    nc.scalar.activation(yy[i], bank[3][:, :], ACT.Copy).then_inc(s_y, 1)

                def per(i):
                    return len(range(i, NE, RING))

                for e in range(RING):
                    expert(e, e, None)
                with act.Fori(1, NE // RING) as q:
                    for i in range(RING):
                        expert(q * RING + i, i, (q + layer * per(i)) * 16)
                for e in range(RING * (NE // RING), NE):
                    expert(e, e % RING, 16 * (e // RING + layer * per(e % RING)))

                o = ov[layer]
                act.wait_ge(s_more, layer + 1)
                n_more = act.value_load(ovn[0:1, 0:1], min_val=0, max_val=NOV)
                act.wait_ge(s_sc[0], 16 * (layer + 1) * per(0))
                with act.If(n_more > 0):
                    with act.Fori(0, NOV) as j:
                        with act.If(n_more > j):
                            act.wait_ge(o["gate_up"], j + 1)
                            nc.scalar.activation(sg, bank[1][:, 0:256], ACT.Silu).then_inc(o["silu"], 1)
                            act.wait_ge(o["down"], j + 1)
                            nc.scalar.activation(yy[0], bank[3][:, :], ACT.Copy).then_inc(o["out"], 1)

            act.preload_act_table_set("natural_log_exp_and_others")
            for t in range(NT):
                act.wait_ge(s_xready, DEPTH * NT + t + 1)
                rstd(xres[:, t, :], t, at(PB0, D), s_rstd)

        @block.vector
        def _(dve):
            chain = [0]

            def link(ins):
                chain[0] += 1
                ins.then_inc(s_dve, 1)
                dve.wait_ge(s_dve, chain[0])

            tt, ts, red = nc.vector.tensor_tensor, nc.vector.tensor_scalar, nc.vector.tensor_reduce

            def ffn_rows(layer, t):
                dve.wait_ge(s_rstd2, layer * NT + t + 1)
                ts(xn2[t % 2], xres[:, t, :], stat[:, 16 + t:17 + t], None, ALU.mult).then_inc(s_xn2, 1)

            def over(v, n):
                return v.unsqueeze(1).broadcast_to([P, n, v.shape[1]])

            def each(v, n):
                return v.unsqueeze(len(v.shape)).broadcast_to([*v.shape, n])

            def first_of(scores, best, index, onehot, scratch, n):
                link(tt(scratch, scores, each(best, n), ALU.is_equal))
                link(tt(scratch, scratch, over(index, NT), ALU.mult))
                link(red(i1, scratch, AX.X, ALU.min))
                link(tt(onehot, over(index, NT), each(i1, n), ALU.is_equal))

            a12f = a12.rearrange("p k t g e -> p k t (g e)")

            def picked(i, v):
                link(tt(rsel, a12f, v, ALU.mult))
                link(red(pick[:, i, :, :], rsel, AX.X, ALU.add))
                return pick[:, i, :, :].rearrange("p k t -> p (k t)")

            def rows_of(layer, name, c0, c1):
                b, n = result(name, layer)
                is_full(dve, name, layer)
                ts(scat[:, c0:c1], bank[b][:, 0:c1 - c0], k("off"), None, ALU.add).then_inc(freed[b], 2)
                is_taken(dve, name, layer)
                return ts(gath[:, c0:c1], scat[:, c0:c1], ~(2 * T), None, ALU.bitwise_and)

            def route(layer):
                g_log = lgt[:, :, 0:NG]
                e_log = lgt[:, :, NG:].rearrange("p t (g e) -> p t g e", g=NG)
                link(red(gmax, g_log, AX.X, ALU.max))
                first_of(g_log, gmax, k("g"), og, gf, NG)
                link(tt(em, e_log, each(og, EPG), ALU.mult))
                link(red(ein, em.rearrange("p t g e -> p t e g"), AX.X, ALU.add))
                link(red(m1, ein, AX.X, ALU.max))
                first_of(ein, m1, k("o"), o1, ef, EPG)
                link(nc.vector.scalar_tensor_tensor(out=ein, in0=o1, scalar=NEG, in1=ein, op0=ALU.mult, op1=ALU.add))
                link(red(m2, ein, AX.X, ALU.max))
                first_of(ein, m2, k("o"), o2, ef, EPG)
                for a, o_ in ((a1, o1), (a2, o2)):
                    link(tt(a, each(og, EPG), o_.unsqueeze(2).broadcast_to([P, NT, NG, EPG]), ALU.mult))
                link(nc.vector.memset(chosen[:, NT, :].bitcast(F32), 0.0))
                tt(chosen[:, 0:NT, :], a12f[:, 0, :, :], a12f[:, 1, :, :], ALU.add).then_inc(s_hot, 1)
                tt(hot_exp[:, :, :], a12f.rearrange("p k t e -> p (k t) e"), each(k("row"), NE), ALU.mult
                   ).then_inc(s_tabin, 1)
                tt(ed, m2, m1, ALU.subtract).then_inc(s_rin, 1)
                tt(gs, g_log, each(gmax, NG), ALU.subtract).then_inc(s_rin, 1)
                b, n = result(("rank",), layer)
                is_full(dve, ("rank",), layer)
                rank = bank[b][:, 0:NT * NE].rearrange("p (t e) -> p t e", t=NT)
                p_rank = picked(0, rank.unsqueeze(1).broadcast_to([P, TOPK, NT, NE]))
                for c in range(TOPK):
                    own = slice(NT * c, NT * (c + 1))
                    tt(hot_slot[:, own, :], over(k("slot"), NT), each(p_rank[:, own], P), ALU.is_equal
                       ).then_inc(s_hots, 1)
                for i in range(2):
                    dve.wait_ge(s_rows[i], 16 * (NT // 2) * (layer + 1))
                link(nc.vector.tensor_copy(wbig, each(nfw[:, layer, :].rearrange("p (h j) -> p j h", h=2), SLOTS)))
                rows_of(layer, ("table",), 0, NE).then_inc(s_tab, 1)

            def final_rows(t):
                if t == 0:
                    dve.wait_ge(s_fw, 16)
                dve.wait_ge(s_rstd, DEPTH * NT + t + 1)
                nc.vector.scalar_tensor_tensor(out=at(FN0 + t * D, D), in0=xres[:, t, :], scalar=stat[:, 16 + t:17 + t],
                                               in1=at(CS0, D), op0=ALU.mult, op1=ALU.mult).then_inc(s_fin, 1)

            def weights(layer):
                dve.wait_ge(s_rexp, 2 * layer + 2)
                link(red(gsum, gs, AX.X, ALU.add))
                link(nc.vector.scalar_tensor_tensor(out=wden, in0=ed, scalar=1.0, in1=gsum, op0=ALU.add, op1=ALU.mult))
                link(nc.vector.reciprocal(wk[:, 0, :], wden))
                link(tt(wk[:, 1, :], wk[:, 0, :], ed, ALU.mult))

            def further(layer):
                b, n = result(("rank",), layer)
                nc.vector.tensor_copy(cnt, bank[b][:, NT * NE:(NT + 1) * NE]).then_inc(freed[b], 2)
                is_taken(dve, ("rank",), layer)
                link(tt(cmp_ov, each(cnt, MAXBLK - 1), over(k("over"), NE), ALU.is_ge))
                link(red(ovc, cmp_ov, AX.X, ALU.add))
                link(nc.vector.tensor_tensor_scan(cum, k("ones")[:, 0:NE], ovc, 0.0, ALU.mult, ALU.add))
                link(tt(ovb, cum, ovc, ALU.subtract))
                p_ovb = picked(1, ovb.unsqueeze(1).unsqueeze(1).broadcast_to([P, TOPK, NT, NE]))
                p_rank = pick[:, 0, :, :].rearrange("p k t -> p (k t)")
                n_, r_, c_, m_ = blkno, rmod, colno, morethan
                link(tt(cmp_st, each(p_rank, MAXBLK - 1), over(k("step"), NT * TOPK), ALU.is_ge))
                link(red(n_, cmp_st, AX.X, ALU.add))
                link(nc.vector.scalar_tensor_tensor(out=r_, in0=n_, scalar=-float(SLOTS), in1=p_rank, op0=ALU.mult,
                                                    op1=ALU.add))
                link(tt(c_, p_ovb, n_, ALU.add))
                link(ts(m_, n_, 1.0, None, ALU.is_ge))
                link(tt(c_, c_, m_, ALU.mult))
                link(tt(hot_slot[:, :, :], over(k("slot"), NT * TOPK), each(r_, P), ALU.is_equal))
                link(tt(cmp_col, over(k("blk"), NT * TOPK), each(c_, NMORE), ALU.is_equal))
                tt(hot_more[:, :, :], cmp_col, each(k("row"), NMORE), ALU.mult).then_inc(s_morein, 1)
                link(tt(cmp_blk, over(cum, NOV), each(k("blk")[:, 0:NOV], NE), ALU.is_lt))
                link(red(ovef, cmp_blk, AX.X, ALU.add))
                link(nc.vector.tensor_copy(ove[:, :], ovef[0:1, :]))
                link(nc.vector.tensor_copy(ovn[:, :], cum[0:1, NE - 1:NE]))

            dve.wait_ge(s_const, 16)
            for layer in range(DEPTH):
                for t in range(NT):
                    dve.wait_ge(s_rstd, layer * NT + t + 1)
                    ts(xn_mix[:, t, :], xres[:, t, :], stat[:, 16 + t:17 + t], None, ALU.mult).then_inc(s_xn, 1)
                if layer == 0:
                    dve.wait_ge(s_small, 16 * 7 * DEPTH)
                    for l in range(DEPTH):
                        tt(rtw[:, l, :, :], rtw[:, l, :, :], each(nfw[:, l, :], NG + NE), ALU.mult).then_inc(s_rtw, 1)
                rot = layer * 2 * RH
                srow = layer * FH * NT
                for s in STEPS:
                    kind = s[0]
                    if kind == "normT":
                        c = s[1]
                        b, n = result(s, layer)
                        dve.wait_ge(s_hhi, layer * KC + c + 1)
                        nc.vector.scalar_tensor_tensor(out=h_lo[:, c, :], in0=bank[b][:, :],
                                                       scalar=nmw[:, layer, c:c + 1], in1=h_hi[:, c, :].bitcast(F32),
                                                       op0=ALU.mult, op1=ALU.subtract).then_inc(freed[b], 2)
                    elif kind == "ff":
                        b, n = result(s, layer)
                        is_full(dve, s, layer)
                        z, az, ln = at(PB0, T, FH), at(PB0 + T, T, FH), at(PB0 + 2 * T, T, FH)
                        ts(z, bank[b][0:FH, :], fgb[:, layer:layer + 1], None, ALU.add).then_inc(freed[b], 2)
                        is_taken(dve, s, layer)
                        link(ts(at(PB0 + 3 * T, T, FH), z, -1.0, None, ALU.mult))
                        tt(az, z, at(PB0 + 3 * T, T, FH), ALU.max).then_inc(s_fz, 1)
                        link(ts(z, z, 0.0, None, ALU.min))
                        dve.wait_ge(s_fl, layer + 1)
                        link(tt(ln, ln, z, ALU.subtract))
                        dve.wait_ge(s_fz, layer + 1)
                        link(nc.vector.memset(az, 1.0))
                        nc.vector.tensor_tensor_scan(negc, az, ln, 0.0, ALU.mult, ALU.add).then_inc(s_ffc, 1)
                    elif kind == "fk":
                        b, n = result(s, layer)
                        is_full(dve, s, layer)
                        for i in range(2):
                            nc.vector.tensor_copy(kT[0:FD, 2 * s[1] + i, :], bank[b][i * FD:(i + 1) * FD, :]
                                                  ).then_inc(freed[b], 1)
                    elif kind in ("rq", "rk"):
                        b, n = result(s, layer)
                        if rot == 0:
                            dve.wait_ge(s_decay, 16 * 2)
                        dst = (rq if kind == "rq" else rk)[:, s[1], :]
                        is_full(dve, s, layer)
                        dve.wait_ge(s_swap, 2 * (rot + 1))
                        tt(dst, bank[b][:, :], cos, ALU.mult).then_inc(freed[b], 2)
                        link(tt(tmp[rot % 2], tmp[rot % 2], sin, ALU.mult))
                        is_taken(dve, s, layer)
                        tt(dst, dst, tmp[rot % 2], ALU.add).then_inc(s_rot, 1)
                        rot += 1
                    elif kind == "gate":
                        i = s[1]
                        g, buf, done = rg[:, i, :], tmp[i % 2], layer * RH + i + 1
                        stt = nc.vector.scalar_tensor_tensor
                        if s[2] == 0:
                            is_taken(dve, ("rg", i), layer)
                            stt(out=buf, in0=g, scalar=-1.0, in1=g, op0=ALU.mult, op1=ALU.min).then_inc(s_gabs, 1)
                        elif s[2] == 1:
                            dve.wait_ge(s_gln, done)
                            stt(out=buf, in0=g, scalar=0.0, in1=buf, op0=ALU.min, op1=ALU.subtract
                                ).then_inc(s_glog, 1)
                        else:
                            dve.wait_ge(s_gexp, done)
                            tt(g, g, buf, ALU.mult).then_inc(s_gate, 1)
                    elif kind == "S":
                        h, qb = s[1], s[2]
                        srow += 1
                        b, n = result(s, layer)
                        is_full(dve, s, layer)
                        diag = bank[b][:, P * qb:P * (qb + 1)]
                        link(tt(diag, diag, k("mask"), ALU.add))
                        red(rowsum[:, srow % 2:srow % 2 + 1], bank[b][:, 0:P * (qb + 1)], AX.X, ALU.max, negate=True
                            ).then_inc(s_max, 1)
                        dve.wait_ge(s_exp, srow)
                        dve.sem_inc(freed[b], 2)
                        link(nc.vector.reciprocal(rowsum[:, 4:5], rowsum[:, 2 + srow % 2:3 + srow % 2]))
                        pr = prob[h % 2][:, pblk(qb):pblk(qb) + P * (qb + 1)]
                        ts(pr, pr, rowsum[:, 4:5], None, ALU.mult).then_inc(s_prob, 1)
                    elif kind == "RS":
                        r, j = s[1], s[2]
                        b, n = result(s, layer)
                        if r == 0 and j == 0:
                            dve.wait_ge(s_decay, 16 * (2 * layer + 2))
                        if r == 1 and j == 0:
                            dve.wait_ge(s_decay, 16 * (2 * layer + 3))
                        is_full(dve, s, layer)
                        tt(prob[r % 2][:, tblk(j):tblk(j) + T - P * j], bank[b][:, P * j:T], dk[:, r, 0:T - P * j],
                           ALU.mult).then_inc(freed[b], 2)
                    elif kind == "ml":
                        m = s[1]
                        dve.wait_ge(s_mh, layer * KC + m + 1)
                        tt(mix_lo[:, m, :], mixed[:, m, :], mix_hi[:, m, :].bitcast(F32), ALU.subtract
                           ).then_inc(s_ml, 1)
                    elif kind == "RN":
                        r = s[1]
                        b, n = result(s, layer)
                        dve.wait_ge(s_rln, layer * RH + r + 1)
                        dve.sem_inc(freed[b], 2)
                        y, m = probT[0][:, T * (r % 2):T * (r % 2 + 1)], mixed[:, RH + r, :]
                        link(tt(y, y, rg[:, r, :], ALU.mult))
                        tt(m, m, y, ALU.mult).then_inc(s_ret, 1)
                    elif kind == "wo":
                        t, half = s[1], s[2]
                        if t and half:
                            ffn_rows(layer, t - 1)
                        b, n = result(s, layer)
                        is_full(dve, s, layer)
                        xs = xres[:, t, 512 * half:512 * (half + 1)]
                        tt(xs, xs, bank[b][:, :], ALU.add).then_inc(freed[b], 2)
                        if half:
                            is_taken(dve, ("wo", t, 0), layer)
                            is_taken(dve, s, layer)
                            dve.sem_inc(s_xmid, 1)
                    elif kind == "fT":
                        t, half = s[1], s[2]
                        b, n = result(s, layer)
                        is_full(dve, s, layer)
                        nc.vector.tensor_copy(hT2[t % 2][:, 4 * half:4 * (half + 1), :],
                                              bank[b][:, :].rearrange("p (c t) -> p c t", c=4)).then_inc(freed[b], 2)
                        if t == NT - 1 and half:
                            ffn_rows(layer, t)
                    elif kind == "lg" and s[2]:
                        t = s[1]
                        b, n = result(s[:2], layer)
                        is_full(dve, s[:2], layer)
                        dve.wait_ge(s_rstd2, layer * NT + t + 1)
                        nc.vector.scalar_tensor_tensor(out=lgt[:, t, :], in0=bank[b][:, 0:NG + NE],
                                                       scalar=stat[:, 16 + t:17 + t], in1=rtb[:, layer, :],
                                                       op0=ALU.mult, op1=ALU.add).then_inc(freed[b], 2)
                        if t == NT - 1:
                            is_taken(dve, s[:2], layer)

                route(layer)

                def expert(e, last):
                    dve.wait_ge(s_sg, e + (layer * NE + 1))
                    tt(hh, sg, bank[1][:, 256:512], ALU.mult).then_inc(s_h, 1)
                    if not last:
                        take_input(e + 1)
                    dve.wait_ge(s_hxf, e + (layer * NE + 1))
                    nc.vector.tensor_copy(at(HX0, 256), bank[2][:, 0:256]).then_inc(s_hx, 1)

                def take_input(e):
                    dve.wait_ge(s_xtf, e + (layer * NE + 1))
                    tt(at(XT0, 512), bank[0][:, :], at(WB0, 512), ALU.mult).then_inc(s_xt, 1)

                take_input(0)
                weights(layer)
                further(layer)
                with dve.Fori(0, NE - TAIL) as e:
                    expert(e, False)
                link(rows_of(layer, ("more",), NE, NCOL))
                dve.sem_inc(s_more, 1)
                for e in range(NE - TAIL, NE):
                    expert(e, e == NE - 1)

                o = ov[layer]
                dve.wait_ge(s_more, layer + 1)
                n_more = dve.value_load(ovn[0:1, 0:1], min_val=0, max_val=NOV)
                with dve.If(n_more > 0):
                    with dve.Fori(0, NOV) as j:
                        with dve.If(n_more > j):
                            dve.wait_ge(o["xt_full"], j + 1)
                            tt(at(XT0, 512), bank[0][:, :], at(WB0, 512), ALU.mult).then_inc(o["xt"], 1)
                            dve.wait_ge(o["silu"], j + 1)
                            tt(hh, sg, bank[1][:, 256:512], ALU.mult).then_inc(o["hidden"], 1)
                            dve.wait_ge(o["hx_full"], j + 1)
                            nc.vector.tensor_copy(at(HX0, 256), bank[2][:, 0:256]).then_inc(o["hx"], 1)

                if layer == 0:
                    dve.sem_inc(s_xready, NT)
                for t in range(NT):
                    dve.wait_ge(s_yc[t], 16 * (layer + 1))
                    for c in range(TOPK):
                        add = nc.vector.scalar_tensor_tensor(out=xres[:, t, :], in0=yc[t][:, D * c:D * (c + 1)],
                                                             scalar=wk[:, c, t:t + 1], in1=xres[:, t, :],
                                                             op0=ALU.mult, op1=ALU.add)
                        if c + 1 < TOPK:
                            link(add)
                    add.then_inc(s_xready, 1)
                    if layer == DEPTH - 1 and t:
                        final_rows(t - 1)
                    dve.wait_ge(s_xready, (layer + 1) * NT + t + 1)
            final_rows(NT - 1)

        @block.tensor
        def _(pe):
            mm, tr = nc.tensor.matmul, nc.tensor.transpose
            ident = k("ident")

            def table(o, hot_col, n, ready=None):
                for i in range(TOPK * NT):
                    if ready is not None and i % NT == 0:
                        pe.wait_ge(s_hots, ready + i // NT + 1)
                    last = mm(o[:, 0:n], hot_slot[:, i, :], hot_col[:, i, 0:n], start=(i == 0),
                              stop=(i == TOPK * NT - 1))
                return last

            pe.wait_ge(s_const, 16)
            for layer in range(DEPTH):
                srow = layer * FH * NT
                for s in STEPS:
                    kind = s[0]
                    if kind in ("gate", "mh", "ml", "ws"):
                        continue
                    if kind in ("PV", "lg"):
                        name, first = ("O" if kind == "PV" else kind, s[1]), s[2] == 0
                    elif kind == "begin":
                        name, first = ("wo", *s[1:]), True
                    else:
                        name, first = s, s[:2] != ("wo", 0)
                    b, n = result(name, layer)
                    o = bank[b]
                    if first:
                        may_fill(pe, name, layer)
                    if kind == "normT":
                        if s[1] == KC - 1:
                            for t in range(NT):
                                pe.wait_ge(s_xn, NT * layer + t + 1)
                                for c in range(KC):
                                    last = tr(bank[c][:, P * t:P * (t + 1)], xn_mix[:, t, P * c:P * (c + 1)], ident)
                                    if t == NT - 1:
                                        last.then_inc(full[c], 1)
                        continue
                    elif s in UNITS:
                        g = layer * NU + UNITS.index(s)
                        pe.wait_ge(s_wlo, g + 1)
                        hi, lo = w_hi[g % CUT], w_lo[g % CUT]
                        for c in range(KC):
                            if kind == "ff":
                                is_taken(pe, ("normT", c), layer)
                            mm(o[:, :], hi[:, c, :], h_hi[:, c, :], start=(c == 0), stop=False)
                            mm(o[:, :], hi[:, c, :], h_lo[:, c, :], start=False, stop=False)
                            last = mm(o[:, :], lo[:, c, :], h_hi[:, c, :], start=False, stop=(c == KC - 1))
                    elif kind == "vT":
                        is_taken(pe, s[1:], layer)
                        for t in range(NT):
                            last = tr(o[:, P * t:P * (t + 1)], tmp[s[2] % 2][:, P * t:P * (t + 1)], ident)
                    elif kind == "S":
                        h, qb = s[1], s[2]
                        if h == 0 and qb == 0:
                            pe.wait_ge(s_kaug, 16 * (layer + 1))
                            pe.wait_ge(s_ones, layer + 1)
                            for i in range(4):
                                is_taken(pe, ("fq", i), layer)
                                is_taken(pe, ("fk", i), layer)
                        last = mm(o[:, 0:P * (qb + 1)], qT[0:FD + 1, h, P * qb:P * (qb + 1)],
                                  kT[0:FD + 1, h, 0:P * (qb + 1)], start=True, stop=True)
                    elif kind == "PT":
                        h, j = s[1], s[2]
                        if j == 0:
                            pe.wait_ge(s_prob, layer * FH * NT + NT * (h + 1))
                        for qb in range(j, NT):
                            last = tr(o[:, P * qb:P * (qb + 1)],
                                      prob[h % 2][:, pblk(qb) + P * j:pblk(qb) + P * (j + 1)], ident)
                    elif kind == "PV":
                        m, j = s[1], s[2]
                        for i in range(2):
                            is_taken(pe, ("PT", 2 * m + i, j), layer)
                        if m == 0 and j == 0:
                            for t in range(NT):
                                is_taken(pe, ("vT", "fv", t), layer)
                        for i in range(2):
                            h = 2 * m + i
                            last = mm(o[FD * i:FD * (i + 1), P * j:T], fv[:, j, FD * h:FD * (h + 1)],
                                      probT[i][:, tblk(j):tblk(j) + T - P * j], start=(j == 0), stop=(j == NT - 1))
                    elif kind == "RS":
                        r, j = s[1], s[2]
                        pe.wait_ge(s_rot, layer * 2 * RH + RH + r + 1)
                        last = mm(o[:, P * j:T], rk[:, r, P * j:P * (j + 1)], rq[:, r, P * j:T], start=True, stop=True)
                    elif kind == "RV":
                        r = s[1]
                        for t in range(NT):
                            is_taken(pe, ("vT", "rv", t), layer)
                            is_taken(pe, ("RS", r, t), layer)
                        for j in range(NT):
                            last = mm(o[:, P * j:T], rv[:, j, RD * r:RD * (r + 1)],
                                      prob[r % 2][:, tblk(j):tblk(j) + T - P * j], start=(j == 0), stop=(j == NT - 1))
                    elif kind == "RN":
                        pe.wait_ge(s_sq, layer * RH + s[1] + 1)
                        last = mm(o[:, :], k("ones"), tmp[s[1] % 2], start=True, stop=True)
                    elif kind in ("begin", "wo"):
                        t, half = s[1], s[2]
                        split_at = KC - 3
                        for c in range(split_at if s[:2] == ("wo", 0) else 0, split_at if kind == "begin" else KC):
                            if t == 0:
                                pe.wait_ge(s_ml, layer * KC + c + 1)
                                pe.wait_ge(s_wol, layer * KC + 4 * half + c // 2 + 1)
                            m_hi, m_lo = (m[:, c, P * t:P * (t + 1)] for m in (mix_hi, mix_lo))
                            w_h, w_l = wo_hi[half][:, c, :], wo_lo[half][:, c, :]
                            mm(o[:, :], m_hi, w_h, start=(c == 0), stop=False)
                            mm(o[:, :], m_hi, w_l, start=False, stop=False)
                            last = mm(o[:, :], m_lo, w_h, start=False, stop=(c == KC - 1))
                    elif kind == "fT":
                        t, half = s[1], s[2]
                        is_taken(pe, ("wo", t, half), layer)
                        for c in range(4):
                            cc = 4 * half + c
                            last = tr(o[:, P * c:P * (c + 1)], xres[:, t, P * cc:P * (cc + 1)], ident)
                    elif kind == "lg":
                        t, half = s[1], s[2]
                        if layer == 0 and t == 0:
                            pe.wait_ge(s_rtw, DEPTH)
                        is_taken(pe, ("fT", t, half), layer)
                        for c in range(4 * half, 4 * (half + 1)):
                            last = mm(o[:, 0:NG + NE], hT2[t % 2][:, c, :], rtw[:, layer, c, :],
                                      start=(c == 0), stop=(c == KC - 1))
                    elif kind == "rank":
                        pe.wait_ge(s_hot, layer + 1)
                        if layer == 0:
                            pe.wait_ge(s_sums, 2)
                        mm(o[:, 0:NE * (NT + 1)], sums[:, 0, :], chosen[:, :, :].rearrange("p t e -> p (t e)"),
                           start=True, stop=False)
                        for u in range(1, NT + 1):
                            last = mm(o[:, NE * u:NE * (NT + 1)], sums[:, 1, :],
                                      chosen[:, 0:NT + 1 - u, :].rearrange("p t e -> p (t e)"),
                                      start=False, stop=(u == NT))
                    elif kind == "table":
                        pe.wait_ge(s_tabin, layer + 1)
                        last = table(o, hot_exp, NE, TOPK * layer)
                    if kind == "PV":
                        done = s[2] == NT - 1
                    elif kind == "lg":
                        done = s[2] == 1
                    elif kind == "begin":
                        done = False
                    else:
                        done = True
                    if done:
                        last.then_inc(full[b], 1)

                pe.wait_ge(s_tab, layer + 1)

                def input_transpose(e, i, gathered):
                    pe.wait_ge(s_gat[i], gathered)
                    for j in range(4):
                        last = tr(bank[0][:, P * j:P * (j + 1)], xg[i][:, P * j:P * (j + 1)], ident)
                    last.then_inc(s_xtf, 1)

                def gate_up(slot, before_half=None):
                    w = wexp[slot][0]
                    for c in range(KC):
                        if before_half is not None and c % (KC // 2) == 0:
                            before_half(c // (KC // 2))
                        for half in range(2):
                            last = mm(bank[1][SLOTS * half:SLOTS * (half + 1), :], xT[:, c % 4, c // 4, :],
                                      w[:, :, c, 256 * half:256 * (half + 1)], start=(c == 0), stop=(c == KC - 1))
                        if before_half is not None and c == KC // 2 - 1:
                            last.then_inc(s_gh, 1)
                    return last

                def hidden_transpose():
                    for j in range(2):
                        last = tr(bank[2][:, P * j:P * (j + 1)], hh[:, P * j:P * (j + 1)], ident)
                    return last

                def down(slot):
                    w = wexp[slot][1]
                    for c in range(4):
                        for half in range(2):
                            last = mm(bank[3][SLOTS * half:SLOTS * (half + 1), :], hx[:, c % 2, c // 2, :],
                                      w[:, c, 512 * half:512 * (half + 1)], start=(c == 0), stop=(c == 3))
                    return last

                def expert(e, i, loads, next_gathered):
                    g = e + (layer * NE + 1)
                    pe.wait_ge(s_xt, g)
                    gate_up(i, lambda half: pe.wait_ge(s_w[i][half], loads * 2)).then_inc(s_gu, 1)
                    if next_gathered is not None:
                        input_transpose(e + 1, (i + 1) % RING, next_gathered)
                    pe.wait_ge(s_h, g)
                    hidden_transpose().then_inc(s_hxf, 1)
                    pe.wait_ge(s_hx, g)
                    pe.wait_ge(s_w[i][2], loads)
                    down(i).then_inc(s_yf, 1)

                def per(i):
                    return len(range(i, NE, RING))

                input_transpose(0, 0, 16 * (layer * per(0) + 1))
                with pe.Fori(0, NE // RING) as q:
                    for i in range(RING):
                        nxt = (q + (layer * per((i + 1) % RING) + 1 + (1 if i == RING - 1 else 0))) * 16
                        expert(q * RING + i, i, (q + (layer * per(i) + 1)) * 16, nxt)
                pe.wait_ge(s_morein, layer + 1)
                may_fill(pe, ("more",), layer)
                table(bank[WHERE[("more",)][0]], hot_more, NMORE).then_inc(full[WHERE[("more",)][0]], 1)
                for e in range(RING * (NE // RING), NE):
                    i = e % RING
                    nxt = None if e == NE - 1 else 16 * (layer * per((i + 1) % RING) + (e + 1) // RING + 1)
                    expert(e, i, 16 * (layer * per(i) + e // RING + 1), nxt)

                o = ov[layer]
                pe.wait_ge(s_more, layer + 1)
                n_more = pe.value_load(ovn[0:1, 0:1], min_val=0, max_val=NOV)
                pe.wait_ge(s_y, (layer + 1) * NE)
                with pe.If(n_more > 0):
                    with pe.Fori(0, NOV) as j:
                        with pe.If(n_more > j):
                            pe.wait_ge(o["gathered"], (j + 1) * 16)
                            for c in range(4):
                                last = tr(bank[0][:, P * c:P * (c + 1)], xg[0][:, P * c:P * (c + 1)], ident)
                            last.then_inc(o["xt_full"], 1)
                            pe.wait_ge(o["xt"], j + 1)
                            pe.wait_ge(o["weights"], (j + 1) * 48)
                            gate_up(0).then_inc(o["gate_up"], 1)
                            pe.wait_ge(o["hidden"], j + 1)
                            hidden_transpose().then_inc(o["hx_full"], 1)
                            pe.wait_ge(o["hx"], j + 1)
                            down(0).then_inc(o["down"], 1)


_INS = ["x", "norm_mix_w", "w_in", "fox_forget_b", "w_out", "norm_ffn_w", "w_router_group", "b_router_group",
        "w_router_expert", "b_router_expert", "w_expert_gate", "w_expert_up", "w_expert_down", "norm_final_w"]


def kernel(**inputs):
    import numpy as _np
    import concourse.bacc as _bacc
    from concourse import mybir as _mybir
    from concourse.bass_utils import run_bass_kernel_spmd as _run

    nc = _bacc.Bacc("TRN2", target_bir_lowering=False, num_devices=1)
    arrays, args = {}, {}
    for name, a in [(n, _np.ascontiguousarray(inputs[n])) for n in _INS] + list(constants().items()):
        arrays[f"in_{name}_dram"] = a
        args[name] = nc.dram_tensor(f"in_{name}_dram", a.shape, _mybir.dt.from_np(a.dtype), kind="ExternalInput").ap()
    args["out"] = nc.dram_tensor("out_dram", (1, T, D), F32, kind="ExternalOutput").ap()
    trunk_kernel(nc, **args)
    r = _run(nc, [arrays], core_ids=[0])
    return r.results[0]["out_dram"]
```
